# Optimizing a Trainium2 kernel written in Bass

```python
import jax, jax.numpy as jnp
from jax import lax
import numpy as np

D_MODEL = 1024
BATCH = 1
SEQ = 256
DEPTH = 1
DEC_BATCH = 1
DEC_SEQ = 1024
PAST_LEN = 256

GRID_W = 64
HEAD_DIM = 64
D_A = 512
H_A = D_A // HEAD_DIM
D_B = 512
H_B = D_B // HEAD_DIM
R_DECAY = 64
R_ICLR = 64
R_GATE = 128
WIN_ROWS = 8
WIN_COLS = 16
D_FF = 2816
N_MOD = 6
D_IN = 3 * D_A + R_DECAY + R_ICLR + R_GATE + 3 * D_B + 2 * D_MODEL
EPS = 1e-6
GN_EPS = 64e-5
DECAY_SCALE = 0.606531
NEG_INF = -1e30
Q_BLOCK = 128
ATTN_SCALE = HEAD_DIM ** -0.5

kernel_name = "hybrid_rwkv7_natten_prefix_denoise_step"

def rmsnorm(x, g):
    xf = x.astype(jnp.float32)
    y = xf * lax.rsqrt(jnp.mean(xf * xf, axis=-1, keepdims=True) + EPS)
    return (y * g.astype(jnp.float32)).astype(x.dtype)

def modulation(cond, w_ada, b_ada):
    m = jax.nn.silu(cond) @ w_ada + b_ada
    return jnp.split(m[..., None, :], N_MOD, axis=-1)

def dwconv3(x, w):
    xp = jnp.pad(x, ((0, 0), (1, 1), (0, 0)))
    return xp[:, :-2] * w[0] + xp[:, 1:-1] * w[1] + xp[:, 2:] * w[2]

def heads(x, n_heads):
    b, t, _ = x.shape
    return x.reshape(b, t, n_heads, HEAD_DIM).transpose(0, 2, 1, 3)

def merge_heads(x):
    b, h, t, d = x.shape
    return x.transpose(0, 2, 1, 3).reshape(b, t, h * d)

def to_scan(t):
    t = jnp.stack([t[:, :, 0], jnp.flip(t[:, :, 1], axis=1)], axis=2)
    b, n = t.shape[:2]
    return t.reshape(b, n, 2, H_A, HEAD_DIM).transpose(1, 0, 2, 3, 4)

def from_scan(y):
    y = y.transpose(1, 0, 2, 3, 4)
    return y[:, :, 0] + jnp.flip(y[:, :, 1], axis=1)

def rwkv_scan(s0, r, w, a, b, k, v):
    def step(s, inp):
        r_t, w_t, a_t, b_t, k_t, v_t = inp
        sa = jnp.einsum('bdhvk,bdhk->bdhv', s, a_t)
        s = s * w_t[..., None, :] + sa[..., None] * b_t[..., None, :] + v_t[..., None] * k_t[..., None, :]
        return s, jnp.einsum('bdhvk,bdhk->bdhv', s, r_t)
    s_fin, y = lax.scan(step, s0, (r, w, a, b, k, v))
    return y, s_fin

def rwkv_branch(r, k, v, xw, xa, xg, s0, lp):
    out_dtype = r.dtype
    r, k, v, xw, xa, xg = [t.astype(jnp.float32) for t in (r, k, v, xw, xa, xg)]
    b, n, _ = r.shape
    decay = jnp.exp(-DECAY_SCALE * jax.nn.sigmoid(
        lp['decay_w0'] + jnp.einsum('btr,drc->btdc', jnp.tanh(xw), lp['decay_up'])))
    iclr = jax.nn.sigmoid(lp['iclr_a0'] + jnp.einsum('btr,drc->btdc', xa, lp['iclr_up']))
    kk = (k * lp['k_k']).reshape(b, n, H_A, HEAD_DIM)
    kk = kk / jnp.maximum(jnp.linalg.norm(kk, axis=-1, keepdims=True), 1e-12)
    kk = kk.reshape(b, n, D_A)
    k_dir = k[:, :, None] * (1.0 + (iclr - 1.0) * lp['k_a'])
    both = lambda t: jnp.broadcast_to(t[:, :, None], (b, n, 2, D_A))
    y, s_fin = rwkv_scan(s0, to_scan(both(r)), to_scan(decay), to_scan(both(-kk)),
                         to_scan(both(kk) * iclr), to_scan(k_dir), to_scan(both(v)))
    y = from_scan(y)
    mu = jnp.mean(y, axis=-1, keepdims=True)
    var = jnp.mean(jnp.square(y - mu), axis=-1, keepdims=True)
    y = ((y - mu) * lax.rsqrt(var + GN_EPS)).reshape(b, n, D_A) * lp['gn_w'] + lp['gn_b']
    rh, kh, vh = (t.reshape(b, n, H_A, HEAD_DIM) for t in (r, k, v))
    bonus = (jnp.sum(rh * kh * lp['r_k'], axis=-1, keepdims=True) * vh).reshape(b, n, D_A)
    g = jax.nn.sigmoid(xg) @ lp['gate_up']
    return ((y + bonus) * g).astype(out_dtype), s_fin

def context_attention(q, k, v):
    b, h, n, d = q.shape
    qb = q.reshape(b, h, n // Q_BLOCK, Q_BLOCK, d).transpose(2, 0, 1, 3, 4)
    def block(qi):
        s = jnp.einsum('bhqd,bhkd->bhqk', qi, k).astype(jnp.float32) * ATTN_SCALE
        p = jax.nn.softmax(s, axis=-1).astype(v.dtype)
        return jnp.einsum('bhqk,bhkd->bhqd', p, v)
    o = lax.map(block, qb)
    return o.transpose(1, 2, 0, 3, 4).reshape(b, h, n, d)

def neighbourhood_attention(q, k, v, k_ctx, v_ctx, rel_bias):
    b, h, n, d = q.shape
    rows = n // GRID_W
    kh = min(WIN_ROWS, rows)
    qg = q.reshape(b, h, rows, GRID_W, d)
    kg = k.reshape(b, h, rows, GRID_W, d)
    vg = v.reshape(b, h, rows, GRID_W, d)
    col = jnp.arange(GRID_W)
    col_start = jnp.clip(col - WIN_COLS // 2, 0, GRID_W - WIN_COLS)
    col_ok = (col[None, :] >= col_start[:, None]) & (col[None, :] < col_start[:, None] + WIN_COLS)
    dc = jnp.clip(col[None, :] - col[:, None], -(WIN_COLS - 1), WIN_COLS - 1) + (WIN_COLS - 1)
    row_off = jnp.arange(kh)

    def row_block(r):
        r0 = jnp.clip(r - kh // 2, 0, rows - kh)
        qr = lax.dynamic_index_in_dim(qg, r, axis=2, keepdims=False)
        kr = lax.dynamic_slice_in_dim(kg, r0, kh, axis=2)
        vr = lax.dynamic_slice_in_dim(vg, r0, kh, axis=2)
        dr = r0 + row_off - r + (WIN_ROWS - 1)
        bias = rel_bias[:, dr[:, None, None], dc[None]]
        s_win = jnp.einsum('bhqd,bhrkd->bhqrk', qr, kr).astype(jnp.float32) * ATTN_SCALE
        s_win = s_win + bias.transpose(0, 2, 1, 3).astype(jnp.float32)[None]
        s_win = jnp.where(col_ok[:, None, :], s_win, NEG_INF).reshape(b, h, GRID_W, kh * GRID_W)
        s_ctx = jnp.einsum('bhqd,bhld->bhql', qr, k_ctx).astype(jnp.float32) * ATTN_SCALE
        p = jax.nn.softmax(jnp.concatenate([s_win, s_ctx], axis=-1), axis=-1).astype(v.dtype)
        o = jnp.einsum('bhqn,bhnd->bhqd', p[..., :kh * GRID_W], vr.reshape(b, h, kh * GRID_W, d))
        return o + jnp.einsum('bhql,bhld->bhqd', p[..., kh * GRID_W:], v_ctx)

    o = lax.map(row_block, jnp.arange(rows))
    return o.transpose(1, 2, 0, 3, 4).reshape(b, h, n, d)

def conv_ffn(h, lp):
    u, gte = jnp.split(h @ lp['w_ffn_up'], 2, axis=-1)
    u = dwconv3(u, lp['conv_ffn'])
    return (jax.nn.gelu(u) * gte) @ lp['w_ffn_down']

def layer(x, cond, lp, ctx=None):
    sh1, sc1, g1, sh2, sc2, g2 = modulation(cond, lp['w_ada'], lp['b_ada'])
    h = rmsnorm(x, lp['norm1_g']) * (1 + sc1) + sh1
    z = h @ lp['w_in']
    r, k, v = jnp.split(dwconv3(z[..., :3 * D_A], lp['conv_rkv']), 3, axis=-1)
    splits = np.cumsum([R_DECAY, R_ICLR, R_GATE, D_B, D_B, D_B, D_MODEL]).tolist()
    xw, xa, xg, qb, kb, vb, ga, gb = jnp.split(z[..., 3 * D_A:], splits, axis=-1)
    qb, kb, vb = heads(qb, H_B), heads(kb, H_B), heads(vb, H_B)
    if ctx is None:
        s0 = jnp.zeros((x.shape[0], 2, H_A, HEAD_DIM, HEAD_DIM), jnp.float32)
        y_b = context_attention(qb, kb, vb)
    else:
        k_ctx, v_ctx, s0 = ctx
        y_b = neighbourhood_attention(qb, kb, vb, k_ctx, v_ctx, lp['rel_bias'])
    y_a, s_fin = rwkv_branch(r, k, v, xw, xa, xg, s0.astype(jnp.float32), lp)
    mixed = jax.nn.sigmoid(ga) * (y_a @ lp['w_out_a']) + jax.nn.sigmoid(gb) * (merge_heads(y_b) @ lp['w_out_b'])
    x = x + g1 * (mixed @ lp['w_out'])
    h2 = rmsnorm(x, lp['norm2_g']) * (1 + sc2) + sh2
    x = x + g2 * conv_ffn(h2, lp)
    if ctx is None:
        return x, kb, vb, s_fin
    return x

def setup_inputs(seed: int = 0) -> dict:
    key = jax.random.key(seed)
    ks = jax.random.split(key, 31)
    nrm = lambda i, shape, scale=1.0: scale * jax.random.normal(ks[i], shape, jnp.float32)
    conv_center = jnp.array([0.0, 1.0, 0.0], jnp.float32)[None, :, None]
    return {
        'x_prompt': nrm(0, (BATCH, SEQ, D_MODEL)),
        'x_sample': nrm(1, (DEC_BATCH, DEC_SEQ, D_MODEL)),
        'c': nrm(2, (DEC_BATCH, D_MODEL)),
        'cache_k': nrm(3, (DEC_BATCH, DEPTH, H_B, PAST_LEN, HEAD_DIM)),
        'cache_v': nrm(4, (DEC_BATCH, DEPTH, H_B, PAST_LEN, HEAD_DIM)),
        'state_rwkv': nrm(5, (DEC_BATCH, DEPTH, 2, H_A, HEAD_DIM, HEAD_DIM), 0.5),
        'c_ctx': nrm(6, (D_MODEL,)),
        'norm1_g': 1.0 + nrm(7, (DEPTH, D_MODEL), 0.02),
        'norm2_g': 1.0 + nrm(8, (DEPTH, D_MODEL), 0.02),
        'w_ada': nrm(9, (DEPTH, D_MODEL, N_MOD * D_MODEL), 0.5 * D_MODEL ** -0.5),
        'b_ada': nrm(10, (DEPTH, N_MOD * D_MODEL), 0.01),
        'w_in': nrm(11, (DEPTH, D_MODEL, D_IN), D_MODEL ** -0.5),
        'conv_rkv': conv_center + nrm(12, (DEPTH, 3, 3 * D_A), 0.3),
        'decay_w0': nrm(13, (DEPTH, 2, D_A), 0.5),
        'decay_up': nrm(14, (DEPTH, 2, R_DECAY, D_A), 0.5 * R_DECAY ** -0.5),
        'iclr_a0': nrm(15, (DEPTH, 2, D_A), 0.5),
        'iclr_up': nrm(16, (DEPTH, 2, R_ICLR, D_A), 0.5 * R_ICLR ** -0.5),
        'gate_up': nrm(17, (DEPTH, R_GATE, D_A), R_GATE ** -0.5),
        'k_k': 0.85 + nrm(18, (DEPTH, D_A), 0.1),
        'k_a': 1.0 + nrm(19, (DEPTH, D_A), 0.1),
        'r_k': nrm(20, (DEPTH, H_A, HEAD_DIM), 0.5),
        'gn_w': 1.0 + nrm(21, (DEPTH, D_A), 0.02),
        'gn_b': nrm(22, (DEPTH, D_A), 0.01),
        'rel_bias': nrm(23, (DEPTH, H_B, 2 * WIN_ROWS - 1, 2 * WIN_COLS - 1), 0.5),
        'w_out_a': nrm(24, (DEPTH, D_A, D_MODEL), D_A ** -0.5),
        'w_out_b': nrm(25, (DEPTH, D_B, D_MODEL), D_B ** -0.5),
        'w_out': nrm(26, (DEPTH, D_MODEL, D_MODEL), D_MODEL ** -0.5),
        'w_ffn_up': nrm(27, (DEPTH, D_MODEL, 2 * D_FF), D_MODEL ** -0.5),
        'conv_ffn': conv_center + nrm(28, (DEPTH, 3, D_FF), 0.3),
        'w_ffn_down': nrm(29, (DEPTH, D_FF, D_MODEL), D_FF ** -0.5),
        'norm_f_g': 1.0 + nrm(30, (D_MODEL,), 0.02),
    }

def reference(x_prompt, x_sample, c, cache_k, cache_v, state_rwkv, c_ctx,
              norm1_g, norm2_g, w_ada, b_ada, w_in, conv_rkv, decay_w0, decay_up,
              iclr_a0, iclr_up, gate_up, k_k, k_a, r_k, gn_w, gn_b, rel_bias,
              w_out_a, w_out_b, w_out, w_ffn_up, conv_ffn, w_ffn_down, norm_f_g):
    params = {
        'norm1_g': norm1_g, 'norm2_g': norm2_g, 'w_ada': w_ada, 'b_ada': b_ada,
        'w_in': w_in, 'conv_rkv': conv_rkv, 'decay_w0': decay_w0, 'decay_up': decay_up,
        'iclr_a0': iclr_a0, 'iclr_up': iclr_up, 'gate_up': gate_up, 'k_k': k_k,
        'k_a': k_a, 'r_k': r_k, 'gn_w': gn_w, 'gn_b': gn_b, 'rel_bias': rel_bias,
        'w_out_a': w_out_a, 'w_out_b': w_out_b, 'w_out': w_out, 'w_ffn_up': w_ffn_up,
        'conv_ffn': conv_ffn, 'w_ffn_down': w_ffn_down,
    }
    xp, xs = x_prompt, x_sample
    new_k, new_v, new_s = [], [], []
    for l in range(DEPTH):
        lp = {name: arr[l] for name, arr in params.items()}
        xp, k_l, v_l, s_l = layer(xp, c_ctx, lp)
        new_k.append(k_l)
        new_v.append(v_l)
        new_s.append(s_l)
        xs = layer(xs, c, lp, (cache_k[:, l], cache_v[:, l], state_rwkv[:, l]))
    y_prompt = rmsnorm(xp, norm_f_g)
    y_sample = rmsnorm(xs, norm_f_g)
    new_cache_k = jnp.stack(new_k, axis=1)
    new_cache_v = jnp.stack(new_v, axis=1)
    new_state_rwkv = jnp.stack(new_s, axis=1)
    return (y_prompt, y_sample, new_cache_k, new_cache_v, new_state_rwkv)


_drawn_inputs = setup_inputs


def setup_inputs(seed=0):
    import zlib

    import numpy as np

    out = dict(_drawn_inputs(seed))
    spreads = {}
    factors = {'cache_k': 52.024,
     'cache_v': 43.92,
     'state_rwkv': 8.0,
     'norm2_g': 8.0,
     'k_k': 11.069,
     'gn_w': 33.308,
     'gn_b': 63.964,
     'rel_bias': 58.749,
     'norm_f_g': 2.749}
    for name, (base, spread) in spreads.items():
        noise = np.random.default_rng([zlib.crc32(name.encode()), seed]).standard_normal(out[name].shape)
        drawn = base * np.exp(spread * noise) if base else spread * noise
        out[name] = __import__('jax').numpy.asarray(drawn.astype(out[name].dtype))
    for name, factor in factors.items():
        out[name] = (out[name] * factor).astype(out[name].dtype)
    return out
```

```python
import concourse.bass as bass
from concourse import mybir
from concourse.alu_op_type import AluOpType as ALU
from contextlib import ExitStack, contextmanager
import numpy as np

F32 = mybir.dt.float32
ACT = mybir.ActivationFunctionType
AX = mybir.AxisListType

P = 128
D = 1024
KB = D // P
CTX, LAT = 256, 1024
T = CTX + LAT
TB = T // P
HD = 64
NP = 4
DFF = 2816
FB = DFF // P
GRID = 64
ROWS = LAT // GRID
WIN_R, WIN_C = 8, 16
NDR = 2 * WIN_R - 1
NDC = 2 * WIN_C - 1
EPS, GN_EPS = 1e-6, 64e-5
KAPPA = 0.606531
SCALE = HD ** -0.5
NEG = -1e30
C = 64
NC_CTX, NC = CTX // C, T // C
LEVELS = [1, 2, 4, 8, 16, 32]
SEGS = [(0, 256), (256, 512), (768, 512)]
B_R, B_CODE, B_XG, B_Q, B_K, B_V, B_GA, B_GB = 0, 12, 13, 14, 18, 22, 26, 34

PARAMS = {}
for _name, _n in [("cond", 16), ("b_ada", 48), ("norm1", 8), ("norm2", 8), ("conv_rkv", 36), ("conv_ffn", 66),
                  ("bias_wi", 16), ("k_k", 4), ("k_a", 4), ("r_k", 4), ("gn_w", 4), ("gn_b", 4)]:
    PARAMS[_name] = (sum(n for _, n in PARAMS.values()), _n)
N_PARAMS = sum(n for _, n in PARAMS.values())

CONSTS = {}
for _name, _n in [("ident", 128), ("ones", 128), ("flip", 128), ("same", 128), ("win_ok", 64), ("win_neg", 64), ("gram", 384),
                  ("level", 2 * len(LEVELS) * 128), ("head_in", 32), ("head_out", 512)]:
    CONSTS[_name] = (sum(n for _, n in CONSTS.values()), _n)
N_CONSTS = sum(n for _, n in CONSTS.values())


def constants():
    p = np.arange(P)
    out = np.zeros((P, N_CONSTS), np.float32)

    def put(name, a):
        at, n = CONSTS[name]
        out[:, at:at + n] = np.asarray(a, np.float32).reshape(P, n)

    same = (p[:, None] // 64) == (p[None, :] // 64)
    put("ident", np.eye(P))
    put("ones", np.ones((P, P)))
    put("same", same)
    put("flip", same & ((p[:, None] % 64) + (p[None, :] % 64) == 63))
    qc, kc = p[:, None] % 64, np.arange(64)[None, :]
    start = np.clip(qc - WIN_C // 2, 0, GRID - WIN_C)
    ok = (kc >= start) & (kc < start + WIN_C)
    put("win_ok", ok)
    put("win_neg", np.where(ok, 0.0, NEG))
    s, t = p[:, None] % 64, p[None, :] % 64
    before = [s < t, s > t]
    put("gram", np.concatenate([np.concatenate([same & b, (b | (s == t))[:, :64]], 1) for b in before], 1))
    lv = []
    for b in before:
        for m in LEVELS:
            lv.append(same & b & (s // (2 * m) == t // (2 * m)) & (s // m != t // m))
    put("level", np.concatenate(lv, 1))
    hin = np.zeros((P, NP, 8))
    hout = np.zeros((P, NP, P))
    for j in range(NP):
        for h in range(2):
            hin[64 * h:64 * h + 64, j, 2 * j + h] = 1
            hout[2 * j + h, j, 64 * h:64 * h + 64] = 1
    put("head_in", hin)
    put("head_out", hout)
    return out


class Steps:

    def __init__(self, eng, sem):
        self.eng, self.sem, self.base, self.n = eng, sem, 0, 0

    def step(self, ins):
        ins.then_inc(self.sem, 1)
        self.n += 1

    def settle(self):
        self.eng.wait_ge(self.sem, self.base + self.n)

    def link(self, ins):
        self.step(ins)
        self.settle()

    @contextmanager
    def loop(self, first, last, per):
        before = self.n
        with self.eng.Fori(first, last) as i:
            self.base, self.n = (i - first) * per + before, 0
            yield i
            assert self.n == per, f"{self.sem}: {self.n} steps in a turn, not {per}"
        self.base, self.n = 0, before + (last - first) * per


def half_ap(view, h):
    return view[64 * h:64 * h + 64]


def build(nc, dram):
    ctx = ExitStack()
    with ctx:
        def sem(name):
            return ctx.enter_context(nc.semaphore(name))

        WORDS = 53200
        arena = ctx.enter_context(nc.sbuf_tensor("arena", [P, WORDS], F32))
        PS = ctx.enter_context(nc.psum_tensor("PS", [P, 8, 512], F32))

        def view(at, *dims):
            n = int(np.prod(dims))
            assert at + n <= WORDS, (at, dims)
            v = arena[:, at:at + n]
            if len(dims) == 2:
                v = v.rearrange("p (a b) -> p a b", b=dims[1])
            if len(dims) == 3:
                v = v.rearrange("p (a b c) -> p a b c", b=dims[1], c=dims[2])
            return v

        class Space:

            def __init__(self, at):
                self.at = at

            def __call__(self, *dims):
                v = view(self.at, *dims)
                self.at += int(np.prod(dims))
                return v

        keep = Space(0)
        cst = keep(N_CONSTS)
        prm = keep(N_PARAMS)
        mod = keep(48, 2)
        gsc1 = keep(KB, 2)
        gsc2 = keep(KB, 2)
        tokstat = keep(2, TB)
        eps_c = keep(2)
        FREE = keep.at

        def const(name, *dims):
            at, n = CONSTS[name]
            v = cst[:, at:at + n]
            if len(dims) == 2:
                v = v.rearrange("p (a b) -> p a b", b=dims[1])
            if len(dims) == 3:
                v = v.rearrange("p (a b c) -> p a b c", b=dims[1], c=dims[2])
            return v

        ident, ones, flip = const("ident"), const("ones"), const("flip")
        win_ok, win_neg = const("win_ok"), const("win_neg")
        gram_mask = const("gram", 2, 192)
        level_mask = const("level", 2, len(LEVELS), 128)
        same = const("same")
        head_in = const("head_in", NP, 8)
        head_out = const("head_out", NP, P)

        def par(name, k=None):
            at, n = PARAMS[name]
            return prm[:, at:at + n] if k is None else prm[:, at + k:at + k + 1]

        cond = par("cond").rearrange("p (k c) -> p k c", c=2)

        s1 = Space(FREE)
        hT = s1(KB, T)
        ybT = s1(NP, T)
        AFTER_YB = s1.at
        x10 = s1(TB, D)
        diag = s1(TB, P)
        sq = s1(2, D)
        ada_ring = s1(4, KB, P)
        conds = s1(KB, 2)
        s2 = Space(AFTER_YB)
        qkv_ring = s2(3, KB, P)
        s2.at = max(s2.at, AFTER_YB)
        NU = 4 + ROWS
        qbd = s2(NU, P)
        kT = s2(T)
        vtok = s2(TB, P)
        vodd = s2(TB - 3, P)
        kctok = s2(2, P)
        kcT = s2(CTX)
        vctok = s2(2, P)
        bias_flipped = s2(NDR, 64)
        bias = s2(NDR, 64)
        scr = s2(3, 768)
        pT = s2(6, P)
        newk = s2(2, P)
        rowstat = s2(3, 3)
        conds2 = s2(KB, 2)
        s12 = Space(max(s1.at, s2.at))
        ada_ring2 = s12(4, KB, P)

        consts_in = sem("consts_in")
        x_in = [sem(f"x_in{b}") for b in range(TB)]
        ada_in = [sem(f"ada_in{s}") for s in range(4)]
        ada_used = sem("ada_used")
        sumsq_done = sem("sumsq_done")
        diag_ready = sem("diag_ready")
        cond_ready = sem("cond_ready")
        mod_done = sem("mod_done")
        gsc_ready = sem("gsc_ready")
        h_done = sem("h_done")
        h_out_a, h_out_d = sem("h_out_a"), sem("h_out_d")
        act_steps, dve_steps, pool_steps = (sem(n) for n in ("act_steps", "dve_steps", "pool_steps"))

        qkv_in = [sem(f"qkv_in{s}") for s in range(3)]
        cache_in = [sem(f"cache_in{s}") for s in range(3)]
        proj_done = sem("proj_done")
        proj_out_a, proj_out_d = sem("proj_out_a"), sem("proj_out_d")
        vodd_in = sem("vodd_in")
        newkv_out = sem("newkv_out")
        scored = sem("scored")
        win_out, ctx_out = sem("win_out"), sem("ctx_out")
        max_ready, exp_done, recip_ready, p_ready = (sem(n) for n in ("max_ready", "exp_done", "recip_ready", "p_ready"))
        pt_done = sem("pt_done")
        pt_out_a, pt_out_d = sem("pt_out_a"), sem("pt_out_d")
        o_done, o_out = sem("o_done"), sem("o_out")
        zeroed = sem("zeroed")

        MODB = 7
        PROJ_A, PROJ_D = 7, 6

        def unit_window(u):
            r = u - 4
            r0 = min(max(r - WIN_R // 2, 0), ROWS - WIN_R)
            return r0, (r0 - r + WIN_R - 1) * 64

        def unit_keys(u):
            if u < 4:
                return [(vtok, 0), (vtok, 1)]
            r0, _ = unit_window(u)
            src = [(vtok, 2 + r0 // 2 + b) for b in range(4)] if r0 % 2 == 0 else \
                  [(vodd, (r0 - 1) // 2 + b) for b in range(4)]
            return src + [(vctok, 0), (vctok, 1)]

        ADA_FIRST, ADA_PAIR = 16, 8
        ADA_AT = list(range(3, 3 + 2 * ADA_PAIR, 2))

        s3 = Space(AFTER_YB)
        rkv = s3(12, T)
        rT, kTr, vT = rkv[:, 0:4, :], rkv[:, 4:8, :], rkv[:, 8:12, :]
        kk = s3(NP, T)
        xwa = s3(T)
        codes = s3(2, 2, NP * P)
        ya = s3(NP, T)
        SXG_AT = s3.at
        sxg = s3(T)
        rkv_ring = s3(4, KB, P)
        w3 = Space(FREE + KB * T)
        ZP = T + 3
        zpad = w3(2, ZP)
        convt = w3(ZP - 2)
        w3 = Space(FREE + KB * T)
        kksq = w3(2, T)
        norm8 = w3(T)
        wk = Space(FREE)
        AR = wk(2, NP, 192)
        GB = wk(2, NP, 192)
        GK = wk(2, NP, 192)
        Bt = wk(2, NP, P)
        Kt = wk(2, NP, P)
        Vt = wk(2, NP, P)
        Q = wk(2, NP, P)
        S = wk(2, NP, P)
        BD_B, BD_K, BD_V = wk(NP, P), wk(NP, P), wk(NP, P)
        Tm, Z = wk(NP, P), wk(NP, P)
        RH, U = wk(NP, P), wk(NP, P)
        E = wk(2, NP, C)
        PX = wk(3, NP, C)
        SG = wk(2, NP, C)
        TMP = wk(NP, C)
        assert wk.at <= AFTER_YB, wk.at
        wk = Space(SXG_AT)
        RESET = wk(NP * C)
        PEND = wk(2, NP)
        BK = wk(NP, C)
        CS = wk(NP, C)
        assert wk.at <= SXG_AT + T
        wk = Space(SXG_AT + T)
        Lm = wk(len(LEVELS) - 1, NP, P)
        SI = wk(2, NP, P)
        assert wk.at <= WORDS, wk.at
        gate_w = codes[:, 0, 0, :]
        norm8b = xwa

        NUNIT = 2 * NC
        yb_kept, h_kept = sem("yb_kept"), sem("h_kept")
        w_in = [sem(f"w_in{s}") for s in range(4)]
        codes_in, gate_in, state_in = sem("codes_in"), sem("gate_in"), sem("state_in")
        z_done, z_out, conv_done = sem("z_done"), sem("z_out"), sem("conv_done")
        kksq_ready, kksum_done, norm_ready, inv_ready, kkinv_done, kk_ready = (
            sem(n) for n in ("kksq_ready", "kksum_done", "norm_ready", "inv_ready", "kkinv_done", "kk_ready"))
        scan_zeroed = sem("scan_zeroed")
        si_done, si_out = sem("si_done"), sem("si_out")
        code_done, sw_ready, sig_done, e_ready, exps_done, bk_ready, front_done, vt_ready = (
            sem(n) for n in ("code_done", "sw_ready", "sig_done", "e_ready", "exps_done", "bk_ready", "front_done", "vt_ready"))
        gram_done, gram_out, tr_done, tr_out = (sem(n) for n in ("gram_done", "gram_out", "tr_done", "tr_out"))
        q2_ready, lm_ready, lz_done, lz_ready, tq_done, t_out, q_out = (
            sem(n) for n in ("q2_ready", "lm_ready", "lz_done", "lz_ready", "tq_done", "t_out", "q_out"))
        rh_done, rh_out, u_done, u_out, y_done, y_out, st_done, s_ready = (
            sem(n) for n in ("rh_done", "rh_out", "u_done", "u_out", "y_done", "y_out", "st_done", "s_ready"))
        fin_done, fin_read, fin_stored, switched = (sem(n) for n in ("fin_done", "fin_read", "fin_stored", "switched"))
        kkraw_ready, sxg_kept, zpad_zeroed, si_zeroed = (sem(n) for n in ("kkraw_ready", "sxg_kept", "zpad_zeroed", "si_zeroed"))
        SCAN_ZEROED = 5
        OPS_PAIR = 25
        bonus_ready, mean_done, yc_ready, bonus_out, ysq_ready = (
            sem(n) for n in ("bonus_ready", "mean_done", "yc_ready", "bonus_out", "ysq_ready"))
        var_done, sd_ready, isd_ready, gn_done, gn_out, gate_done, ya_ready = (
            sem(n) for n in ("var_done", "sd_ready", "isd_ready", "gn_done", "gn_out", "gate_done", "ya_ready"))

        def chunk_at(d, step, ctx_part):
            if d == 0:
                return step * C
            return step * (-C) + ((NC_CTX - 1) * C if ctx_part else (NC_CTX + NC - 1) * C)

        s4 = Space(AFTER_YB)
        mix = s4(KB, T)
        gates = s4(2, T)
        gated_b = s4(T)
        X1_AT = s4.at
        x1 = s4(KB, T)
        S5_AT = s4.at
        w_ring = rkv_ring
        h2T = hT
        x_again = view(FREE, TB, D)
        x1sq = [view(FREE + (KB + k) * T, T) for k in range(NP)] + [gates[:, 0, :], gates[:, 1, :], gated_b, view(S5_AT, T)]
        diag2 = view(FREE + 2 * KB * T, TB, P)

        GROUPS = [(0, 8), (8, 8), (16, 6)]
        MAXF = 8
        fact = view(FREE + KB * T, MAXF, T)
        s5 = Space(FREE + KB * T + MAXF * T)
        upad = s5(2, ZP)
        uconv = s5(ZP - 2)
        assert s5.at <= X1_AT
        s5 = Space(S5_AT)
        ugelu = s5(2, T)
        tstat = s5(2, TB)
        assert s5.at <= SXG_AT + T
        y_tok = view(FREE, 4, D)
        y_sq = view(FREE + 4 * D, D)
        gain_f = view(FREE + 5 * D, D)

        W4 = [4, 4, 3, 3]
        WO = [w + KB for w in W4]
        WF = [w + KB // 4 for w in WO]
        h_again = sem("h_again")
        mix_mm, gate_out, mix_out, mix_ready = (sem(n) for n in ("mix_mm", "gate_out", "mix_out", "mix_ready"))
        xt_done, xt_out, wo_mm, x1_out = (sem(n) for n in ("xt_done", "xt_out", "wo_mm", "x1_out"))
        x1sq_ready, ms_done, ms_ready, diag2_ready, rs_done, h2_scaled, h2_ready = (
            sem(n) for n in ("x1sq_ready", "ms_done", "ms_ready", "diag2_ready", "rs_done", "h2_scaled", "h2_ready"))
        u_copied, uconv_ready, gelu_ready, fact_ready, down_done, down_out, upad_zeroed = (
            sem(n) for n in ("u_copied", "uconv_ready", "gelu_ready", "fact_ready", "down_done", "down_out", "upad_zeroed"))
        up_done, gain_in, yt_done, yss_ready, y_ready = (
            sem(n) for n in ("up_done", "gain_in", "yt_done", "yss_ready", "y_ready"))
        y_stored = [sem(f"y_stored{s}") for s in range(4)]

        def ffn_tiles(g):
            f0, _ = GROUPS[g]
            at = 2 * f0 + KB * g
            return at, at + 2 * GROUPS[g][1]

        block = ctx.enter_context(nc.Block())

        @block.sync
        def _(sp):
            sp.dma_start(cst, dram["consts"]).then_inc(consts_in, 16)
            sp.dma_start(prm, dram["params"]).then_inc(consts_in, 16)
            for b in range(TB):
                sp.dma_start(x10[:, b, :], dram["x"][b]).then_inc(x_in[b], 16)

            def load_ada(n, s, first=False):
                if not first:
                    sp.wait_ge(ada_used, n - 3)
                sp.dma_start(ada_ring2[:, s, :, :].rearrange("p k n -> p (k n)"),
                             dram["w_ada"][bass.ds(n, 1)].rearrange("a p n -> p (a n)")).then_inc(ada_in[s], 16)

            for s in range(4):
                load_ada(s, s, first=True)
            with sp.Fori(1, ADA_FIRST // 4) as i:
                for s in range(4):
                    load_ada(i * 4 + s, s)

            sp.wait_ge(h_done, 3 * KB)
            sp.dma_start(dram["start"], ident[0:1, 0:64]).then_inc(newkv_out, 16)
            with sp.Fori(0, NP) as i:
                for s, col in enumerate((B_Q, B_K, B_V)):
                    sp.wait_ge(proj_done, i * 13 + 1)
                    sp.dma_start(qkv_ring[:, s].rearrange("p k n -> p (k n)"),
                                 dram["w_in"][bass.ds(i + col, 1)].rearrange("a p n -> p (a n)")).then_inc(qkv_in[s], 16)
                sp.wait_ge(o_done, i * NU + 1)
                sp.dma_start(kctok, dram["ck"][bass.ds(i, 1)].rearrange("a b s c -> s (a b) c")).then_inc(cache_in[0], 16)
                sp.dma_start(vctok, dram["cv"][bass.ds(i, 1)].rearrange("a b s c -> s (a b) c")).then_inc(cache_in[1], 16)
                for hh in range(2):
                    rb = dram["rel"]
                    win = rb[bass.ds(i * (2 * NDR * NDC) + hh * NDR * NDC, 1)]
                    src = bass.AP(win.tensor, win.offset, [[1, 64], [NDC, NDR], [1, 64]])
                    sp.dma_start(half_ap(bias_flipped, hh), src).then_inc(cache_in[2], 16)
                for s in range(4):
                    load_ada(i * ADA_PAIR + (ADA_FIRST + s), s)
                sp.wait_ge(proj_out_a, i * PROJ_A + PROJ_A)
                nodd = TB - 3
                sp.dma_start(vodd[0:64, :, :], vtok[64:128, 2:2 + nodd, :]).then_inc(vodd_in, 16)
                sp.dma_start(vodd[64:128, :, :], vtok[0:64, 3:3 + nodd, :]).then_inc(vodd_in, 16)
                sp.wait_ge(proj_out_d, i * PROJ_D + PROJ_D)
                sp.dma_start(dram["new_k"][bass.ds(i, 1)].rearrange("a b s c -> s (a b) c"), newk[:, :, :]).then_inc(newkv_out, 16)
                sp.dma_start(dram["new_v"][bass.ds(i, 1)].rearrange("a b s c -> s (a b) c"), vtok[:, 0:2, :]).then_inc(newkv_out, 16)
                for s in range(4, ADA_PAIR):
                    load_ada(i * ADA_PAIR + (ADA_FIRST + s), s % 4)
            def load_rkv(idx, s, first=False):
                if not first:
                    sp.wait_ge(z_done, idx - 3)
                sp.dma_start(rkv_ring[:, s, :, :].rearrange("p k n -> p (k n)"),
                             dram["w_in"][bass.ds(idx, 1)].rearrange("a p n -> p (a n)")).then_inc(w_in[s], 16)

            for s in range(4):
                load_rkv(s, s, first=True)
            sp.wait_ge(o_out, NP * 2 * NU)
            sp.dma_start(dram["yb_kept"], ybT.rearrange("p j t -> p (j t)")).then_inc(yb_kept, 16)
            sp.dma_start(dram["h_kept"], hT.rearrange("p k t -> p (k t)")).then_inc(h_kept, 16)
            sp.wait_ge(ada_used, 48)
            sp.wait_ge(o_done, NP * NU + 1)
            sp.dma_start(codes[:, :, :, :].rearrange("p q d n -> p (q d n)"), dram["codes"]).then_inc(codes_in, 16)
            with sp.Fori(1, 3) as i:
                for s in range(4):
                    load_rkv(i * 4 + s, s)
            load_rkv(12, 0)
            load_rkv(13, 1)
            sp.wait_ge(z_out, 14)
            sp.dma_start(dram["sxg_kept"], sxg).then_inc(sxg_kept, 16)
            sp.wait_ge(si_zeroed, 1)
            for d in range(2):
                for h in range(2):
                    sp.dma_start(SI[64 * h:64 * h + 64, d, :, 64 * h:64 * h + 64],
                                 dram["state"][d, :, 64 * h:64 * h + 64, :].rearrange("j v k -> v j k")).then_inc(state_in, 16)
            for d in range(2):
                sp.wait_ge(fin_read, d + 1)
                for h in range(2):
                    sp.dma_start(dram["new_state"][d, :, 64 * h:64 * h + 64, :].rearrange("j v k -> v j k"),
                                 SI[64 * h:64 * h + 64, d, :, 64 * h:64 * h + 64]).then_inc(fin_stored, 16)
            sp.wait_ge(y_out, NUNIT)
            sp.wait_ge(rh_out, NUNIT)
            sp.wait_ge(s_ready, NUNIT + 2)
            sp.dma_start(gate_w, dram["gate_up"]).then_inc(gate_in, 16)
            sp.dma_start(sxg, dram["sxg_kept"]).then_inc(gate_in, 16)
            sp.wait_ge(fin_stored, 64)

            sp.dma_start(hT.rearrange("p k t -> p (k t)"), dram["h_kept"]).then_inc(h_again, 16)
            sp.dma_start(ybT.rearrange("p j t -> p (j t)"), dram["yb_kept"]).then_inc(h_again, 16)

            def load_mix(n, first):
                for s, (name, at, kb) in enumerate((("w_in", B_GA, KB), ("w_oa", 0, NP), ("w_in", B_GB, KB), ("w_ob", 0, NP))):
                    if not first:
                        sp.wait_ge(mix_mm, n * 4 + (s - 3))
                    sp.dma_start(w_ring[:, s, 0:kb, :].rearrange("p k n -> p (k n)"),
                                 dram[name][bass.ds(n + at, 1)].rearrange("a p n -> p (a n)")).then_inc(w_in[s], 16)

            load_mix(0, True)
            with sp.Fori(1, KB) as n:
                load_mix(n, False)
            for n in range(KB):
                sp.wait_ge(mix_mm, 4 * KB - 3 + n) if n < 4 else sp.wait_ge(wo_mm, 3 * (n - 3))
                sp.dma_start(w_ring[:, n % 4, :, :].rearrange("p k n -> p (k n)"), dram["w_o"][n]).then_inc(w_in[n % 4], 16)
                if n == 2:
                    for b in range(TB):
                        sp.dma_start(x_again[:, b, :], dram["x"][b]).then_inc(x_in[b], 16)

            def load_free(s, src):
                sp.dma_start(src[0], src[1]).then_inc(w_in[s], 16)

            def up_tile(f, s):
                return (w_ring[:, s, :, :].rearrange("p k n -> p (k n)"),
                        dram["w_up"][bass.ds(f + (s % 2) * FB, 1)].rearrange("a p n -> p (a n)"))

            def down_tile(g, n, s):
                f0, nf = GROUPS[g]
                return (w_ring[:, s, 0:nf, :].rearrange("p k n -> p (k n)"),
                        dram["w_down"][bass.ds(n, 1), :, f0 * P:(f0 + nf) * P].rearrange("a p n -> p (a n)"))

            def up_turn(done, f, s):
                sp.wait_ge(up_done, done)
                load_free(s, up_tile(f, s))

            for g, (f0, nf) in enumerate(GROUPS):
                for s in range(4):
                    if g == 0:
                        sp.wait_ge(wo_mm, 3 * (KB - 3 + s))
                    else:
                        sp.wait_ge(down_done, KB * g - 3 + s)
                    load_free(s, up_tile(f0 + s // 2, s))
                with sp.Fori(1, nf // 2) as i:
                    for s in range(4):
                        up_turn(i * 4 + (2 * f0 + s - 3), i * 2 + (f0 + s // 2), s)
                for s in range(4):
                    sp.wait_ge(up_done, 2 * (f0 + nf) - 3 + s)
                    load_free(s, down_tile(g, s, s))
                with sp.Fori(1, KB // 4) as i:
                    for s in range(4):
                        sp.wait_ge(down_done, i * 4 + (KB * g + s - 3))
                        load_free(s, down_tile(g, i * 4 + s, s))
            sp.wait_ge(up_done, 2 * FB)
            sp.dma_start(gain_f, dram["norm_f"].to_broadcast([P, D])).then_inc(gain_in, 16)
            for b in range(TB):
                sp.wait_ge(y_ready, b + 1)
                sp.dma_start(dram["y"][b], y_tok[:, b % 4, :]).then_inc(y_stored[b % 4], 16)
            for s in range(4):
                sp.wait_ge(y_stored[s], 16 * len(range(s, TB, 4)))
            sp.wait_ge(fin_stored, 64)
            sp.wait_ge(newkv_out, (2 * NP + 1) * 16)

        @block.tensor
        def _(pe):
            mm = pe.matmul

            def ada_block(n, s, turn):
                pe.wait_ge(ada_in[s], turn * 16)
                for k in range(KB):
                    ins = mm(PS[:, MODB, bass.ds(n * 2, 2)], ada_ring2[:, s, k, :], conds[:, k, :],
                             start=(k == 0), stop=(k == KB - 1))
                ins.then_inc(ada_used, 1)

            pe.wait_ge(cond_ready, 1)
            with pe.Fori(0, ADA_FIRST // 4) as i:
                for s in range(4):
                    ada_block(i * 4 + s, s, i + 1)
            pe.wait_ge(diag_ready, TB)
            for k in range(KB):
                for g, (t0, n) in enumerate(SEGS):
                    bank = 3 * (k % 2) + g
                    if k >= 2:
                        pe.wait_ge(h_out_a if g == 1 else h_out_d, (k - 1) if g == 1 else 2 * (k - 2) + (1 if g == 0 else 2))
                    for b in range(t0 // P, (t0 + n) // P):
                        ins = mm(PS[:, bank, b * P - t0:b * P - t0 + P], x10[:, b, k * P:(k + 1) * P], diag[:, b, :],
                                 start=True, stop=True)
                    ins.then_inc(h_done, 1)
            pe.wait_ge(h_out_a, KB)
            pe.wait_ge(h_out_d, 2 * KB)
            pe.wait_ge(mod_done, 1)
            mm(PS[:, 0, 0:64], ident, ident[:, 0:64], start=True, stop=True).then_inc(proj_done, 1)
            mm(PS[:, 0, 0:64], ident, ident[:, 0:64], start=True, stop=True).then_inc(o_done, 1)

            def attention(i):
                def project(s, g):
                    t0, n = SEGS[g]
                    for k in range(KB):
                        ins = mm(PS[:, 3 * s + g, 0:n], qkv_ring[:, s, k, :], hT[:, k, t0:t0 + n],
                                 start=(k == 0), stop=(k == KB - 1))
                    return ins

                pe.wait_ge(qkv_in[0], i * 16 + 16)
                for g in range(3):
                    ins = project(0, g)
                    ins.then_inc(proj_done, 1)
                pe.wait_ge(qkv_in[1], i * 16 + 16)
                for g in range(3):
                    ins = project(1, g)
                    ins.then_inc(proj_done, 1)
                pe.wait_ge(cache_in[2], i * 32 + 32)
                mm(PS[:, 6, 0:512], flip, bias_flipped[:, 0:8, :], start=True, stop=True).then_inc(proj_done, 1)
                pe.wait_ge(proj_out_a, i * PROJ_A + 1)
                mm(PS[:, 0, 0:448], flip, bias_flipped[:, 8:NDR, :], start=True, stop=True).then_inc(proj_done, 1)
                pe.wait_ge(cache_in[0], i * 16 + 16)
                pe.wait_ge(proj_out_a, i * PROJ_A + 2)
                for b in range(2):
                    ins = pe.transpose(PS[:, 1, b * P:(b + 1) * P], kctok[:, b, :], ident)
                ins.then_inc(proj_done, 1)
                pe.wait_ge(qkv_in[2], i * 16 + 16)
                for n, (bank, ready, at) in enumerate([(2, proj_out_a, i * PROJ_A + 3), (3, proj_out_d, i * PROJ_D + 1),
                                                       (4, proj_out_d, i * PROJ_D + 2)]):
                    pe.wait_ge(ready, at)
                    for b in range(4 * n, min(4 * n + 4, TB)):
                        for k in range(KB):
                            ins = mm(PS[:, bank, (b % 4) * P:(b % 4 + 1) * P], hT[:, k, b * P:(b + 1) * P],
                                     qkv_ring[:, 2, k, :], start=(k == 0), stop=(k == KB - 1))
                    ins.then_inc(proj_done, 1)
                pe.wait_ge(proj_out_d, i * PROJ_D + 3)
                for b in range(2):
                    ins = pe.transpose(PS[:, 5, b * P:(b + 1) * P], kT[:, b * P:(b + 1) * P], ident)
                ins.then_inc(proj_done, 1)
                pe.wait_ge(proj_out_a, i * PROJ_A + PROJ_A)
                pe.wait_ge(proj_out_d, i * PROJ_D + PROJ_D)
                pe.wait_ge(cache_in[1], i * 16 + 16)
                pe.wait_ge(vodd_in, i * 32 + 32)

                for t in range(NU + 2):
                    if t < NU:
                        u, bank = t, 2 * (t % 2)
                        if u >= 2:
                            pe.wait_ge(ctx_out, i * NU + (u - 1))
                        if u >= 6:
                            pe.wait_ge(win_out, i * ROWS + (u - 5))
                        if u >= 4:
                            r0, _ = unit_window(u)
                            mm(PS[:, bank, :], qbd[:, u, :], kT[:, CTX + GRID * r0:CTX + GRID * r0 + 512],
                               start=True, stop=True)
                        mm(PS[:, bank + 1, 0:256], qbd[:, u, :], kcT if u >= 4 else kT[:, 0:CTX],
                           start=True, stop=True).then_inc(scored, 1)
                    if t >= 2:
                        u = t - 2
                        nb = 2 if u < 4 else 6
                        pe.wait_ge(p_ready, i * NU + u + 1)
                        if u >= 1:
                            pe.wait_ge(pt_out_a, i * NU + u)
                        if u >= 5:
                            pe.wait_ge(pt_out_d, i * ROWS + (u - 4))
                        for b in range(nb):
                            at = 512 + b * P if u < 4 else b * P
                            ins = pe.transpose(PS[:, 4 + b // 4, (b % 4) * P:(b % 4 + 1) * P],
                                               scr[:, u % 3, at:at + P], ident)
                        ins.then_inc(pt_done, 1)
                        if t in ADA_AT:
                            s = ADA_AT.index(t)
                            ada_block(i * ADA_PAIR + (ADA_FIRST + s), s % 4, i * 2 + (ADA_FIRST // 4 + s // 4 + 1))
                        pe.wait_ge(pt_out_a, i * NU + u + 1)
                        if u >= 4:
                            pe.wait_ge(pt_out_d, i * ROWS + (u - 3))
                        if u >= 1:
                            pe.wait_ge(o_out, i * 2 * NU + 2 * u)
                        for b, (src, at) in enumerate(unit_keys(u)):
                            ins = mm(PS[:, 6, 0:P], src[:, at, :], pT[:, b, :], start=(b == 0), stop=(b == nb - 1))
                        ins.then_inc(o_done, 1)
                pe.wait_ge(o_out, i * 2 * NU + 2 * NU)

            with pe.Fori(0, NP) as i:
                attention(i)
            pe.wait_ge(o_out, NP * 2 * NU)
            pe.wait_ge(mod_done, 2)

            def project(w, bank):
                for g, (t0, n) in enumerate(SEGS):
                    for k in range(KB):
                        ins = mm(PS[:, bank + g, 0:n], w[:, k, :], hT[:, k, t0:t0 + n], start=(k == 0), stop=(k == KB - 1))
                return ins

            def rkv_blocks(i, slots, first=False):
                for s in slots:
                    pe.wait_ge(w_in[s], i * 16 + 16)
                    if not (first and s < 2):
                        pe.wait_ge(z_out, i * 4 + s - 1)
                    project(rkv_ring[:, s], 3 * (s % 2)).then_inc(z_done, 1)

            rkv_blocks(0, range(4), first=True)
            with pe.Fori(1, 3) as i:
                rkv_blocks(i, range(4))
            rkv_blocks(3, range(2))
            pe.wait_ge(z_out, 14)
            for j in range(NP):
                pe.wait_ge(kksq_ready, j + 1)
                for g, (t0, n) in enumerate(SEGS):
                    ins = mm(PS[0:8, g, 0:n], head_in[:, j, :], kksq[:, j % 2, t0:t0 + n], start=(j == 0), stop=(j == NP - 1))
                ins.then_inc(kksum_done, 1)
            pe.wait_ge(inv_ready, 1)
            for j in range(NP):
                if j >= 2:
                    pe.wait_ge(kk_ready, 3 * (j - 1))
                for g, (t0, n) in enumerate(SEGS):
                    mm(PS[:, 3 * (j % 2) + g, 0:n], head_out[0:8, j, :], norm8[0:8, t0:t0 + n], start=True, stop=True) \
                        .then_inc(kkinv_done, 1)

            pe.wait_ge(state_in, 64)
            pe.wait_ge(kk_ready, 3 * NP)
            for d in range(2):
                for j in range(NP):
                    ins = pe.transpose(PS[:, 5 + d, j * P:(j + 1) * P], SI[:, d, j, :], ident)
                ins.then_inc(si_done, 1)

            def four(out_bank, lhs, rhs, n=P, start=True, stop=True):
                for j in range(NP):
                    ins = mm(PS[:, out_bank, j * n:(j + 1) * n], lhs(j), rhs(j), start=start, stop=stop)
                return ins

            def code_products(e, at):
                for q in range(2):
                    for j in range(NP):
                        ins = mm(PS[:, 0, (q * NP + j) * C:(q * NP + j + 1) * C], codes[:, q, e, j * P:(j + 1) * P],
                                 xwa[:, bass.ds(at, C)], start=True, stop=True)
                ins.then_inc(code_done, 1)

            def pe_half(n, d, seq, front):
                e = 1 - d
                if seq:
                    seq_rhs(n - 1, e)
                pe.wait_ge(front_done, n + 1)
                for q, bd in enumerate((BD_B, BD_K)):
                    if q == 1 and not (isinstance(n, int) and n == 0):
                        pe.wait_ge(q_out, n * 5)
                    for b in range(2):
                        for j in (2 * b, 2 * b + 1):
                            ins = mm(PS[:, 1 + 2 * q + b, (j % 2) * 192:(j % 2 + 1) * 192], bd[:, j, :], AR[:, d, j, :],
                                     start=True, stop=True)
                        ins.then_inc(gram_done, 1)
                for j in range(NP):
                    ins = pe.transpose(PS[:, 7, j * P:(j + 1) * P], BD_B[:, j, :], ident)
                ins.then_inc(tr_done, 1)
                for j in range(NP):
                    ins = pe.transpose(PS[:, 0, j * P:(j + 1) * P], BD_K[:, j, :], ident)
                ins.then_inc(tr_done, 1)
                if seq:
                    seq_u(n - 1, e)
                pe.wait_ge(vt_ready, n + 1)
                pe.wait_ge(tr_out, n * 3 + 1)
                for j in range(NP):
                    ins = pe.transpose(PS[:, 7, j * P:(j + 1) * P], BD_V[:, j, :], ident)
                ins.then_inc(tr_done, 1)
                pe.wait_ge(q2_ready, n + 1)
                for j in range(NP):
                    ins = pe.transpose(PS[:, 2, j * P:(j + 1) * P], Q[:, d, j, :], ident)
                ins.then_inc(tq_done, 1)
                if seq:
                    seq_y(n - 1, e)
                for lv in range(len(LEVELS) - 1):
                    last = lv == len(LEVELS) - 2
                    pe.wait_ge(lm_ready, n * 5 + lv + 1)
                    pe.wait_ge(t_out, n * 5 + lv + 1)
                    four(1, lambda j: Lm[:, lv, j, :], lambda j: Tm[:, j, :]).then_inc(lz_done, 1)
                    if lv == 0 and seq:
                        seq_state(n - 1, e)
                    if lv == 1 and front is not None:
                        code_products(e, front)
                    pe.wait_ge(lz_ready, n * 5 + lv + 1)
                    if lv >= 1:
                        pe.wait_ge(q_out, n * 5 + lv)
                    if not last:
                        four(2, lambda j: Q[:, d, j, :], lambda j: Z[:, j, :]).then_inc(tq_done, 1)
                    four(3, lambda j: Z[:, j, :], lambda j: Q[:, d, j, :]).then_inc(tq_done, 1)

            def seq_rhs(n, d):
                pe.wait_ge(s_ready, n + 1)
                if not (isinstance(n, int) and n == 0):
                    pe.wait_ge(y_out, n)
                pe.wait_ge(tr_out, n * 3 + 3)
                pe.wait_ge(gram_out, n * 4 + 4)
                for j in range(NP):
                    mm(PS[:, 5, j * P:(j + 1) * P], AR[:, d, j, 0:P], S[:, d, j, :], start=True, stop=False)
                    ins = mm(PS[:, 5, j * P:(j + 1) * P], GK[:, d, j, 0:P], Vt[:, d, j, :], start=False, stop=True)
                ins.then_inc(rh_done, 1)

            def seq_u(n, d):
                pe.wait_ge(rh_out, n + 1)
                pe.wait_ge(q_out, n * 5 + 5)
                four(6, lambda j: Q[:, d, j, :], lambda j: RH[:, j, :]).then_inc(u_done, 1)

            def seq_y(n, d):
                pe.wait_ge(u_out, n + 1)
                for j in range(NP):
                    out = PS[:, 5, j * C:(j + 1) * C]
                    mm(out, S[:, d, j, :], AR[:, d, j, P:192], start=True, stop=False)
                    mm(out, U[:, j, :], GB[:, d, j, P:192], start=False, stop=False)
                    ins = mm(out, Vt[:, d, j, :], GK[:, d, j, P:192], start=False, stop=True)
                ins.then_inc(y_done, 1)

            def seq_state(n, d):
                for j in range(NP):
                    out = PS[:, 6, j * P:(j + 1) * P]
                    mm(out, Bt[:, d, j, :], U[:, j, :], start=True, stop=False)
                    ins = mm(out, Kt[:, d, j, :], Vt[:, d, j, :], start=False, stop=True)
                ins.then_inc(st_done, 1)

            def keep_state(d, n):
                pe.wait_ge(s_ready, n + 3)
                pe.wait_ge(y_out, n + 1)
                pe.wait_ge(u_out, n + 1)
                for j in range(NP):
                    ins = pe.transpose(PS[:, 5, j * P:(j + 1) * P], S[:, d, j, :], ident)
                ins.then_inc(fin_done, 1)
                pe.wait_ge(fin_read, d + 1)
                pe.wait_ge(switched, d + 1)

            def pe_pair(i, ctx_f, seq=True, last=False):
                pe_half(2 * i, 0, seq, chunk_at(1, i, ctx_f))
                pe_half(2 * i + 1, 1, True, None if last else chunk_at(0, i + 1, ctx_f))

            pe.wait_ge(si_out, 2)
            pe.wait_ge(scan_zeroed, SCAN_ZEROED)
            code_products(0, 0)
            pe_pair(0, True, seq=False)
            with pe.Fori(1, NC_CTX) as i:
                pe_pair(i, True)
            keep_state(0, 2 * NC_CTX - 2)
            pe_pair(NC_CTX, False)
            keep_state(1, 2 * NC_CTX - 1)
            with pe.Fori(NC_CTX + 1, NC - 1) as i:
                pe_pair(i, False)
            pe_pair(NC - 1, False, last=True)
            seq_rhs(NUNIT - 1, 1)
            seq_u(NUNIT - 1, 1)
            seq_y(NUNIT - 1, 1)
            seq_state(NUNIT - 1, 1)

            pe.wait_ge(y_out, NUNIT)
            pe.wait_ge(s_ready, NUNIT + 2)
            pe.wait_ge(rh_out, NUNIT)
            for j in range(NP):
                if j >= 1:
                    pe.wait_ge(yc_ready, 3 * j)
                for g, (t0, n) in enumerate(SEGS):
                    mm(PS[:, g, 0:n], same, ya[:, j, t0:t0 + n], start=True, stop=True).then_inc(mean_done, 1)
                pe.wait_ge(bonus_ready, j + 1)
                if j >= 1:
                    pe.wait_ge(bonus_out, 3 * j)
                for g, (t0, n) in enumerate(SEGS):
                    mm(PS[:, 3 + g, 0:n], same, kTr[:, j, t0:t0 + n], start=True, stop=True).then_inc(mean_done, 1)
            pe.wait_ge(ysq_ready, NP)
            pe.wait_ge(yc_ready, 3 * NP)
            for g, (t0, n) in enumerate(SEGS):
                for j in range(NP):
                    ins = mm(PS[0:8, g, 0:n], head_in[:, j, :], rT[:, j, t0:t0 + n], start=(j == 0), stop=(j == NP - 1))
                ins.then_inc(var_done, 1)
            pe.wait_ge(gate_in, 32)
            pe.wait_ge(bonus_out, 3 * NP)
            for j in range(NP):
                if j >= 1:
                    pe.wait_ge(ya_ready, 3 * j)
                for g, (t0, n) in enumerate(SEGS):
                    mm(PS[:, 3 + g, 0:n], gate_w[:, j * P:(j + 1) * P], sxg[:, t0:t0 + n], start=True, stop=True) \
                        .then_inc(gate_done, 1)
                if j == 0:
                    pe.wait_ge(isd_ready, 1)
                else:
                    pe.wait_ge(gn_out, 3 * j)
                for g, (t0, n) in enumerate(SEGS):
                    mm(PS[:, g, 0:n], head_out[0:8, j, :], norm8b[0:8, t0:t0 + n], start=True, stop=True) \
                        .then_inc(gn_done, 1)

            def first(n):
                return isinstance(n, int) and n == 0

            def all_tokens(bank, w, src, kb):
                for g, (t0, n) in enumerate(SEGS):
                    for k in range(kb):
                        ins = mm(PS[:, bank + g, 0:n], w[:, k, :], src[:, k, t0:t0 + n], start=(k == 0), stop=(k == kb - 1))
                return ins

            def mix_block(n):
                for s, (src, kb) in enumerate(((hT, KB), (ya, NP), (hT, KB), (ybT, NP))):
                    pe.wait_ge(w_in[s], n * 16 + (W4[s] + 1) * 16)
                    if s % 2 == 0 and not (first(n) and s == 0):
                        pe.wait_ge(gate_out, n * 2 + s // 2)
                    if s % 2 == 1 and not (first(n) and s == 1):
                        pe.wait_ge(mix_out, n * 2 + s // 2)
                    all_tokens(3 * (s % 2), w_ring[:, s], src, kb).then_inc(mix_mm, 1)

            pe.wait_ge(ya_ready, 3 * NP)
            pe.wait_ge(gn_out, 3 * NP)
            pe.wait_ge(h_again, 32)
            mix_block(0)
            with pe.Fori(1, KB) as n:
                mix_block(n)

            for b in range(TB):
                pe.wait_ge(x_in[b], 32)
            pe.wait_ge(gate_out, 2 * KB)
            pe.wait_ge(mix_out, 2 * KB)
            for n in range(KB):
                for g, (t0, m) in enumerate(SEGS):
                    if 3 * n + g >= 2:
                        pe.wait_ge(xt_out, 3 * n + g - 1)
                    for b in range(t0 // P, (t0 + m) // P):
                        ins = pe.transpose(PS[:, 6 + (3 * n + g) % 2, b * P - t0:b * P - t0 + P],
                                           x_again[:, b, n * P:(n + 1) * P], ident)
                    ins.then_inc(xt_done, 1)
                    if g == 0:
                        pe.wait_ge(w_in[n % 4], (WO[n % 4] + n // 4 + 1) * 16)
                    if n == 0 and g == 0:
                        pe.wait_ge(mix_ready, KB)
                    if n >= 2:
                        pe.wait_ge(x1_out, 3 * (n - 2) + g + 1)
                    for k in range(KB):
                        ins = mm(PS[:, 3 * (n % 2) + g, 0:m], w_ring[:, n % 4, k, :], mix[:, k, t0:t0 + m],
                                 start=(k == 0), stop=(k == KB - 1))
                    ins.then_inc(wo_mm, 1)
            pe.wait_ge(x1sq_ready, KB)
            pe.wait_ge(xt_out, 3 * KB)
            for b in range(TB):
                for k in range(KB):
                    ins = mm(PS[:, 6, b:b + 1], x1sq[k][:, b * P:(b + 1) * P], ones[:, 0:1], start=(k == 0), stop=(k == KB - 1))
            ins.then_inc(ms_done, 1)
            pe.wait_ge(x1_out, 3 * KB)
            for g, (t0, m) in enumerate(SEGS):
                for b in range(t0 // P, (t0 + m) // P):
                    pe.wait_ge(diag2_ready, b + 1)
                    ins = mm(PS[:, g, b * P - t0:b * P - t0 + P], ones, diag2[:, b, :], start=True, stop=True)
                ins.then_inc(rs_done, 1)

            def ffn_up(f, s, turn, ready=False):
                for q in range(2):
                    pe.wait_ge(w_in[s + q], turn * 16 + WF[s + q] * 16)
                    if not first(f):
                        if q == 0:
                            pe.wait_ge(u_copied, f)
                        else:
                            pe.wait_ge(fact_ready, f)
                    if first(f) and q == 1:
                        pe.wait_ge(h2_scaled, 3 * KB)
                    bank = 3 * (1 - q)
                    for g, (t0, m) in enumerate(SEGS):
                        for k in range(KB):
                            if first(f) and q == 0:
                                pe.wait_ge(h2_ready, g * KB + k + 1)
                            ins = mm(PS[:, bank + g, 0:m], w_ring[:, s + q, k, :], h2T[:, k, t0:t0 + m],
                                     start=(k == 0), stop=(k == KB - 1))
                    ins.then_inc(up_done, 1)

            def ffn_down(g, n, s, turn, wait_banks):
                nf = GROUPS[g][1]
                pe.wait_ge(w_in[s], turn * 16 + WF[s] * 16)
                if wait_banks:
                    pe.wait_ge(down_out, n + (KB * g - 1))
                all_tokens(3 * (s % 2), w_ring[:, s], fact, nf).then_inc(down_done, 1)

            for g, (f0, nf) in enumerate(GROUPS):
                q_up, q_down = ffn_tiles(g)
                if g > 0:
                    pe.wait_ge(down_out, KB * g)
                if g == 0:
                    for s in (0, 2):
                        ffn_up(s // 2, s, 1)
                i0 = 1 if g == 0 else 0
                with pe.Fori(i0, nf // 2) as i:
                    for s in (0, 2):
                        ffn_up(i * 2 + (f0 + s // 2), s, i + (q_up // 4 + 1))
                pe.wait_ge(fact_ready, f0 + nf)
                pe.wait_ge(u_copied, f0 + nf)
                for s in range(4):
                    ffn_down(g, s, s, q_down // 4 + 1, s >= 2)
                with pe.Fori(1, KB // 4) as i:
                    for s in range(4):
                        ffn_down(g, i * 4 + s, s, i + (q_down // 4 + 1), True)
            for b in range(TB):
                pe.wait_ge(down_out, 3 * KB)
                if b >= 4:
                    pe.wait_ge(y_ready, b - 3)
                for k in range(KB):
                    ins = pe.transpose(PS[:, 2 * (b % 4) + k // 4, (k % 4) * P:(k % 4 + 1) * P],
                                       x1[:, k, b * P:(b + 1) * P], ident)
                ins.then_inc(yt_done, 1)

        @block.scalar
        def _(act):
            A = Steps(act, act_steps)
            act.wait_ge(consts_in, 32)
            A.link(act.activation(conds[:, :, :], cond, ACT.Sigmoid))
            for b in range(TB):
                act.wait_ge(x_in[b], 16)
                act.activation(sq[:, b % 2, :], x10[:, b, :], ACT.Square, accum_out=tokstat[:, 0, b:b + 1]) \
                    .then_inc(sumsq_done, 1)
                act.wait_ge(sumsq_done, b + 1)
            act.wait_ge(zeroed, 1)
            act.activation(tokstat[:, 1, :], tokstat[:, 0, :], ACT.Sqrt, bias=eps_c[:, 0:1], scale=1.0 / D) \
                .then_inc(sumsq_done, 1)
            act.wait_ge(gsc_ready, 1)
            for k in range(KB):
                act.wait_ge(h_done, 3 * k + 2)
                act.activation(hT[:, k, 256:768], PS[:, 3 * (k % 2) + 1, :], ACT.Identity,
                               bias=mod[:, k, 1:2], scale=gsc1[:, k, 1:2]).then_inc(h_out_a, 1)

            def attention(i):
                for g, (t0, n) in enumerate(SEGS):
                    act.wait_ge(proj_done, i * 13 + 1 + g + 1)
                    src = PS[:, g, 0:n].rearrange("p (u t) -> p u t", t=64)
                    dst = qbd[:, t0 // 64:(t0 + n) // 64, :]
                    A.step(act.activation(dst[0:64, :, 0:64], src[0:64], ACT.Copy))
                    act.activation(dst[64:128, :, 64:128], src[64:128], ACT.Copy).then_inc(proj_out_a, 1)
                act.wait_ge(proj_done, i * 13 + 1 + 9)
                act.activation(kcT, PS[:, 1, 0:256], ACT.Copy).then_inc(proj_out_a, 1)
                act.wait_ge(newkv_out, i * 32 + 16)
                for n, bank in enumerate((2, 3, 4)):
                    act.wait_ge(proj_done, i * 13 + 1 + 10 + n)
                    nb = min(4, TB - 4 * n)
                    act.activation(vtok[:, 4 * n:4 * n + nb, :].rearrange("p b n -> p (b n)"), PS[:, bank, 0:nb * P], ACT.Copy) \
                        .then_inc(proj_out_a, 1)
                for t in range(NU + 2):
                    if t < NU:
                        u, bank = t, 2 * (t % 2)
                        act.wait_ge(scored, i * NU + u + 1)
                        if u >= 3:
                            act.wait_ge(pt_done, i * NU + u - 2)
                        act.activation(scr[:, u % 3, 512:768], PS[:, bank + 1, 0:256], ACT.Copy, scale=SCALE) \
                            .then_inc(ctx_out, 1)
                    if 1 <= t <= NU:
                        u = t - 1
                        lo = 512 if u < 4 else 0
                        act.wait_ge(recip_ready, i * NU + u + 1)
                        act.activation(scr[:, u % 3, lo:768], scr[:, u % 3, lo:768], ACT.Copy,
                                       scale=rowstat[:, u % 3, 2:3]).then_inc(p_ready, 1)
                    if t >= 2:
                        u = t - 2
                        nb = 2 if u < 4 else 4
                        act.wait_ge(pt_done, i * NU + u + 1)
                        if u >= 1:
                            act.wait_ge(o_done, i * NU + u + 1)
                        act.activation(pT[:, 0:nb, :].rearrange("p b n -> p (b n)"), PS[:, 4, 0:nb * P], ACT.Copy) \
                            .then_inc(pt_out_a, 1)
                    if t < NU:
                        u = t
                        lo = 512 if u < 4 else 0
                        act.wait_ge(max_ready, i * NU + u + 1)
                        act.activation(scr[:, u % 3, lo:768], scr[:, u % 3, lo:768], ACT.Exp,
                                       bias=rowstat[:, u % 3, 0:1], accum_out=rowstat[:, u % 3, 1:2]).then_inc(exp_done, 1)

            act.wait_ge(pool_steps, 1)
            with A.loop(0, NP, 3) as i:
                attention(i)
            def z_copy(idx, s, i=None):
                act.wait_ge(z_done, idx + 1)
                if not (isinstance(idx, int) and idx < 2):
                    act.wait_ge(conv_done, idx - 1)
                for g, (t0, n) in enumerate(SEGS):
                    at = t0 + (1 if g == 0 else 2)
                    ins = act.activation(zpad[:, s % 2, at:at + n], PS[:, 3 * (s % 2) + g, 0:n], ACT.Copy)
                    if g < 2:
                        A.step(ins)
                    else:
                        ins.then_inc(z_out, 1)

            act.wait_ge(zpad_zeroed, 1)
            for s in range(4):
                z_copy(s, s)
            with A.loop(1, 3, 8) as i:
                for s in range(4):
                    z_copy(i * 4 + s, s)
            act.wait_ge(z_done, 13)
            for g, (t0, n) in enumerate(SEGS):
                A.step(act.activation(xwa[0:64, t0:t0 + n], PS[0:64, g, 0:n], ACT.Tanh))
                ins = act.activation(xwa[64:128, t0:t0 + n], PS[64:128, g, 0:n], ACT.Copy)
                if g < 2:
                    A.step(ins)
                else:
                    ins.then_inc(z_out, 1)
            act.wait_ge(z_done, 14)
            for g, (t0, n) in enumerate(SEGS):
                ins = act.activation(sxg[:, t0:t0 + n], PS[:, 3 + g, 0:n], ACT.Sigmoid)
                if g < 2:
                    A.step(ins)
                else:
                    ins.then_inc(z_out, 1)
            for j in range(NP):
                act.wait_ge(kkraw_ready, j + 1)
                if j >= 2:
                    act.wait_ge(kksum_done, j - 1)
                act.activation(kksq[:, j % 2, :], kk[:, j, :], ACT.Square).then_inc(kksq_ready, 1)
            act.wait_ge(kksum_done, NP)
            for g, (t0, n) in enumerate(SEGS):
                act.activation(norm8[0:8, t0:t0 + n], PS[0:8, g, 0:n], ACT.Sqrt).then_inc(norm_ready, 1)
            for d in range(2):
                act.wait_ge(si_done, d + 1)
                act.activation(SI[:, d, :, :].rearrange("p j n -> p (j n)"), PS[:, 5 + d, :], ACT.Copy).then_inc(si_out, 1)

            def flat(v):
                return v.rearrange("p j n -> p (j n)")

            def act_values(n, e, at):
                if not (isinstance(n, int) and n == 0):
                    act.wait_ge(tr_done, n * 3)
                A.step(act.activation(BD_V[0:64, :, 0:64], vT[0:64, :, bass.ds(at, C)], ACT.Copy))
                act.activation(BD_V[64:128, :, 64:128], vT[64:128, :, bass.ds(at, C)], ACT.Copy).then_inc(vt_ready, 1)

            def act_sigmoid(n):
                act.wait_ge(sw_ready, n + 1)
                act.activation(SG[:, :, :, :].rearrange("p q j t -> p (q j t)"), SG[:, :, :, :].rearrange("p q j t -> p (q j t)"),
                               ACT.Sigmoid).then_inc(sig_done, 1)

            def act_decays(n):
                act.wait_ge(e_ready, n + 1)
                if not (isinstance(n, int) and n == 0):
                    act.wait_ge(front_done, n)
                A.step(act.activation(PX[:, 0:2, :, :].rearrange("p q j t -> p (q j t)"),
                                      E[:, :, :, :].rearrange("p q j t -> p (q j t)"), ACT.Exp, scale=-KAPPA))
                act.activation(flat(PX[:, 2, :, :]), flat(E[:, 1, :, :]), ACT.Exp, scale=KAPPA).then_inc(exps_done, 1)

            def act_half(n, d, seq, front):
                e = 1 - d
                if seq:
                    act_rh(n - 1)
                for q, (dst, bank) in enumerate(((Bt, 7), (Kt, 0))):
                    act.wait_ge(tr_done, n * 3 + q + 1)
                    act.activation(flat(dst[:, d, :, :]), PS[:, bank, :], ACT.Copy).then_inc(tr_out, 1)
                if seq:
                    act_u(n - 1)
                act.wait_ge(tr_done, n * 3 + 3)
                act.activation(flat(Vt[:, d, :, :]), PS[:, 7, :], ACT.Copy).then_inc(tr_out, 1)
                act.wait_ge(tq_done, n * 10 + 1)
                act.activation(flat(Tm), PS[:, 2, :], ACT.Copy).then_inc(t_out, 1)
                for lv in range(5):
                    if lv < 4:
                        act.wait_ge(tq_done, n * 10 + 2 * lv + 2)
                        act.activation(flat(Tm), PS[:, 2, :], ACT.Copy).then_inc(t_out, 1)
                    act.wait_ge(tq_done, n * 10 + min(2 * lv + 3, 10))
                    act.activation(flat(Q[:, d, :, :]), PS[:, 3, :], ACT.Copy).then_inc(q_out, 1)
                    if front is not None:
                        if lv == 1:
                            act_sigmoid(n + 1)
                        if lv == 3:
                            act_decays(n + 1)
                if front is not None:
                    act_values(n + 1, e, front)

            def act_rh(n):
                act.wait_ge(rh_done, n + 1)
                act.activation(flat(RH), PS[:, 5, :], ACT.Copy).then_inc(rh_out, 1)

            def act_u(n):
                act.wait_ge(u_done, n + 1)
                act.activation(flat(U), PS[:, 6, :], ACT.Copy).then_inc(u_out, 1)

            def act_keep_state(d):
                act.wait_ge(fin_done, d + 1)
                act.wait_ge(switched, d + 1)
                act.activation(flat(SI[:, d, :, :]), PS[:, 5, :], ACT.Copy).then_inc(fin_read, 1)

            def act_pair(i, ctx_f, seq=True, last=False):
                act_half(2 * i, 0, seq, chunk_at(1, i, ctx_f))
                act_half(2 * i + 1, 1, True, None if last else chunk_at(0, i + 1, ctx_f))

            act.wait_ge(scan_zeroed, SCAN_ZEROED)
            act_sigmoid(0)
            act_decays(0)
            act_values(0, 0, 0)
            act_pair(0, True, seq=False)
            with A.loop(1, NC_CTX, 4) as i:
                act_pair(i, True)
            act_keep_state(0)
            act_pair(NC_CTX, False)
            act_keep_state(1)
            with A.loop(NC_CTX + 1, NC - 1, 4) as i:
                act_pair(i, False)
            act_pair(NC - 1, False, last=True)
            act_rh(NUNIT - 1)
            act_u(NUNIT - 1)
            for j in range(NP):
                act.wait_ge(yc_ready, 3 * j + 3)
                act.activation(rT[:, j, :], ya[:, j, :], ACT.Square).then_inc(ysq_ready, 1)
            for g, (t0, n) in enumerate(SEGS):
                act.wait_ge(var_done, g + 1)
                act.activation(norm8b[0:8, t0:t0 + n], PS[0:8, g, 0:n], ACT.Sqrt, bias=eps_c[0:8, 1:2], scale=1.0 / HD) \
                    .then_inc(sd_ready, 1)

            def first(n):
                return isinstance(n, int) and n == 0

            def mix_gates(n):
                for q in range(2):
                    act.wait_ge(mix_mm, n * 4 + 2 * q + 1)
                    if not first(n):
                        act.wait_ge(mix_ready, n)
                    for g, (t0, m) in enumerate(SEGS):
                        ins = act.activation(gates[:, q, t0:t0 + m], PS[:, g, 0:m], ACT.Sigmoid)
                        if g < 2:
                            A.step(ins)
                        else:
                            ins.then_inc(gate_out, 1)

            mix_gates(0)
            with A.loop(1, KB, 4) as n:
                mix_gates(n)
            for n in range(KB):
                for g, (t0, m) in enumerate(SEGS):
                    act.wait_ge(xt_done, 3 * n + g + 1)
                    act.activation(x1[:, n, t0:t0 + m], PS[:, 6 + (3 * n + g) % 2, 0:m], ACT.Copy).then_inc(xt_out, 1)
                if n >= 1:
                    act.wait_ge(x1_out, 3 * n)
                    act.activation(x1sq[n - 1], x1[:, n - 1, :], ACT.Square).then_inc(x1sq_ready, 1)
            act.wait_ge(x1_out, 3 * KB)
            act.activation(x1sq[KB - 1], x1[:, KB - 1, :], ACT.Square).then_inc(x1sq_ready, 1)
            act.wait_ge(ms_done, 1)
            act.activation(tokstat[:, 0, :], PS[:, 6, 0:TB], ACT.Sqrt, bias=eps_c[:, 0:1], scale=1.0 / D).then_inc(ms_ready, 1)
            for g, (t0, m) in enumerate(SEGS):
                c = 0 if g == 0 else 1
                for k in range(KB):
                    act.wait_ge(h2_scaled, g * KB + k + 1)
                    act.activation(h2T[:, k, t0:t0 + m], h2T[:, k, t0:t0 + m], ACT.Identity, bias=mod[:, 24 + k, c:c + 1]) \
                        .then_inc(h2_ready, 1)

            def u_copy(f, s):
                act.wait_ge(up_done, f * 2 + 1)
                if not (isinstance(f, int) and f < 2):
                    act.wait_ge(uconv_ready, f - 1)
                for g, (t0, m) in enumerate(SEGS):
                    at = t0 + (1 if g == 0 else 2)
                    ins = act.activation(upad[:, s, at:at + m], PS[:, 3 + g, 0:m], ACT.Copy)
                    if g < 2:
                        A.step(ins)
                    else:
                        ins.then_inc(u_copied, 1)
                act.wait_ge(uconv_ready, f + 1)
                if not (isinstance(f, int) and f < 2):
                    act.wait_ge(fact_ready, f - 1)
                act.activation(ugelu[:, s, :], uconv[:, 0:T], ACT.Gelu_apprx_tanh).then_inc(gelu_ready, 1)

            act.wait_ge(upad_zeroed, 1)
            for g, (f0, nf) in enumerate(GROUPS):
                i0 = 0
                if g == 0:
                    u_copy(0, 0)
                    u_copy(1, 1)
                    i0 = 1
                with A.loop(i0, nf // 2, 4) as i:
                    for s in range(2):
                        u_copy(i * 2 + (f0 + s), s)
            for b in range(TB):
                act.wait_ge(yt_done, b + 1)
                if b == 0:
                    act.wait_ge(down_out, 3 * KB)
                else:
                    act.wait_ge(yss_ready, 2 * b)
                banks = PS[:, 2 * (b % 4):2 * (b % 4) + 2, :].rearrange("p a n -> p (a n)")
                act.activation(y_sq, banks, ACT.Square, accum_out=tstat[:, 0, b:b + 1]).then_inc(yss_ready, 1)
                act.wait_ge(yss_ready, 2 * b + 1)
                act.activation(tstat[:, 1, b:b + 1], tstat[:, 0, b:b + 1], ACT.Sqrt, bias=eps_c[:, 0:1], scale=1.0 / D) \
                    .then_inc(yss_ready, 1)

        @block.vector
        def _(dve):
            V = Steps(dve, dve_steps)
            stt, tt, ts = dve.scalar_tensor_tensor, dve.tensor_tensor, dve.tensor_scalar
            dve.memset(eps_c[:, 0:1], EPS).then_inc(zeroed, 1)
            V.step(dve.memset(eps_c[:, 1:2], GN_EPS))
            dve.wait_ge(act_steps, 1)
            tt(conds[:, :, :], conds[:, :, :], cond, ALU.mult).then_inc(cond_ready, 1)
            dve.wait_ge(sumsq_done, TB + 1)
            V.link(dve.reciprocal(tokstat[:, 1, :], tokstat[:, 1, :]))
            for b in range(TB):
                ts(diag[:, b, :], ident, tokstat[:, 1, b:b + 1], None, ALU.mult).then_inc(diag_ready, 1)

            def mod_blocks(a, b):
                tt(mod[:, a:b, :], PS[:, MODB, 2 * a:2 * b].rearrange("p (n c) -> p n c", c=2),
                   par("b_ada")[:, a:b].unsqueeze(2).to_broadcast([P, b - a, 2]), ALU.add).then_inc(mod_done, 1)

            def scale_with_gain(dst, blk, gain, ev):
                V.link(ts(dst[:, :, :], mod[:, blk:blk + KB, :], 1.0, None, ALU.add))
                tt(dst[:, :, :], dst[:, :, :], par(gain).unsqueeze(2).to_broadcast([P, KB, 2]), ALU.mult) \
                    .then_inc(ev, 1)

            dve.wait_ge(ada_used, ADA_FIRST)
            mod_blocks(0, ADA_FIRST)
            dve.wait_ge(mod_done, 1)
            scale_with_gain(gsc1, 8, "norm1", gsc_ready)
            dve.wait_ge(gsc_ready, 1)
            for k in range(KB):
                for g in (0, 2):
                    t0, n = SEGS[g]
                    dve.wait_ge(h_done, 3 * k + g + 1)
                    c = 0 if g == 0 else 1
                    ts(hT[:, k, t0:t0 + n], PS[:, 3 * (k % 2) + g, 0:n], gsc1[:, k, c:c + 1], mod[:, k, c:c + 1],
                       ALU.mult, ALU.add).then_inc(h_out_d, 1)

            def attention(i):
                for g, (t0, n) in enumerate(SEGS):
                    dve.wait_ge(proj_done, i * 13 + 1 + 4 + g)
                    dve.tensor_copy(kT[:, t0:t0 + n], PS[:, 3 + g, 0:n]).then_inc(proj_out_d, 1)
                for n, (bank, d0, nd) in enumerate([(6, 0, 8), (0, 8, 7)]):
                    dve.wait_ge(proj_done, i * 13 + 1 + 7 + n)
                    part = bias[:, d0:d0 + nd, :]
                    V.link(tt(part, PS[:, bank, 0:nd * 64].rearrange("p (d c) -> p d c", c=64),
                              win_ok.unsqueeze(1).to_broadcast([P, nd, 64]), ALU.mult))
                    tt(part, part, win_neg.unsqueeze(1).to_broadcast([P, nd, 64]), ALU.add).then_inc(proj_out_d, 1)
                dve.wait_ge(proj_done, i * 13 + 1 + 13)
                dve.wait_ge(newkv_out, i * 32 + 16)
                dve.tensor_copy(newk[:, :, :].rearrange("p b n -> p (b n)"), PS[:, 5, 0:256]).then_inc(proj_out_d, 1)
                dve.wait_ge(proj_out_d, i * PROJ_D + PROJ_D)
                for t in range(NU + 2):
                    if 1 <= t <= NU:
                        u = t - 1
                        dve.wait_ge(exp_done, i * NU + u + 1)
                        dve.reciprocal(rowstat[:, u % 3, 2:3], rowstat[:, u % 3, 1:2]).then_inc(recip_ready, 1)
                    if t < NU:
                        u, bank = t, 2 * (t % 2)
                        lo = 512 if u < 4 else 0
                        dve.wait_ge(ctx_out, i * NU + u + 1)
                        if u >= 4:
                            _, b0 = unit_window(u)
                            stt(scr[:, u % 3, 0:512], PS[:, bank, :], SCALE,
                                bias[:, b0 // 64:b0 // 64 + 8, :].rearrange("p d c -> p (d c)"), ALU.mult, ALU.add) \
                                .then_inc(win_out, 1)
                            dve.wait_ge(win_out, i * ROWS + u - 3)
                        if u >= 3:
                            dve.wait_ge(p_ready, i * NU + u - 2)
                        dve.tensor_reduce(rowstat[:, u % 3, 0:1], scr[:, u % 3, lo:768], AX.X, ALU.max, negate=True) \
                            .then_inc(max_ready, 1)
                    if t >= 2:
                        u = t - 2
                        if u >= 4:
                            dve.wait_ge(pt_done, i * NU + u + 1)
                            if u >= 1:
                                dve.wait_ge(o_done, i * NU + u + 1)
                            dve.tensor_copy(pT[:, 4:6, :].rearrange("p b n -> p (b n)"), PS[:, 5, 0:256]).then_inc(pt_out_d, 1)
                        dve.wait_ge(o_done, i * NU + u + 2)
                        for h in range(2):
                            dst = ybT[:, bass.ds(i, 1), u * 64:(u + 1) * 64].rearrange("p a t -> p (a t)")
                            dve.tensor_copy(dst[64 * h:64 * h + 64], PS[64 * h:64 * h + 64, 6, 64 * h:64 * h + 64]) \
                                .then_inc(o_out, 1)

            with V.loop(0, NP, 2) as i:
                attention(i)
            dve.wait_ge(ada_used, 48)
            mod_blocks(ADA_FIRST, 48)
            dve.wait_ge(mod_done, 2)
            scale_with_gain(gsc2, 32, "norm2", gsc_ready)
            dve.wait_ge(gsc_ready, 2)
            def conv_taps(name, idx, tap):
                at = PARAMS[name][0]
                return prm[:, bass.ds(idx * 3 + (at + tap), 1)]

            def conv(idx, s):
                dve.wait_ge(z_out, idx + 1)
                V.link(ts(convt, zpad[:, s % 2, 1:ZP - 1], conv_taps("conv_rkv", idx, 1), None, ALU.mult))
                V.link(stt(convt, zpad[:, s % 2, 0:ZP - 2], conv_taps("conv_rkv", idx, 0), convt, ALU.mult, ALU.add))
                dst = rkv[:, bass.ds(idx, 1), :].rearrange("p a t -> p (a t)")
                V.step(stt(dst[:, 0:CTX], zpad[:, s % 2, 2:CTX + 2], conv_taps("conv_rkv", idx, 2), convt[:, 0:CTX],
                           ALU.mult, ALU.add))
                stt(dst[:, CTX:T], zpad[:, s % 2, CTX + 3:ZP], conv_taps("conv_rkv", idx, 2), convt[:, CTX + 1:T + 1],
                    ALU.mult, ALU.add).then_inc(conv_done, 1)
                dve.wait_ge(conv_done, idx + 1)

            for s in range(4):
                conv(s, s)
            with V.loop(1, 3, 12) as i:
                for s in range(4):
                    conv(i * 4 + s, s)
            for j in range(NP):
                ts(kk[:, j, :], kTr[:, j, :], par("k_k", j), None, ALU.mult).then_inc(kkraw_ready, 1)
            dve.wait_ge(norm_ready, 3)
            V.link(ts(norm8[0:8, :], norm8[0:8, :], 1e-12, None, ALU.max))
            dve.reciprocal(norm8[0:8, :], norm8[0:8, :]).then_inc(inv_ready, 1)
            dve.wait_ge(kkraw_ready, NP)
            for j in range(NP):
                for g, (t0, n) in enumerate(SEGS):
                    dve.wait_ge(kkinv_done, 3 * j + g + 1)
                    tt(kk[:, j, t0:t0 + n], kk[:, j, t0:t0 + n], PS[:, 3 * (j % 2) + g, 0:n], ALU.mult).then_inc(kk_ready, 1)
            dve.wait_ge(kk_ready, 3 * NP)
            dve.wait_ge(h_kept, 16)
            for d in range(2):
                dve.memset(S[:, d, :, :], 0.0).then_inc(s_ready, 1)
            dve.wait_ge(scan_zeroed, SCAN_ZEROED)
            dve.wait_ge(codes_in, 16)

            def codes_bias(n, e):
                dve.wait_ge(code_done, n + 1)
                at = PARAMS["bias_wi"][0] + 8 * e
                tt(SG[:, :, :, :].rearrange("p q j t -> p (q j) t"), PS[:, 0, :].rearrange("p (q t) -> p q t", t=C),
                   prm[:, at:at + 8].unsqueeze(2).to_broadcast([P, 8, C]), ALU.add).then_inc(sw_ready, 1)

            def decay_sums(n, e):
                dve.wait_ge(sig_done, n + 1)
                sg, cs, e0, e1 = SG[:, 0, :, :], CS[:, :, :], E[:, 0, :, :], E[:, 1, :, :]
                out = e1 if e == 0 else cs
                V.link(dve.tensor_tensor_scan(out.rearrange("p j t -> p (j t)"), RESET, sg.rearrange("p j t -> p (j t)"),
                                              0.0, ALU.mult, ALU.add))
                if e == 0:
                    tt(e0, e1, sg, ALU.subtract).then_inc(e_ready, 1)
                else:
                    V.link(tt(e0, cs[:, :, C - 1:C].to_broadcast([P, NP, C]), cs, ALU.subtract))
                    tt(e1, e0, sg, ALU.add).then_inc(e_ready, 1)
                V.step(stt(TMP, SG[:, 1, :, :], -1.0, par("k_a").unsqueeze(2).to_broadcast([P, NP, C]), ALU.add, ALU.mult))

            def operands(n, e, at):
                V.settle()
                V.link(stt(TMP, TMP, 1.0, kTr[:, :, bass.ds(at, C)], ALU.add, ALU.mult))
                dve.wait_ge(exps_done, n + 1)
                dve.wait_ge(bk_ready, n + 1)
                if not (isinstance(n, int) and n == 0):
                    dve.wait_ge(tr_done, n * 3)
                for h in range(2):
                    r, c = slice(64 * h, 64 * h + 64), slice(64 * h, 64 * h + 64)
                    V.step(tt(BD_B[r, :, c], BK[r, :, :], PX[r, 2, :, :], ALU.mult))
                    V.step(tt(BD_K[r, :, c], TMP[r, :, :], PX[r, 2, :, :], ALU.mult))
                    V.step(stt(AR[r, e, :, c], kk[r, :, bass.ds(at, C)], -1.0, PX[r, 0, :, :], ALU.mult, ALU.mult))
                V.step(tt(AR[:, e, :, P:192], rT[:, :, bass.ds(at, C)], PX[:, 1, :, :], ALU.mult))
                end = C - 1 if e == 0 else 0
                dve.tensor_copy(PEND[:, e, :].unsqueeze(2), PX[:, 1, :, end:end + 1]).then_inc(front_done, 1)
                V.settle()

            def dve_half(n, d, seq, front, y_at):
                e = 1 - d
                for q, dst in enumerate((GB, GK)):
                    for b in range(2):
                        dve.wait_ge(gram_done, n * 4 + 2 * q + b + 1)
                        tt(dst[:, d, 2 * b:2 * b + 2, :], PS[:, 1 + 2 * q + b, 0:384].rearrange("p (j t) -> p j t", t=192),
                           gram_mask[:, d, :].unsqueeze(1).to_broadcast([P, 2, 192]), ALU.mult).then_inc(gram_out, 1)
                    if q == 0:
                        dve.wait_ge(gram_out, n * 4 + 2)
                        V.link(tt(Q[:, d, :, :], GB[:, d, :, 0:P],
                                  level_mask[:, d, 0, :].unsqueeze(1).to_broadcast([P, NP, P]), ALU.mult))
                        tt(Q[:, d, :, :], Q[:, d, :, :], ident.unsqueeze(1).to_broadcast([P, NP, P]), ALU.add) \
                            .then_inc(q2_ready, 1)
                for lv in range(5):
                    dve.wait_ge(lz_done, n * 5 + lv + 1)
                    tt(Z, PS[:, 1, :].rearrange("p (j t) -> p j t", t=P), ident.unsqueeze(1).to_broadcast([P, NP, P]),
                       ALU.add).then_inc(lz_ready, 1)
                    if lv == 0 and seq:
                        dve_seq(n - 1, e, y_at)
                    if lv == 1 and front is not None:
                        codes_bias(n + 1, e)
                    if lv == 2 and front is not None:
                        decay_sums(n + 1, e)
                if front is not None:
                    operands(n + 1, e, front)

            def dve_seq(n, d, at):
                dve.wait_ge(y_done, n + 1)
                yc = ya[:, :, bass.ds(at, C)]
                tt(yc, yc, PS[:, 5, 0:NP * C].rearrange("p (j t) -> p j t", t=C), ALU.add).then_inc(y_out, 1)
                dve.wait_ge(st_done, n + 1)
                s = S[:, d, :, :]
                V.link(tt(s, s, PS[:, 6, :].rearrange("p (j v) -> p j v", v=P), ALU.add))
                tt(s, s, PEND[:, d, :].unsqueeze(2).to_broadcast([P, NP, P]), ALU.mult).then_inc(s_ready, 1)
                dve.wait_ge(s_ready, n + 3)

            def switch_state(d):
                dve.wait_ge(fin_done, d + 1)
                dve.tensor_copy(S[:, d, :, :], SI[:, d, :, :]).then_inc(switched, 1)
                dve.wait_ge(switched, d + 1)

            def dve_pair(i, ctx_f, seq=True, last=False, ctx_before=None):
                ctx_before = ctx_f if ctx_before is None else ctx_before
                dve_half(2 * i, 0, seq, chunk_at(1, i, ctx_f), chunk_at(1, i - 1, ctx_before))
                dve_half(2 * i + 1, 1, True, None if last else chunk_at(0, i + 1, ctx_f), chunk_at(0, i, ctx_f))

            dve.wait_ge(si_out, 2)
            codes_bias(0, 0)
            decay_sums(0, 0)
            operands(0, 0, 0)
            dve_pair(0, True, seq=False)
            with V.loop(1, NC_CTX, OPS_PAIR) as i:
                dve_pair(i, True)
            switch_state(0)
            dve_pair(NC_CTX, False, ctx_before=True)
            switch_state(1)
            with V.loop(NC_CTX + 1, NC - 1, OPS_PAIR) as i:
                dve_pair(i, False)
            dve_pair(NC - 1, False, last=True)
            dve_seq(NUNIT - 1, 1, chunk_at(1, NC - 1, False))
            dve.wait_ge(y_out, NUNIT)
            for j in range(NP):
                stt(kTr[:, j, :], kTr[:, j, :], par("r_k", j), rT[:, j, :], ALU.mult, ALU.mult).then_inc(bonus_ready, 1)
                for g, (t0, n) in enumerate(SEGS):
                    dve.wait_ge(mean_done, 6 * j + g + 1)
                    stt(ya[:, j, t0:t0 + n], PS[:, g, 0:n], -1.0 / HD, ya[:, j, t0:t0 + n], ALU.mult, ALU.add) \
                        .then_inc(yc_ready, 1)
                for g, (t0, n) in enumerate(SEGS):
                    dve.wait_ge(mean_done, 6 * j + g + 4)
                    tt(vT[:, j, t0:t0 + n], PS[:, 3 + g, 0:n], vT[:, j, t0:t0 + n], ALU.mult).then_inc(bonus_out, 1)
            dve.wait_ge(sd_ready, 3)
            dve.reciprocal(norm8b[0:8, :], norm8b[0:8, :]).then_inc(isd_ready, 1)
            dve.wait_ge(yc_ready, 3 * NP)
            dve.wait_ge(ysq_ready, NP)
            dve.wait_ge(bonus_out, 3 * NP)
            for j in range(NP):
                for g, (t0, n) in enumerate(SEGS):
                    dve.wait_ge(gn_done, 3 * j + g + 1)
                    stt(ya[:, j, t0:t0 + n], ya[:, j, t0:t0 + n], par("gn_w", j), PS[:, g, 0:n], ALU.mult, ALU.mult) \
                        .then_inc(gn_out, 1)
                dve.wait_ge(gn_out, 3 * j + 3)
                V.link(stt(ya[:, j, :], ya[:, j, :], par("gn_b", j), vT[:, j, :], ALU.add, ALU.add))
                for g, (t0, n) in enumerate(SEGS):
                    dve.wait_ge(gate_done, 3 * j + g + 1)
                    tt(ya[:, j, t0:t0 + n], ya[:, j, t0:t0 + n], PS[:, 3 + g, 0:n], ALU.mult).then_inc(ya_ready, 1)

            def mix_products(n):
                out = mix[:, bass.ds(n, 1), :].rearrange("p a t -> p (a t)")
                for q, dst in enumerate((out, gated_b)):
                    dve.wait_ge(gate_out, n * 2 + q + 1)
                    dve.wait_ge(mix_mm, n * 4 + 2 * q + 2)
                    for g, (t0, m) in enumerate(SEGS):
                        ins = tt(dst[:, t0:t0 + m], gates[:, q, t0:t0 + m], PS[:, 3 + g, 0:m], ALU.mult)
                        if g < 2:
                            V.step(ins)
                        else:
                            ins.then_inc(mix_out, 1)
                dve.wait_ge(mix_out, n * 2 + 2)
                tt(out, out, gated_b, ALU.add).then_inc(mix_ready, 1)
                dve.wait_ge(mix_ready, n + 1)

            dve.wait_ge(ya_ready, 3 * NP)
            mix_products(0)
            with V.loop(1, KB, 4) as n:
                mix_products(n)
            for n in range(KB):
                for g, (t0, m) in enumerate(SEGS):
                    c = 0 if g == 0 else 1
                    dve.wait_ge(wo_mm, 3 * n + g + 1)
                    dve.wait_ge(xt_out, 3 * n + g + 1)
                    stt(x1[:, n, t0:t0 + m], PS[:, 3 * (n % 2) + g, 0:m], mod[:, 16 + n, c:c + 1], x1[:, n, t0:t0 + m],
                        ALU.mult, ALU.add).then_inc(x1_out, 1)
            dve.wait_ge(ms_ready, 1)
            V.link(dve.reciprocal(tokstat[:, 1, :], tokstat[:, 0, :]))
            for b in range(TB):
                ts(diag2[:, b, :], ident, tokstat[:, 1, b:b + 1], None, ALU.mult).then_inc(diag2_ready, 1)
            dve.wait_ge(x1_out, 3 * KB)
            for g, (t0, m) in enumerate(SEGS):
                c = 0 if g == 0 else 1
                dve.wait_ge(rs_done, g + 1)
                for k in range(KB):
                    stt(h2T[:, k, t0:t0 + m], x1[:, k, t0:t0 + m], gsc2[:, k, c:c + 1], PS[:, g, 0:m], ALU.mult, ALU.mult) \
                        .then_inc(h2_scaled, 1)

            def ffn_act(f, s, local):
                dve.wait_ge(u_copied, f + 1)
                if not (isinstance(f, int) and f == 0):
                    dve.wait_ge(gelu_ready, f)
                V.link(ts(uconv, upad[:, s, 1:ZP - 1], conv_taps("conv_ffn", f, 1), None, ALU.mult))
                V.link(stt(uconv, upad[:, s, 0:ZP - 2], conv_taps("conv_ffn", f, 0), uconv, ALU.mult, ALU.add))
                V.link(stt(uconv[:, 0:CTX], upad[:, s, 2:CTX + 2], conv_taps("conv_ffn", f, 2), uconv[:, 0:CTX],
                           ALU.mult, ALU.add))
                stt(uconv[:, CTX:T], upad[:, s, CTX + 3:ZP], conv_taps("conv_ffn", f, 2), uconv[:, CTX + 1:T + 1],
                    ALU.mult, ALU.add).then_inc(uconv_ready, 1)
                dve.wait_ge(gelu_ready, f + 1)
                dve.wait_ge(up_done, f * 2 + 2)
                for g, (t0, m) in enumerate(SEGS):
                    dst = fact[:, bass.ds(local, 1), t0:t0 + m].rearrange("p a t -> p (a t)")
                    ins = tt(dst, ugelu[:, s, t0:t0 + m], PS[:, g, 0:m], ALU.mult)
                    if g < 2:
                        V.step(ins)
                    else:
                        ins.then_inc(fact_ready, 1)

            def ffn_add(g, n, s):
                dve.wait_ge(down_done, n + (KB * g + 1))
                for q, (t0, m) in enumerate(SEGS):
                    c = 0 if q == 0 else 1
                    dst = x1[:, bass.ds(n, 1), t0:t0 + m].rearrange("p a t -> p (a t)")
                    gate = mod[:, bass.ds(n + 40, 1), c:c + 1].rearrange("p a c -> p (a c)")
                    ins = stt(dst, PS[:, 3 * (s % 2) + q, 0:m], gate, dst, ALU.mult, ALU.add)
                    if q < 2:
                        V.step(ins)
                    else:
                        ins.then_inc(down_out, 1)

            dve.wait_ge(upad_zeroed, 1)
            for g, (f0, nf) in enumerate(GROUPS):
                i0 = 0
                if g > 0:
                    dve.wait_ge(down_out, KB * g)
                if g == 0:
                    ffn_act(0, 0, 0)
                    ffn_act(1, 1, 1)
                    i0 = 1
                with V.loop(i0, nf // 2, 10) as i:
                    for s in range(2):
                        ffn_act(i * 2 + (f0 + s), s, i * 2 + s)
                with V.loop(0, KB // 4, 8) as i:
                    for s in range(4):
                        ffn_add(g, i * 4 + s, s)
            dve.wait_ge(down_out, 3 * KB)
            dve.wait_ge(gain_in, 16)
            for b in range(TB):
                dve.wait_ge(yss_ready, 2 * b + 2)
                V.link(dve.reciprocal(tstat[:, 1, b:b + 1], tstat[:, 1, b:b + 1]))
                if b >= 4:
                    dve.wait_ge(y_stored[b % 4], 16 * (b // 4))
                banks = PS[:, 2 * (b % 4):2 * (b % 4) + 2, :].rearrange("p a n -> p (a n)")
                stt(y_tok[:, b % 4, :], banks, tstat[:, 1, b:b + 1], gain_f, ALU.mult, ALU.mult).then_inc(y_ready, 1)

        @block.gpsimd
        def _(pool):
            G = Steps(pool, pool_steps)
            pool.wait_ge(h_done, 3 * KB)
            pool.wait_ge(consts_in, 32)
            G.link(pool.memset(qbd[:, :, :], 0.0))
            pool.wait_ge(yb_kept, 16)
            pool.memset(zpad[:, :, :], 0.0).then_inc(zpad_zeroed, 1)
            pool.wait_ge(z_done, 14)
            pool.memset(SI[:, :, :, :], 0.0).then_inc(si_zeroed, 1)
            pool.memset(ya[:, :, :], 0.0).then_inc(scan_zeroed, 1)
            pool.wait_ge(h_kept, 16)
            pool.wait_ge(kk_ready, 3 * NP)
            pool.memset(AR[:, :, :, :], 0.0).then_inc(scan_zeroed, 1)
            for bd in (BD_B, BD_K, BD_V):
                G.step(pool.memset(bd, 0.0))
            pool.wait_ge(sxg_kept, 16)
            pool.memset(RESET, 1.0).then_inc(scan_zeroed, 1)
            pool.wait_ge(scan_zeroed, 3)
            pool.memset(RESET.rearrange("p (j t) -> p j t", t=C)[:, :, 0:1], 0.0).then_inc(scan_zeroed, 1)
            G.settle()
            pool.memset(PEND[:, :, :], 0.0).then_inc(scan_zeroed, 1)

            def pool_keys(n, at):
                pool.wait_ge(sig_done, n + 1)
                if not (isinstance(n, int) and n == 0):
                    pool.wait_ge(front_done, n)
                pool.tensor_tensor(BK, kk[:, :, bass.ds(at, C)], SG[:, 1, :, :], ALU.mult).then_inc(bk_ready, 1)

            def pool_half(n, d, front):
                pool.wait_ge(gram_out, n * 4 + 2)
                for lv in range(5):
                    if not (isinstance(n, int) and n == 0):
                        pool.wait_ge(lz_done, n * 5 + (lv - 4))
                    pool.tensor_tensor(Lm[:, lv, :, :], GB[:, d, :, 0:P],
                                       level_mask[:, d, lv + 1, :].unsqueeze(1).to_broadcast([P, NP, P]), ALU.mult) \
                        .then_inc(lm_ready, 1)
                if front is not None:
                    pool_keys(n + 1, front)

            def pool_pair(i, ctx_f, last=False):
                pool_half(2 * i, 0, chunk_at(1, i, ctx_f))
                pool_half(2 * i + 1, 1, None if last else chunk_at(0, i + 1, ctx_f))

            pool_keys(0, 0)
            pool_pair(0, True)
            with pool.Fori(1, NC_CTX) as i:
                pool_pair(i, True)
            pool_pair(NC_CTX, False)
            with pool.Fori(NC_CTX + 1, NC - 1) as i:
                pool_pair(i, False)
            pool_pair(NC - 1, False, last=True)
            pool.wait_ge(diag2_ready, TB)
            pool.wait_ge(rs_done, 3)
            pool.wait_ge(x1sq_ready, KB)
            pool.memset(upad[:, :, :], 0.0).then_inc(upad_zeroed, 1)


def kernel(**inputs):
    import concourse.bacc as _bacc
    from concourse.bass_utils import run_bass_kernel_spmd as _run

    a = {k: np.asarray(v) for k, v in inputs.items()}
    one = {k: a[k][0] for k in ("w_ada", "b_ada", "w_in", "conv_rkv", "decay_w0", "decay_up", "iclr_a0", "iclr_up",
                                "gate_up", "k_k", "k_a", "r_k", "gn_w", "gn_b", "rel_bias", "w_out_a", "w_out_b",
                                "w_out", "w_ffn_up", "conv_ffn", "w_ffn_down", "norm1_g", "norm2_g")}

    def blocks(w):
        k, n = w.shape
        return w.reshape(k // P, P, n // P, P).transpose(2, 1, 0, 3).reshape(n // P, P, k)

    def per_feature(v, n):
        return v.reshape(-1, n, P).transpose(2, 1, 0).reshape(P, -1)

    params = np.empty((P, N_PARAMS), np.float32)

    def put(name, v):
        at, n = PARAMS[name]
        params[:, at:at + n] = v.reshape(P, n)

    put("cond", per_feature(np.stack([a["c_ctx"], a["c"][0]]), KB))
    put("b_ada", per_feature(one["b_ada"], 48))
    put("norm1", per_feature(one["norm1_g"], KB))
    put("norm2", per_feature(one["norm2_g"], KB))
    put("conv_rkv", per_feature(one["conv_rkv"], 12))
    put("conv_ffn", per_feature(one["conv_ffn"], FB))
    put("bias_wi", np.stack([one["decay_w0"], one["iclr_a0"]], 1).reshape(4, NP, P).transpose(2, 0, 1))
    for name in ("k_k", "k_a", "r_k", "gn_w", "gn_b"):
        put(name, per_feature(one[name].reshape(-1), NP))

    codes = np.zeros((P, 2, 2, NP * P), np.float32)
    codes[0:64, 0] = one["decay_up"].transpose(1, 0, 2)
    codes[64:128, 1] = one["iclr_up"].transpose(1, 0, 2)
    state = a["state_rwkv"][0, 0].reshape(2, NP, P, HD)

    def pairs(x):
        return x[0, 0].reshape(NP, 2, 2, P, HD).transpose(0, 2, 3, 1, 4).reshape(NP, 2, P, P)

    ins = {
        "consts": constants(),
        "params": params,
        "x": np.concatenate([a["x_prompt"][0], a["x_sample"][0]]).reshape(TB, P, D),
        "w_ada": blocks(one["w_ada"]),
        "w_in": blocks(one["w_in"]),
        "w_oa": blocks(one["w_out_a"]),
        "w_ob": blocks(one["w_out_b"]),
        "w_o": blocks(one["w_out"]),
        "w_up": blocks(one["w_ffn_up"]),
        "w_down": blocks(one["w_ffn_down"]),
        "codes": codes.reshape(P, -1),
        "gate_up": one["gate_up"],
        "norm_f": a["norm_f_g"].reshape(1, D),
        "ck": pairs(a["cache_k"]),
        "cv": pairs(a["cache_v"]),
        "rel": np.pad(one["rel_bias"].reshape(-1), (GRID - WIN_C, 2 * GRID)),
        "state": state,
    }
    outs = {"y": (TB, P, D), "new_k": (NP, 2, P, P), "new_v": (NP, 2, P, P), "new_state": (2, NP, P, HD)}
    nc = _bacc.Bacc("TRN2", target_bir_lowering=False, num_devices=1)
    arrays, dram = {}, {}
    for name, v in ins.items():
        arrays[f"in_{name}"] = np.ascontiguousarray(v)
        dram[name] = nc.dram_tensor(f"in_{name}", v.shape, mybir.dt.from_np(v.dtype), kind="ExternalInput").ap()
    for name, shape in outs.items():
        dram[name] = nc.dram_tensor(f"out_{name}", shape, F32, kind="ExternalOutput").ap()
    dram["start"] = nc.dram_tensor("start", (1, 64), F32).ap()
    dram["h_kept"] = nc.dram_tensor("h_kept", (P, KB * T), F32).ap()
    dram["sxg_kept"] = nc.dram_tensor("sxg_kept", (P, T), F32).ap()
    dram["yb_kept"] = nc.dram_tensor("yb_kept", (P, NP * T), F32).ap()
    build(nc, dram)
    r = _run(nc, [arrays], core_ids=[0]).results[0]
    y = r["out_y"].reshape(1, T, D)

    def unpair(x):
        return x.reshape(NP, 2, P, 2, HD).transpose(0, 3, 1, 2, 4).reshape(1, 1, 2 * NP, CTX, HD)

    return (y[:, :CTX], y[:, CTX:], unpair(r["out_new_k"]), unpair(r["out_new_v"]),
            r["out_new_state"].reshape(1, 1, 2, 2 * NP, HD, HD))
```

```python
import concourse.bass as bass
from concourse import mybir
from concourse.alu_op_type import AluOpType as ALU
from contextlib import ExitStack, contextmanager
import numpy as np

F32 = mybir.dt.float32
F32R = mybir.dt.float32r
ACT = mybir.ActivationFunctionType
AX = mybir.AxisListType

P = 128
D = 1024
KB = D // P
CTX, LAT = 256, 1024
T = CTX + LAT
TB = T // P
HD = 64
NP = 4
DFF = 2816
FB = DFF // P
GRID = 64
ROWS = LAT // GRID
WIN_R, WIN_C = 8, 16
NDR = 2 * WIN_R - 1
NDC = 2 * WIN_C - 1
EPS, GN_EPS = 1e-6, 64e-5
KAPPA = 0.606531
SCALE = HD ** -0.5
NEG = -1e30
C = 64
NC_CTX, NC = CTX // C, T // C
LEVELS = [1, 2, 4, 8, 16, 32]
SEGS = [(0, 256), (256, 512), (768, 512)]
B_R, B_CODE, B_XG, B_Q, B_K, B_V, B_GA, B_GB = 0, 12, 13, 14, 18, 22, 26, 34

PARAMS = {}
for _name, _n in [("cond", 16), ("b_ada", 48), ("norm1", 8), ("norm2", 8), ("conv_rkv", 36), ("conv_ffn", 66),
                  ("bias_wi", 16), ("k_k", 4), ("k_a", 4), ("r_k", 4), ("gn_w", 4), ("gn_b", 4)]:
    PARAMS[_name] = (sum(n for _, n in PARAMS.values()), _n)
N_PARAMS = sum(n for _, n in PARAMS.values())

CONSTS = {}
for _name, _n in [("ident", 128), ("ones", 128), ("flip", 128), ("same", 128), ("win_ok", 64), ("win_neg", 64), ("gram", 384),
                  ("level", 2 * len(LEVELS) * 128), ("head_in", 32), ("head_out", 512)]:
    CONSTS[_name] = (sum(n for _, n in CONSTS.values()), _n)
N_CONSTS = sum(n for _, n in CONSTS.values())


def constants():
    p = np.arange(P)
    out = np.zeros((P, N_CONSTS), np.float32)

    def put(name, a):
        at, n = CONSTS[name]
        out[:, at:at + n] = np.asarray(a, np.float32).reshape(P, n)

    same = (p[:, None] // 64) == (p[None, :] // 64)
    put("ident", np.eye(P))
    put("ones", np.ones((P, P)))
    put("same", same)
    put("flip", same & ((p[:, None] % 64) + (p[None, :] % 64) == 63))
    qc, kc = p[:, None] % 64, np.arange(64)[None, :]
    start = np.clip(qc - WIN_C // 2, 0, GRID - WIN_C)
    ok = (kc >= start) & (kc < start + WIN_C)
    put("win_ok", ok)
    put("win_neg", np.where(ok, 0.0, NEG))
    s, t = p[:, None] % 64, p[None, :] % 64
    before = [s < t, s > t]
    put("gram", np.concatenate([np.concatenate([same & b, (b | (s == t))[:, :64]], 1) for b in before], 1))
    lv = []
    for b in before:
        for m in LEVELS:
            lv.append(same & b & (s // (2 * m) == t // (2 * m)) & (s // m != t // m))
    put("level", np.concatenate(lv, 1))
    hin = np.zeros((P, NP, 8))
    hout = np.zeros((P, NP, P))
    for j in range(NP):
        for h in range(2):
            hin[64 * h:64 * h + 64, j, 2 * j + h] = 1
            hout[2 * j + h, j, 64 * h:64 * h + 64] = 1
    put("head_in", hin)
    put("head_out", hout)
    return out


class Steps:

    def __init__(self, eng, sem):
        self.eng, self.sem, self.base, self.n = eng, sem, 0, 0

    def step(self, ins):
        ins.then_inc(self.sem, 1)
        self.n += 1

    def settle(self):
        self.eng.wait_ge(self.sem, self.base + self.n)

    def link(self, ins):
        self.step(ins)
        self.settle()

    @contextmanager
    def loop(self, first, last, per):
        before = self.n
        with self.eng.Fori(first, last) as i:
            self.base, self.n = (i - first) * per + before, 0
            yield i
            assert self.n == per, f"{self.sem}: {self.n} steps in a turn, not {per}"
        self.base, self.n = 0, before + (last - first) * per


def half_ap(view, h):
    return view[64 * h:64 * h + 64]


def build(nc, dram):
    ctx = ExitStack()
    with ctx:
        def sem(name):
            return ctx.enter_context(nc.semaphore(name))

        WORDS = 53200
        MEMORY_AT = -(-nc.sbuf_base // 32) * 32
        placed = []
        PS = ctx.enter_context(nc.psum_tensor("PS", [P, 8, 512], F32))

        def view(at, *dims, dtype=F32):
            n = int(np.prod(dims))
            assert at + n <= WORDS, (at, dims)
            placed.append(nc.alloc_sbuf_tensor_at(f"buffer{len(placed)}", [P, n], dtype, offset=MEMORY_AT + 4 * at, align_bytes=4))
            v = placed[-1][:, :]
            if len(dims) == 2:
                v = v.rearrange("p (a b) -> p a b", b=dims[1])
            if len(dims) == 3:
                v = v.rearrange("p (a b c) -> p a b c", b=dims[1], c=dims[2])
            return v

        class Space:

            def __init__(self, at):
                self.at = at

            def __call__(self, *dims, dtype=F32):
                v = view(self.at, *dims, dtype=dtype)
                self.at += int(np.prod(dims))
                return v

        keep = Space(0)
        cst = keep(N_CONSTS)
        prm = keep(N_PARAMS)
        mod = keep(48, 2)
        gsc1 = keep(KB, 2)
        gsc2 = keep(KB, 2)
        tokstat = keep(2, TB)
        eps_c = keep(2)
        FREE = keep.at

        def const(name, *dims):
            at, n = CONSTS[name]
            v = cst[:, at:at + n]
            if len(dims) == 2:
                v = v.rearrange("p (a b) -> p a b", b=dims[1])
            if len(dims) == 3:
                v = v.rearrange("p (a b c) -> p a b c", b=dims[1], c=dims[2])
            return v

        ones_tile = const("ones").unsqueeze(1).to_broadcast([P, KB, P])
        ident, ones, flip = const("ident"), const("ones"), const("flip")
        win_ok, win_neg = const("win_ok"), const("win_neg")
        gram_mask = const("gram", 2, 192)
        level_mask = const("level", 2, len(LEVELS), 128)
        same = const("same")
        head_in = const("head_in", NP, 8)
        head_out = const("head_out", NP, P)

        def par(name, k=None):
            at, n = PARAMS[name]
            return prm[:, at:at + n] if k is None else prm[:, at + k:at + k + 1]

        cond = par("cond").rearrange("p (k c) -> p k c", c=2)

        RING = WORDS - 6 * KB * P
        ring = Space(RING)
        raw = [ring(KB, P) for _ in range(2)]
        hi, lo = [None, None], [None, None]
        for s in range(2):
            hi[s], lo[s] = ring(KB, P, dtype=F32R), ring(KB, P, dtype=F32R)

        s1 = Space(FREE)
        hH = s1(KB, T, dtype=F32R)
        ybT = s1(NP, T)
        AFTER_YB = s1.at
        LO_AT = AFTER_YB + 12 * T
        h_full = view(LO_AT, KB, T)
        hL = view(LO_AT, KB, T, dtype=F32R)
        UPPER = LO_AT + KB * T
        x10 = s1(TB, D)
        diag = s1(TB, P)
        sq = s1(2, D)
        assert s1.at <= LO_AT
        s2 = Space(AFTER_YB)
        qkv_lo = view(s2.at, 3, KB, P, dtype=F32R)
        qkv_ring = s2(3, KB, P)
        NU = 4 + ROWS
        qbd = s2(NU, P)
        kT = s2(T)
        vtok = s2(TB, P)
        vodd = s2(TB - 3, P)
        kctok = s2(2, P)
        kcT = s2(CTX)
        vctok = s2(2, P)
        bias_flipped = s2(NDR, 64)
        bias = s2(NDR, 64)
        scr = s2(3, 768)
        pT = s2(6, P)
        newk = s2(2, P)
        rowstat = s2(3, 3)
        assert s2.at <= LO_AT
        s2 = Space(UPPER)
        pT = [pT, view(s2.at, 6, P)]
        vT2 = s2(T)
        conds = s2(KB, 2)
        qkv_hi = s2(3, KB, P, dtype=F32R)
        assert s2.at <= WORDS - 4 * KB * P
        ada_ring2 = view(WORDS - 4 * KB * P, 4, KB, P)

        consts_in = sem("consts_in")
        x_in = [sem(f"x_in{b}") for b in range(TB)]
        ada_in = [sem(f"ada_in{s}") for s in range(4)]
        ada_used = sem("ada_used")
        sumsq_done = sem("sumsq_done")
        diag_ready = sem("diag_ready")
        cond_ready = sem("cond_ready")
        mod_done = sem("mod_done")
        gsc_ready = sem("gsc_ready")
        h_done = sem("h_done")
        h_rounded, h_split = sem("h_rounded"), sem("h_split")
        qkv_split = sem("qkv_split")
        h_out_a, h_out_d = sem("h_out_a"), sem("h_out_d")
        act_steps, dve_steps, pool_steps = (sem(n) for n in ("act_steps", "dve_steps", "pool_steps"))

        qkv_in = [sem(f"qkv_in{s}") for s in range(3)]
        cache_in = [sem(f"cache_in{s}") for s in range(3)]
        proj_done = sem("proj_done")
        proj_out_a, proj_out_d = sem("proj_out_a"), sem("proj_out_d")
        vodd_in = sem("vodd_in")
        newkv_out = sem("newkv_out")
        scored = sem("scored")
        win_out, ctx_out = sem("win_out"), sem("ctx_out")
        max_ready, exp_done, recip_ready, p_ready = (sem(n) for n in ("max_ready", "exp_done", "recip_ready", "p_ready"))
        pt_done = sem("pt_done")
        pt_out_a, pt_out_d = sem("pt_out_a"), sem("pt_out_d")
        o_done, o_out = sem("o_done"), sem("o_out")
        zeroed = sem("zeroed")

        MODB = 7
        PROJ = 16
        PROJ_A, PROJ_D = 10, 6

        def unit_window(u):
            r = u - 4
            r0 = min(max(r - WIN_R // 2, 0), ROWS - WIN_R)
            return r0, (r0 - r + WIN_R - 1) * 64

        def unit_keys(u):
            if u < 4:
                return [(vtok, 0), (vtok, 1)]
            r0, _ = unit_window(u)
            src = [(vtok, 2 + r0 // 2 + b) for b in range(4)] if r0 % 2 == 0 else \
                  [(vodd, (r0 - 1) // 2 + b) for b in range(4)]
            return src + [(vctok, 0), (vctok, 1)]

        ADA_FIRST, ADA_PAIR = 16, 8
        ADA_AT = list(range(3, 3 + 2 * ADA_PAIR, 2))

        s3 = Space(AFTER_YB)
        rkv = s3(12, T)
        rT, kTr, vT = rkv[:, 0:4, :], rkv[:, 4:8, :], rkv[:, 8:12, :]
        kk = s3(NP, T)
        KK_AT = LO_AT
        ya = s3(NP, T)
        assert s3.at == UPPER
        xwa = s3(T)
        SXG_AT = s3.at
        sxg = s3(T)
        assert s3.at <= RING
        codes = view(WORDS - 4 * NP * P, 2, 2, NP * P)
        w3 = Space(FREE + KB * T)
        ZP = T + 3
        zpad = w3(2, ZP)
        convt = w3(ZP - 2)
        w3 = Space(FREE + KB * T)
        kksq = w3(2, T)
        inv_tok = w3(TB, 8)
        norm8 = w3(T)
        sd_tok = view(WORDS - TB * 8, TB, 8)
        wk = Space(FREE)
        AR = wk(2, NP, 192)
        GB = wk(2, NP, 192)
        GK = wk(2, NP, 192)
        Bt = wk(2, NP, P)
        Kt = wk(2, NP, P)
        Vt = wk(2, NP, P)
        Q = wk(2, NP, P)
        S = wk(2, NP, P)
        BD_B, BD_K, BD_V = wk(NP, P), wk(NP, P), wk(NP, P)
        Tm, Z = wk(NP, P), wk(NP, P)
        RH, U = wk(NP, P), wk(NP, P)
        E = wk(2, NP, C)
        PX = wk(3, NP, C)
        SG = wk(2, NP, C)
        TMP = wk(NP, C)
        assert wk.at <= AFTER_YB, wk.at
        wk = Space(SXG_AT)
        RESET = wk(NP * C)
        PEND = wk(2, NP)
        BK = wk(NP, C)
        CS = wk(NP, C)
        assert wk.at <= SXG_AT + T
        wk = Space(RING)
        Lm = wk(len(LEVELS) - 1, NP, P)
        SI = wk(2, NP, P)
        assert wk.at <= WORDS - 4 * NP * P, wk.at
        gate_w = codes[:, 0, 0, :]
        norm8b = xwa

        NUNIT = 2 * NC
        yb_kept, h_kept = sem("yb_kept"), sem("h_kept")
        w_in = [sem(f"w_in{s}") for s in range(2)]
        w_split, w_used = sem("w_split"), sem("w_used")
        RKV_TILES = 14
        codes_in, gate_in, state_in = sem("codes_in"), sem("gate_in"), sem("state_in")
        z_out, conv_done = sem("z_out"), sem("conv_done")
        inv_back, inv_in = sem("inv_back"), sem("inv_in")
        kksq_ready, kksum_done, norm_ready, inv_ready, kkinv_done, kk_ready = (
            sem(n) for n in ("kksq_ready", "kksum_done", "norm_ready", "inv_ready", "kkinv_done", "kk_ready"))
        scan_zeroed = sem("scan_zeroed")
        si_done, si_out = sem("si_done"), sem("si_out")
        code_done, sw_ready, sig_done, e_ready, exps_done, bk_ready, front_done, vt_ready = (
            sem(n) for n in ("code_done", "sw_ready", "sig_done", "e_ready", "exps_done", "bk_ready", "front_done", "vt_ready"))
        gram_done, gram_out, tr_done, tr_out = (sem(n) for n in ("gram_done", "gram_out", "tr_done", "tr_out"))
        q2_ready, lm_ready, lz_done, lz_ready, tq_done, t_out, q_out = (
            sem(n) for n in ("q2_ready", "lm_ready", "lz_done", "lz_ready", "tq_done", "t_out", "q_out"))
        rh_done, rh_out, u_done, u_out, y_done, y_out, st_done, s_ready = (
            sem(n) for n in ("rh_done", "rh_out", "u_done", "u_out", "y_done", "y_out", "st_done", "s_ready"))
        fin_done, fin_read, fin_stored, switched = (sem(n) for n in ("fin_done", "fin_read", "fin_stored", "switched"))
        kkraw_ready, sxg_kept, zpad_zeroed, si_zeroed = (sem(n) for n in ("kkraw_ready", "sxg_kept", "zpad_zeroed", "si_zeroed"))
        SCAN_ZEROED = 5
        OPS_PAIR = 25
        bonus_ready, mean_done, yc_ready, bonus_out, ysq_ready = (
            sem(n) for n in ("bonus_ready", "mean_done", "yc_ready", "bonus_out", "ysq_ready"))
        var_done, gn_done, gn_out, gate_done, ya_ready = (
            sem(n) for n in ("var_done", "gn_done", "gn_out", "gate_done", "ya_ready"))

        def chunk_at(d, step, ctx_part):
            if d == 0:
                return step * C
            return step * (-C) + ((NC_CTX - 1) * C if ctx_part else (NC_CTX + NC - 1) * C)

        hL4 = view(FREE + KB * T, KB, T, dtype=F32R)
        yb4 = view(KK_AT, NP, T)
        mix = view(FREE + 2 * KB * T, KB, T)
        mixL = view(FREE + 2 * KB * T, KB, T, dtype=F32R)
        assert FREE + 3 * KB * T == LO_AT
        gates = view(UPPER, 2, T)
        mixH = view(FREE, KB, T, dtype=F32R)
        x_again = view(FREE + KB * T, TB, D)
        X1_AT = KK_AT + 4
        x1 = view(X1_AT, KB, T)
        x1sq = view(UPPER + 4, T)
        x1sq_sum = view(UPPER + 4 + T, T)
        assert UPPER + 4 + 2 * T <= RING
        diag2 = view(FREE + 2 * KB * T, TB, P)

        h2H = view(FREE, KB, T, dtype=F32R)
        h2_scaled_x = view(FREE + KB * T, KB, T)
        h2L = view(FREE + KB * T, KB, T, dtype=F32R)
        s5 = Space(FREE + 2 * KB * T)
        factH = s5(3, T, dtype=F32R)
        factL = view(s5.at, 3, T, dtype=F32R)
        fact = s5(3, T)
        uconv = [s5(ZP - 2), s5(ZP - 2)]
        assert s5.at <= X1_AT
        s5 = Space(X1_AT + KB * T)
        upad = s5(2, ZP)
        assert s5.at <= RING
        y_tok = view(FREE, 4, D)
        y_sq = view(FREE + 4 * D, D)
        gain_f = view(FREE + 5 * D, D)
        tstat = view(FREE + 6 * D, 2, TB)

        GATE_TILE = RKV_TILES
        WO_TILE = GATE_TILE + 2 * KB
        FFN_TILE = WO_TILE + KB
        FFN_USED = FFN_TILE
        W4 = RKV_TILES // 2
        WO = W4 + 2 * KB
        WF = WO + KB // 2

        NG = FB // 2

        def up_at(i, odd):
            if isinstance(i, int) and i == 0:
                return FFN_TILE + 2 * odd, FFN_USED + 2 * odd
            return i * 6 + (FFN_TILE - 2 + 4 * odd), i * 12 + (FFN_USED - 8 + 10 * odd)

        def down_at(i):
            if isinstance(i, int) and i == NG:
                return FFN_TILE + 6 * NG - 2, FFN_USED + 12 * NG - 8
            return i * 6 + FFN_TILE, i * 12 + (FFN_USED - 6)

        h_again, yb_again = sem("h_again"), sem("yb_again")
        mix_mm, gate_out, mix_out, mix_ready, mix_rounded, mix_split = (
            sem(n) for n in ("mix_mm", "gate_out", "mix_out", "mix_ready", "mix_rounded", "mix_split"))
        xt_done, xt_out, x1_out = (sem(n) for n in ("xt_done", "xt_out", "x1_out"))
        x1sq_ready, x1sq_added, ms_done, ms_ready, diag2_ready, rs_done, h2_scaled, h2_rounded, h2_ready = (
            sem(n) for n in ("x1sq_ready", "x1sq_added", "ms_done", "ms_ready", "diag2_ready", "rs_done", "h2_scaled",
                             "h2_rounded", "h2_ready"))
        u_copied, uconv_ready, gelu_ready, fact_ready, fact_rounded, fact_split, down_out, upad_zeroed = (
            sem(n) for n in ("u_copied", "uconv_ready", "gelu_ready", "fact_ready", "fact_rounded", "fact_split",
                             "down_out", "upad_zeroed"))
        gain_in, yt_done, yss_ready, y_ready = (sem(n) for n in ("gain_in", "yt_done", "yss_ready", "y_ready"))
        y_stored = [sem(f"y_stored{s}") for s in range(4)]

        block = ctx.enter_context(nc.Block())

        @block.sync
        def _(sp):
            sp.dma_start(cst, dram["consts"]).then_inc(consts_in, 16)
            sp.dma_start(prm, dram["params"]).then_inc(consts_in, 16)
            for b in range(TB):
                sp.dma_start(x10[:, b, :], dram["x"][b]).then_inc(x_in[b], 16)

            def load_ada(n, s, first=False):
                if not first:
                    sp.wait_ge(ada_used, n - 3)
                sp.dma_start(ada_ring2[:, s, :, :].rearrange("p k n -> p (k n)"),
                             dram["w_ada"][bass.ds(n, 1)].rearrange("a p n -> p (a n)")).then_inc(ada_in[s], 16)

            for n in range(ADA_FIRST):
                load_ada(n, n % 4, first=(n < 4))

            sp.wait_ge(h_done, 3 * KB)
            sp.dma_start(dram["start"], ident[0:1, 0:64]).then_inc(newkv_out, 16)

            def attention(i, first=False):
                for s, col in enumerate((B_Q, B_K, B_V)):
                    sp.wait_ge(proj_done, i * PROJ + 1)
                    sp.dma_start(qkv_ring[:, s].rearrange("p k n -> p (k n)"),
                                 dram["w_in"][bass.ds(i + col, 1)].rearrange("a p n -> p (a n)")).then_inc(qkv_in[s], 16)
                sp.wait_ge(o_done, i * NU + 1)
                sp.dma_start(kctok, dram["ck"][bass.ds(i, 1)].rearrange("a b s c -> s (a b) c")).then_inc(cache_in[0], 16)
                sp.dma_start(vctok, dram["cv"][bass.ds(i, 1)].rearrange("a b s c -> s (a b) c")).then_inc(cache_in[1], 16)
                for hh in range(2):
                    rb = dram["rel"]
                    win = rb[bass.ds(i * (2 * NDR * NDC) + hh * NDR * NDC, 1)]
                    src = bass.AP(win.tensor, win.offset, [[1, 64], [NDC, NDR], [1, 64]])
                    sp.dma_start(half_ap(bias_flipped, hh), src).then_inc(cache_in[2], 16)
                for s in range(4):
                    load_ada(i * ADA_PAIR + (ADA_FIRST + s), s)
                sp.wait_ge(proj_out_a, i * PROJ_A + PROJ_A)
                nodd = TB - 3
                sp.dma_start(vodd[0:64, :, :], vtok[64:128, 2:2 + nodd, :]).then_inc(vodd_in, 16)
                sp.dma_start(vodd[64:128, :, :], vtok[0:64, 3:3 + nodd, :]).then_inc(vodd_in, 16)
                sp.wait_ge(proj_out_d, i * PROJ_D + PROJ_D)
                sp.dma_start(dram["new_k"][bass.ds(i, 1)].rearrange("a b s c -> s (a b) c"), newk[:, :, :]).then_inc(newkv_out, 16)
                sp.dma_start(dram["new_v"][bass.ds(i, 1)].rearrange("a b s c -> s (a b) c"), vtok[:, 0:2, :]).then_inc(newkv_out, 16)
                if first:
                    sp.wait_ge(h_split, KB)
                    for part, kept in enumerate((hH, hL)):
                        sp.dma_start(dram["h_kept"][:, part * KB * T:(part + 1) * KB * T],
                                     kept.bitcast(F32).rearrange("p k t -> p (k t)")).then_inc(h_kept, 16)
                for s in range(4, ADA_PAIR):
                    load_ada(i * ADA_PAIR + (ADA_FIRST + s), s % 4)

            attention(0, first=True)
            with sp.Fori(1, NP) as i:
                attention(i)
            def load_tile(s, src, split=None):
                if split is not None:
                    sp.wait_ge(w_split, split)
                sp.dma_start(raw[s].rearrange("p k n -> p (k n)"), src).then_inc(w_in[s], 16)

            def w_in_block(idx):
                return dram["w_in"][bass.ds(idx, 1)].rearrange("a p n -> p (a n)")

            sp.wait_ge(proj_done, (NP - 1) * PROJ + 1 + 12)
            for s in range(2):
                load_tile(s, w_in_block(s))
            sp.wait_ge(o_out, NP * 2 * NU)
            sp.dma_start(dram["yb_kept"], ybT.rearrange("p j t -> p (j t)")).then_inc(yb_kept, 16)
            with sp.Fori(1, RKV_TILES // 2) as i:
                for s in range(2):
                    load_tile(s, w_in_block(i * 2 + s), i * 2 + (s - 1))
            sp.wait_ge(w_used, RKV_TILES)
            sp.dma_start(codes[:, :, :, :].rearrange("p q d n -> p (q d n)"), dram["codes"]).then_inc(codes_in, 16)
            sp.wait_ge(z_out, 14)
            sp.dma_start(dram["sxg_kept"], sxg).then_inc(sxg_kept, 16)
            sp.wait_ge(si_zeroed, 1)
            for d in range(2):
                for h in range(2):
                    sp.dma_start(SI[64 * h:64 * h + 64, d, :, 64 * h:64 * h + 64],
                                 dram["state"][d, :, 64 * h:64 * h + 64, :].rearrange("j v k -> v j k")).then_inc(state_in, 16)
            for d in range(2):
                sp.wait_ge(fin_read, d + 1)
                for h in range(2):
                    sp.dma_start(dram["new_state"][d, :, 64 * h:64 * h + 64, :].rearrange("j v k -> v j k"),
                                 SI[64 * h:64 * h + 64, d, :, 64 * h:64 * h + 64]).then_inc(fin_stored, 16)
            sp.wait_ge(y_out, NUNIT)
            sp.wait_ge(rh_out, NUNIT)
            sp.wait_ge(s_ready, NUNIT + 2)
            sp.dma_start(gate_w, dram["gate_up"]).then_inc(gate_in, 16)
            sp.dma_start(sxg, dram["sxg_kept"]).then_inc(gate_in, 16)

            sp.dma_start(yb4.rearrange("p j t -> p (j t)"), dram["yb_kept"]).then_inc(yb_again, 16)

            def load_mix(n, first):
                for q, (gate, out) in enumerate(((B_GA, "w_oa"), (B_GB, "w_ob"))):
                    load_tile(0, w_in_block(n + gate), n * 2 + (GATE_TILE + q))
                    if not (first and q == 0):
                        sp.wait_ge(mix_mm, n * 2 + q)
                    sp.dma_start(raw[1][:, 0:NP, :].rearrange("p k n -> p (k n)"),
                                 dram[out][bass.ds(n, 1)].rearrange("a p n -> p (a n)")).then_inc(w_in[1], 16)

            load_mix(0, True)
            with sp.Fori(1, KB) as n:
                load_mix(n, False)
            for n in range(KB):
                if n == 1:
                    sp.wait_ge(mix_mm, 2 * KB)
                load_tile(n % 2, dram["w_o"][n], WO_TILE + n - (0 if n < 2 else 1))
                if n == 1:
                    sp.wait_ge(w_used, WO_TILE)
                    for b in range(TB):
                        sp.dma_start(x_again[:, b, :], dram["x"][b]).then_inc(x_in[b], 16)

            def load_up(i, odd):
                tile, _ = up_at(i, odd)
                for s in range(2):
                    load_tile(s, dram["w_up"][bass.ds(i * 2 + (odd + s * FB), 1)].rearrange("a p n -> p (a n)"), tile + (s - 1))

            def load_down(i):
                tile, _ = down_at(i)
                for s in range(2):
                    load_tile(s, dram["w_down"][bass.ds(i * 2 + (s - 2), 1)].rearrange("a p n -> p (a n)"), tile + (s - 1))

            load_up(0, 0)
            load_up(0, 1)
            with sp.Fori(1, NG) as i:
                load_up(i, 0)
                load_down(i)
                load_up(i, 1)
            load_down(NG)
            sp.wait_ge(w_used, down_at(NG)[1])
            sp.dma_start(gain_f, dram["norm_f"].to_broadcast([P, D])).then_inc(gain_in, 16)
            for b in range(TB):
                sp.wait_ge(y_ready, b + 1)
                sp.dma_start(dram["y"][b], y_tok[:, b % 4, :]).then_inc(y_stored[b % 4], 16)
            for s in range(4):
                sp.wait_ge(y_stored[s], 16 * len(range(s, TB, 4)))
            sp.wait_ge(fin_stored, 64)
            sp.wait_ge(newkv_out, (2 * NP + 1) * 16)

        @block.tensor
        def _(pe):
            mm = pe.matmul

            def split_mm(out, w_hi, w_lo, x_hi, x_lo, start, stop):
                mm(out, w_hi, x_hi, start=start, stop=False)
                mm(out, w_hi, x_lo, start=False, stop=False)
                return mm(out, w_lo, x_hi, start=False, stop=stop)


            def ada_block(n, s, turn):
                pe.wait_ge(ada_in[s], turn * 16)
                for k in range(KB):
                    ins = mm(PS[:, MODB, bass.ds(n * 2, 2)], ada_ring2[:, s, k, :], conds[:, k, :],
                             start=(k == 0), stop=(k == KB - 1))
                ins.then_inc(ada_used, 1)

            pe.wait_ge(cond_ready, 1)
            with pe.Fori(0, ADA_FIRST // 4) as i:
                for s in range(4):
                    ada_block(i * 4 + s, s, i + 1)
            pe.wait_ge(diag_ready, TB)
            for k in range(KB):
                for g, (t0, n) in enumerate(SEGS):
                    bank = 3 * (k % 2) + g
                    if k >= 2:
                        pe.wait_ge(h_out_a if g == 1 else h_out_d, (k - 1) if g == 1 else 2 * (k - 2) + (1 if g == 0 else 2))
                    for b in range(t0 // P, (t0 + n) // P):
                        ins = mm(PS[:, bank, b * P - t0:b * P - t0 + P], x10[:, b, k * P:(k + 1) * P], diag[:, b, :],
                                 start=True, stop=True)
                    ins.then_inc(h_done, 1)
            pe.wait_ge(h_out_a, KB)
            pe.wait_ge(h_out_d, 2 * KB)
            pe.wait_ge(h_split, KB)
            pe.wait_ge(mod_done, 1)
            mm(PS[:, 0, 0:64], ident, ident[:, 0:64], start=True, stop=True).then_inc(proj_done, 1)
            mm(PS[:, 0, 0:64], ident, ident[:, 0:64], start=True, stop=True).then_inc(o_done, 1)

            def attention(i):
                def project(s, g):
                    t0, n = SEGS[g]
                    for k in range(KB):
                        ins = split_mm(PS[:, (0, 3, 2)[s] + g, 0:n], qkv_hi[:, s, k, :], qkv_lo[:, s, k, :],
                                       hH[:, k, t0:t0 + n], hL[:, k, t0:t0 + n], k == 0, k == KB - 1)
                    return ins

                pe.wait_ge(qkv_split, i * 3 + 1)
                for g in range(3):
                    ins = project(0, g)
                    ins.then_inc(proj_done, 1)
                pe.wait_ge(qkv_split, i * 3 + 2)
                for g in range(3):
                    ins = project(1, g)
                    ins.then_inc(proj_done, 1)
                pe.wait_ge(cache_in[2], i * 32 + 32)
                mm(PS[:, 6, 0:512], flip, bias_flipped[:, 0:8, :], start=True, stop=True).then_inc(proj_done, 1)
                pe.wait_ge(proj_out_a, i * PROJ_A + 1)
                mm(PS[:, 0, 0:448], flip, bias_flipped[:, 8:NDR, :], start=True, stop=True).then_inc(proj_done, 1)
                pe.wait_ge(cache_in[0], i * 16 + 16)
                pe.wait_ge(proj_out_a, i * PROJ_A + 2)
                for b in range(2):
                    ins = pe.transpose(PS[:, 1, b * P:(b + 1) * P], kctok[:, b, :], ident)
                ins.then_inc(proj_done, 1)
                pe.wait_ge(qkv_split, i * 3 + 3)
                for n, (bank, ready, at) in enumerate([(2, proj_out_a, i * PROJ_A + 3), (3, proj_out_d, i * PROJ_D + 1),
                                                       (4, proj_out_d, i * PROJ_D + 2)]):
                    pe.wait_ge(ready, at)
                    project(2, n).then_inc(proj_done, 1)
                pe.wait_ge(proj_out_d, i * PROJ_D + 3)
                for b in range(2):
                    ins = pe.transpose(PS[:, 5, b * P:(b + 1) * P], kT[:, b * P:(b + 1) * P], ident)
                ins.then_inc(proj_done, 1)
                pe.wait_ge(proj_out_a, i * PROJ_A + 7)
                for n in range(3):
                    for b in range(4 * n, min(4 * n + 4, TB)):
                        ins = pe.transpose(PS[:, 2 + n, (b % 4) * P:(b % 4 + 1) * P], vT2[:, b * P:(b + 1) * P], ident)
                    ins.then_inc(proj_done, 1)
                pe.wait_ge(proj_out_a, i * PROJ_A + PROJ_A)
                pe.wait_ge(proj_out_d, i * PROJ_D + PROJ_D)
                pe.wait_ge(cache_in[1], i * 16 + 16)

                for t in range(NU + 3):
                    if t < NU:
                        u, bank = t, 2 * (t % 2)
                        if u >= 2:
                            pe.wait_ge(ctx_out, i * NU + (u - 1))
                        if u >= 6:
                            pe.wait_ge(win_out, i * ROWS + (u - 5))
                        if u >= 4:
                            r0, _ = unit_window(u)
                            mm(PS[:, bank, :], qbd[:, u, :], kT[:, CTX + GRID * r0:CTX + GRID * r0 + 512],
                               start=True, stop=True)
                        mm(PS[:, bank + 1, 0:256], qbd[:, u, :], kcT if u >= 4 else kT[:, 0:CTX],
                           start=True, stop=True).then_inc(scored, 1)
                    if 2 <= t < NU + 2:
                        u = t - 2
                        nb = 2 if u < 4 else 6
                        pe.wait_ge(p_ready, i * NU + u + 1)
                        if u >= 1:
                            pe.wait_ge(pt_out_a, i * NU + u)
                        if u >= 5:
                            pe.wait_ge(pt_out_d, i * ROWS + (u - 4))
                        for b in range(nb):
                            at = 512 + b * P if u < 4 else b * P
                            ins = pe.transpose(PS[:, 4 + b // 4, (b % 4) * P:(b % 4 + 1) * P],
                                               scr[:, u % 3, at:at + P], ident)
                        ins.then_inc(pt_done, 1)
                        if t in ADA_AT:
                            s = ADA_AT.index(t)
                            ada_block(i * ADA_PAIR + (ADA_FIRST + s), s % 4, i * 2 + (ADA_FIRST // 4 + s // 4 + 1))
                    if t >= 3:
                        u = t - 3
                        nb = 2 if u < 4 else 6
                        pe.wait_ge(pt_out_a, i * NU + u + 1)
                        if u >= 4:
                            pe.wait_ge(pt_out_d, i * ROWS + (u - 3))
                        if u >= 1:
                            pe.wait_ge(o_out, i * 2 * NU + 2 * u)
                        if u == 4:
                            pe.wait_ge(vodd_in, i * 32 + 32)
                        for b, (src, at) in enumerate(unit_keys(u)):
                            ins = mm(PS[:, 6, 0:P], src[:, at, :], pT[u % 2][:, b, :], start=(b == 0), stop=(b == nb - 1))
                        ins.then_inc(o_done, 1)
                pe.wait_ge(o_out, i * 2 * NU + 2 * NU)

            with pe.Fori(0, NP) as i:
                attention(i)
            pe.wait_ge(o_out, NP * 2 * NU)
            pe.wait_ge(mod_done, 2)

            def project(s, bank):
                for g, (t0, n) in enumerate(SEGS):
                    for k in range(KB):
                        ins = split_mm(PS[:, bank + g, 0:n], hi[s][:, k, :], lo[s][:, k, :], hH[:, k, t0:t0 + n],
                                       hL[:, k, t0:t0 + n], k == 0, k == KB - 1)
                return ins

            def rkv_blocks(i, first=False):
                for s in range(2):
                    pe.wait_ge(w_split, i * 2 + s + 1)
                    if not first:
                        pe.wait_ge(z_out, i * 2 + s - 1)
                    project(s, 3 * s).then_inc(w_used, 1)

            rkv_blocks(0, first=True)
            with pe.Fori(1, RKV_TILES // 2) as i:
                rkv_blocks(i)
            def head_sums(bank, squares, j):
                for b in range(TB):
                    ins = mm(PS[:, bank, 8 * b + 2 * j:8 * b + 2 * j + 2], squares[:, b * P:(b + 1) * P], head_in[:, 0, 0:2],
                             start=True, stop=True)
                return ins

            def inverses_back(bank, tok):
                for g, (t0, n) in enumerate(SEGS):
                    for b in range(t0 // P, (t0 + n) // P):
                        ins = pe.transpose(PS[0:8, bank + g, b * P - t0:b * P - t0 + P], tok[:, b, :], ident)
                    ins.then_inc(inv_back, 1)

            pe.wait_ge(z_out, 14)
            for j in range(NP):
                pe.wait_ge(kksq_ready, j + 1)
                head_sums(0, kksq[:, j % 2, :], j).then_inc(kksum_done, 1)
            pe.wait_ge(inv_ready, 1)
            inverses_back(3, inv_tok)
            for j in range(NP):
                if j >= 2:
                    pe.wait_ge(kk_ready, 3 * (j - 1))
                for g, (t0, n) in enumerate(SEGS):
                    if j == 0:
                        pe.wait_ge(inv_in, g + 1)
                    mm(PS[:, 3 * (j % 2) + g, 0:n], head_out[0:8, j, :], norm8[0:8, t0:t0 + n], start=True, stop=True) \
                        .then_inc(kkinv_done, 1)

            pe.wait_ge(state_in, 64)
            pe.wait_ge(kk_ready, 3 * NP)
            for d in range(2):
                for j in range(NP):
                    ins = pe.transpose(PS[:, 5 + d, j * P:(j + 1) * P], SI[:, d, j, :], ident)
                ins.then_inc(si_done, 1)

            def four(out_bank, lhs, rhs, n=P, start=True, stop=True):
                for j in range(NP):
                    ins = mm(PS[:, out_bank, j * n:(j + 1) * n], lhs(j), rhs(j), start=start, stop=stop)
                return ins

            def code_products(e, at):
                for q in range(2):
                    for j in range(NP):
                        ins = mm(PS[:, 0, (q * NP + j) * C:(q * NP + j + 1) * C], codes[:, q, e, j * P:(j + 1) * P],
                                 xwa[:, bass.ds(at, C)], start=True, stop=True)
                ins.then_inc(code_done, 1)

            def pe_half(n, d, seq, front):
                e = 1 - d
                pe.wait_ge(front_done, n + 1)
                for q, bd in enumerate((BD_B, BD_K)):
                    if q == 1 and seq:
                        seq_u(n - 1, e)
                    if q == 1 and not (isinstance(n, int) and n == 0):
                        pe.wait_ge(q_out, n * 5)
                    for b in range(2):
                        for j in (2 * b, 2 * b + 1):
                            ins = mm(PS[:, 1 + 2 * q + b, (j % 2) * 192:(j % 2 + 1) * 192], bd[:, j, :], AR[:, d, j, :],
                                     start=True, stop=True)
                        ins.then_inc(gram_done, 1)
                for j in range(NP):
                    ins = pe.transpose(PS[:, 7, j * P:(j + 1) * P], BD_B[:, j, :], ident)
                ins.then_inc(tr_done, 1)
                for j in range(NP):
                    ins = pe.transpose(PS[:, 0, j * P:(j + 1) * P], BD_K[:, j, :], ident)
                ins.then_inc(tr_done, 1)
                pe.wait_ge(vt_ready, n + 1)
                pe.wait_ge(tr_out, n * 3 + 1)
                for j in range(NP):
                    ins = pe.transpose(PS[:, 7, j * P:(j + 1) * P], BD_V[:, j, :], ident)
                ins.then_inc(tr_done, 1)
                pe.wait_ge(q2_ready, n + 1)
                for j in range(NP):
                    ins = pe.transpose(PS[:, 2, j * P:(j + 1) * P], Q[:, d, j, :], ident)
                ins.then_inc(tq_done, 1)
                if seq:
                    seq_y(n - 1, e, 0)
                for lv in range(len(LEVELS) - 1):
                    last = lv == len(LEVELS) - 2
                    pe.wait_ge(lm_ready, n * 5 + lv + 1)
                    pe.wait_ge(t_out, n * 5 + lv + 1)
                    four(1, lambda j: Lm[:, lv, j, :], lambda j: Tm[:, j, :]).then_inc(lz_done, 1)
                    if lv == 0 and front is not None:
                        code_products(e, front)
                    if lv in (1, 2) and seq:
                        seq_state(n - 1, e, lv - 1)
                    if lv == 3 and seq:
                        seq_y(n - 1, e, 1)
                    if last:
                        seq_rhs(n, d)
                    pe.wait_ge(lz_ready, n * 5 + lv + 1)
                    if lv >= 1:
                        pe.wait_ge(q_out, n * 5 + lv)
                    if not last:
                        four(2, lambda j: Q[:, d, j, :], lambda j: Z[:, j, :]).then_inc(tq_done, 1)
                    four(3, lambda j: Z[:, j, :], lambda j: Q[:, d, j, :]).then_inc(tq_done, 1)

            def seq_rhs(n, d):
                pe.wait_ge(s_ready, n + 1)
                pe.wait_ge(tr_out, n * 3 + 3)
                pe.wait_ge(gram_out, n * 4 + 4)
                for j in range(NP):
                    mm(PS[:, 4, j * P:(j + 1) * P], AR[:, d, j, 0:P], S[:, d, j, :], start=True, stop=False)
                    ins = mm(PS[:, 4, j * P:(j + 1) * P], GK[:, d, j, 0:P], Vt[:, d, j, :], start=False, stop=True)
                ins.then_inc(rh_done, 1)

            def seq_u(n, d):
                pe.wait_ge(s_ready, n + 2)
                pe.wait_ge(rh_out, n + 1)
                pe.wait_ge(q_out, n * 5 + 5)
                four(6, lambda j: Q[:, d, j, :], lambda j: RH[:, j, :]).then_inc(u_done, 1)

            def seq_y(n, d, half):
                pe.wait_ge(u_out, n + 1)
                if not (isinstance(n, int) and n == 0):
                    pe.wait_ge(y_out, n)
                for j in (2 * half, 2 * half + 1):
                    out = PS[:, 5, j * C:(j + 1) * C]
                    mm(out, S[:, d, j, :], AR[:, d, j, P:192], start=True, stop=False)
                    mm(out, U[:, j, :], GB[:, d, j, P:192], start=False, stop=False)
                    ins = mm(out, Vt[:, d, j, :], GK[:, d, j, P:192], start=False, stop=True)
                if half == 1:
                    ins.then_inc(y_done, 1)

            def seq_state(n, d, half):
                for j in (2 * half, 2 * half + 1):
                    out = PS[:, 6, j * P:(j + 1) * P]
                    mm(out, Bt[:, d, j, :], U[:, j, :], start=True, stop=False)
                    ins = mm(out, Kt[:, d, j, :], Vt[:, d, j, :], start=False, stop=True)
                if half == 1:
                    ins.then_inc(st_done, 1)

            def keep_state(d, n):
                pe.wait_ge(s_ready, n + 3)
                pe.wait_ge(y_out, n + 1)
                pe.wait_ge(u_out, n + 1)
                for j in range(NP):
                    ins = pe.transpose(PS[:, 5, j * P:(j + 1) * P], S[:, d, j, :], ident)
                ins.then_inc(fin_done, 1)
                pe.wait_ge(fin_read, d + 1)
                pe.wait_ge(switched, d + 1)

            def pe_pair(i, ctx_f, seq=True, last=False):
                pe_half(2 * i, 0, seq, chunk_at(1, i, ctx_f))
                pe_half(2 * i + 1, 1, True, None if last else chunk_at(0, i + 1, ctx_f))

            pe.wait_ge(si_out, 2)
            pe.wait_ge(scan_zeroed, SCAN_ZEROED)
            code_products(0, 0)
            pe_pair(0, True, seq=False)
            with pe.Fori(1, NC_CTX) as i:
                pe_pair(i, True)
            keep_state(0, 2 * NC_CTX - 2)
            pe_half(2 * NC_CTX, 0, True, chunk_at(1, NC_CTX, False))
            keep_state(1, 2 * NC_CTX - 1)
            pe_half(2 * NC_CTX + 1, 1, True, chunk_at(0, NC_CTX + 1, False))
            with pe.Fori(NC_CTX + 1, NC - 1) as i:
                pe_pair(i, False)
            pe_pair(NC - 1, False, last=True)
            seq_u(NUNIT - 1, 1)
            for half in range(2):
                seq_y(NUNIT - 1, 1, half)
                seq_state(NUNIT - 1, 1, half)

            pe.wait_ge(y_out, NUNIT)
            pe.wait_ge(s_ready, NUNIT + 2)
            pe.wait_ge(rh_out, NUNIT)
            for j in range(NP):
                if j >= 1:
                    pe.wait_ge(yc_ready, 3 * j)
                for g, (t0, n) in enumerate(SEGS):
                    mm(PS[:, g, 0:n], same, ya[:, j, t0:t0 + n], start=True, stop=True).then_inc(mean_done, 1)
                pe.wait_ge(bonus_ready, j + 1)
                if j >= 1:
                    pe.wait_ge(bonus_out, 3 * j)
                for g, (t0, n) in enumerate(SEGS):
                    mm(PS[:, 3 + g, 0:n], same, kTr[:, j, t0:t0 + n], start=True, stop=True).then_inc(mean_done, 1)
                if j >= 1:
                    pe.wait_ge(ysq_ready, j)
                    head_sums(6, rT[:, j - 1, :], j - 1)
            pe.wait_ge(ysq_ready, NP)
            head_sums(6, rT[:, NP - 1, :], NP - 1).then_inc(var_done, 1)
            pe.wait_ge(yc_ready, 3 * NP)
            pe.wait_ge(gate_in, 32)
            pe.wait_ge(bonus_out, 3 * NP)
            for j in range(NP):
                if j >= 1:
                    pe.wait_ge(ya_ready, 3 * j)
                for g, (t0, n) in enumerate(SEGS):
                    mm(PS[:, 3 + g, 0:n], gate_w[:, j * P:(j + 1) * P], sxg[:, t0:t0 + n], start=True, stop=True) \
                        .then_inc(gate_done, 1)
                if j == 0:
                    pe.wait_ge(inv_ready, 2)
                    inverses_back(0, sd_tok)
                else:
                    pe.wait_ge(gn_out, 3 * j)
                for g, (t0, n) in enumerate(SEGS):
                    if j == 0:
                        pe.wait_ge(inv_in, 3 + g + 1)
                    mm(PS[:, g, 0:n], head_out[0:8, j, :], norm8b[0:8, t0:t0 + n], start=True, stop=True) \
                        .then_inc(gn_done, 1)

            def first(n):
                return isinstance(n, int) and n == 0

            def mix_block(n):
                for q, src in enumerate((ya, yb4)):
                    pe.wait_ge(w_split, n * 2 + (GATE_TILE + q + 1))
                    if not (first(n) and q == 0):
                        pe.wait_ge(gate_out, n * 2 + q)
                    for g, (t0, m) in enumerate(SEGS):
                        for k in range(KB):
                            ins = split_mm(PS[:, g, 0:m], hi[q][:, k, :], lo[q][:, k, :], hH[:, k, t0:t0 + m],
                                           hL4[:, k, t0:t0 + m], k == 0, k == KB - 1)
                    ins.then_inc(w_used, 1)
                    pe.wait_ge(w_in[1], n * 32 + (W4 + q + 1) * 16)
                    if not (first(n) and q == 0):
                        pe.wait_ge(mix_out, n * 2 + q)
                    for g, (t0, m) in enumerate(SEGS):
                        for k in range(NP):
                            ins = mm(PS[:, 3 + g, 0:m], raw[1][:, k, :], src[:, k, t0:t0 + m], start=(k == 0), stop=(k == NP - 1))
                    ins.then_inc(mix_mm, 1)

            pe.wait_ge(ya_ready, 3 * NP)
            pe.wait_ge(gn_out, 3 * NP)
            pe.wait_ge(h_again, 48)
            pe.wait_ge(yb_again, 16)
            mix_block(0)
            with pe.Fori(1, KB) as n:
                mix_block(n)

            pe.wait_ge(gate_out, 2 * KB)
            pe.wait_ge(mix_out, 2 * KB)

            def transpose_x(n, g):
                t0, m = SEGS[g]
                if 3 * n + g >= 2:
                    pe.wait_ge(xt_out, 3 * n + g - 1)
                for b in range(t0 // P, (t0 + m) // P):
                    if n == 0:
                        pe.wait_ge(x_in[b], 32)
                    ins = pe.transpose(PS[:, 6 + (3 * n + g) % 2, b * P - t0:b * P - t0 + P],
                                       x_again[:, b, n * P:(n + 1) * P], ident)
                ins.then_inc(xt_done, 1)

            for n in range(KB):
                s = n % 2
                pe.wait_ge(w_split, WO_TILE + n + 1)
                if n == 0:
                    for k in range(KB):
                        pe.wait_ge(mix_split, k + 1)
                        for g, (t0, m) in enumerate(SEGS):
                            ins = split_mm(PS[:, g, 0:m], hi[0][:, k, :], lo[0][:, k, :], mixH[:, k, t0:t0 + m],
                                           mixL[:, k, t0:t0 + m], k == 0, k == KB - 1)
                for g, (t0, m) in enumerate(SEGS):
                    if n >= 2:
                        pe.wait_ge(x1_out, 3 * (n - 2) + g + 1)
                    for k in range(KB if n > 0 else 0):
                        ins = split_mm(PS[:, 3 * s + g, 0:m], hi[s][:, k, :], lo[s][:, k, :], mixH[:, k, t0:t0 + m],
                                       mixL[:, k, t0:t0 + m], k == 0, k == KB - 1)
                    if g == 2:
                        ins.then_inc(w_used, 1)
                    if n >= 1:
                        transpose_x(n - 1, g)
            for g in range(3):
                transpose_x(KB - 1, g)
            pe.wait_ge(x1sq_added, KB)
            pe.wait_ge(xt_out, 3 * KB)
            for b in range(TB):
                ins = mm(PS[:, 6, b:b + 1], x1sq_sum[:, b * P:(b + 1) * P], ones[:, 0:1], start=True, stop=True)
            ins.then_inc(ms_done, 1)
            pe.wait_ge(x1_out, 3 * KB)
            for g, (t0, m) in enumerate(SEGS):
                for b in range(t0 // P, (t0 + m) // P):
                    pe.wait_ge(diag2_ready, b + 1)
                    ins = mm(PS[:, 3 + g, b * P - t0:b * P - t0 + P], ones, diag2[:, b, :], start=True, stop=True)
                ins.then_inc(rs_done, 1)

            def ffn_up(i, odd):
                tile, _ = up_at(i, odd)
                start = first(i) and odd == 0
                if start:
                    for g, (t0, m) in enumerate(SEGS):
                        for s in range(2):
                            pe.wait_ge(w_split, tile + (s + 1))
                            pe.wait_ge(h2_scaled, (g + 1) * KB)
                            for k in range(KB):
                                if s == 0:
                                    pe.wait_ge(h2_ready, g * KB + k + 1)
                                ins = split_mm(PS[:, 3 * s + g, 0:m], hi[s][:, k, :], lo[s][:, k, :], h2H[:, k, t0:t0 + m],
                                               h2L[:, k, t0:t0 + m], k == 0, k == KB - 1)
                            if g == 2:
                                ins.then_inc(w_used, 1)
                    return
                for s in range(2):
                    pe.wait_ge(w_split, tile + (s + 1))
                    pe.wait_ge((u_copied, fact_ready)[s], i * 2 + odd)
                    if odd and not first(i):
                        pe.wait_ge(down_out, i * KB + (s - 1))
                    for g, (t0, m) in enumerate(SEGS):
                        for k in range(KB):
                            ins = split_mm(PS[:, 3 * s + g, 0:m], hi[s][:, k, :], lo[s][:, k, :], h2H[:, k, t0:t0 + m],
                                           h2L[:, k, t0:t0 + m], k == 0, k == KB - 1)
                    ins.then_inc(w_used, 1)

            def ffn_down(i, slots):
                tile, _ = down_at(i)
                last = isinstance(i, int) and i == NG
                pe.wait_ge(fact_split, i * 2)
                for n in range(KB):
                    s, at = n // 4, n % 4
                    if at == 0:
                        pe.wait_ge(w_split, tile + (s + 1))
                    if n < 2:
                        pe.wait_ge((u_copied, fact_ready)[n], i * 2 + (0 if last else 1))
                    else:
                        pe.wait_ge(down_out, i * KB + (n - 1 - KB))
                    for g, (t0, m) in enumerate(SEGS):
                        for k in range(2):
                            ins = split_mm(PS[:, 3 * (n % 2) + g, 0:m], hi[s][:, 2 * at + k, :], lo[s][:, 2 * at + k, :],
                                           factH[:, slots[k], t0:t0 + m], factL[:, slots[k], t0:t0 + m], k == 0, k == 1)
                    ins.then_inc(w_used, 1)

            def ffn_turn(i, even_slot):
                ffn_up(i, 0)
                ffn_down(i, (3 - even_slot, 0))
                ffn_up(i, 1)

            ffn_up(0, 0)
            ffn_up(0, 1)
            with pe.Fori(0, (NG - 1) // 2) as j:
                ffn_turn(j * 2 + 1, 2)
                ffn_turn(j * 2 + 2, 1)
            ffn_down(NG, (1, 0))
            for b in range(TB):
                pe.wait_ge(down_out, NG * KB)
                if b >= 4:
                    pe.wait_ge(y_ready, b - 3)
                for k in range(KB):
                    ins = pe.transpose(PS[:, 2 * (b % 4) + k // 4, (k % 4) * P:(k % 4 + 1) * P],
                                       x1[:, k, b * P:(b + 1) * P], ident)
                ins.then_inc(yt_done, 1)

        @block.scalar
        def _(act):
            A = Steps(act, act_steps)
            act.wait_ge(consts_in, 32)
            A.link(act.activation(conds[:, :, :], cond, ACT.Sigmoid))
            for b in range(TB):
                act.wait_ge(x_in[b], 16)
                act.activation(sq[:, b % 2, :], x10[:, b, :], ACT.Square, accum_out=tokstat[:, 0, b:b + 1]) \
                    .then_inc(sumsq_done, 1)
                act.wait_ge(sumsq_done, b + 1)
            act.wait_ge(zeroed, 1)
            act.activation(tokstat[:, 1, :], tokstat[:, 0, :], ACT.Sqrt, bias=eps_c[:, 0:1], scale=1.0 / D) \
                .then_inc(sumsq_done, 1)
            act.wait_ge(gsc_ready, 1)

            def round_h(k):
                act.wait_ge(h_out_a, k + 1)
                act.wait_ge(h_out_d, 2 * k + 2)
                act.activation(hH[:, k, :], h_full[:, k, :], ACT.Copy).then_inc(h_rounded, 1)

            for k in range(KB):
                act.wait_ge(h_done, 3 * k + 2)
                act.activation(h_full[:, k, 256:768], PS[:, 3 * (k % 2) + 1, :], ACT.Identity,
                               bias=mod[:, k, 1:2], scale=gsc1[:, k, 1:2]).then_inc(h_out_a, 1)
                if k >= 1:
                    round_h(k - 1)
            round_h(KB - 1)

            def attention(i):
                for g, (t0, n) in enumerate(SEGS):
                    act.wait_ge(proj_done, i * PROJ + 1 + g + 1)
                    src = PS[:, g, 0:n].rearrange("p (u t) -> p u t", t=64)
                    dst = qbd[:, t0 // 64:(t0 + n) // 64, :]
                    A.step(act.activation(dst[0:64, :, 0:64], src[0:64], ACT.Copy))
                    act.activation(dst[64:128, :, 64:128], src[64:128], ACT.Copy).then_inc(proj_out_a, 1)
                act.wait_ge(proj_done, i * PROJ + 1 + 9)
                act.activation(kcT, PS[:, 1, 0:256], ACT.Copy).then_inc(proj_out_a, 1)
                for g, (t0, n) in enumerate(SEGS):
                    act.wait_ge(proj_done, i * PROJ + 1 + 10 + g)
                    act.activation(vT2[:, t0:t0 + n], PS[:, 2 + g, 0:n], ACT.Copy).then_inc(proj_out_a, 1)
                act.wait_ge(newkv_out, i * 32 + 16)
                for n, bank in enumerate((2, 3, 4)):
                    act.wait_ge(proj_done, i * PROJ + 1 + 14 + n)
                    nb = min(4, TB - 4 * n)
                    act.activation(vtok[:, 4 * n:4 * n + nb, :].rearrange("p b n -> p (b n)"), PS[:, bank, 0:nb * P], ACT.Copy) \
                        .then_inc(proj_out_a, 1)
                for t in range(NU + 3):
                    if t < NU:
                        u, bank = t, 2 * (t % 2)
                        act.wait_ge(scored, i * NU + u + 1)
                        if u >= 3:
                            act.wait_ge(pt_done, i * NU + u - 2)
                        act.activation(scr[:, u % 3, 512:768], PS[:, bank + 1, 0:256], ACT.Copy, scale=SCALE) \
                            .then_inc(ctx_out, 1)
                    if 1 <= t <= NU:
                        u = t - 1
                        lo = 512 if u < 4 else 0
                        act.wait_ge(recip_ready, i * NU + u + 1)
                        act.activation(scr[:, u % 3, lo:768], scr[:, u % 3, lo:768], ACT.Copy,
                                       scale=rowstat[:, u % 3, 2:3]).then_inc(p_ready, 1)
                    if 2 <= t < NU + 2:
                        u = t - 2
                        nb = 2 if u < 4 else 4
                        act.wait_ge(pt_done, i * NU + u + 1)
                        if u >= 2:
                            act.wait_ge(o_done, i * NU + u)
                        act.activation(pT[u % 2][:, 0:nb, :].rearrange("p b n -> p (b n)"), PS[:, 4, 0:nb * P], ACT.Copy) \
                            .then_inc(pt_out_a, 1)
                    if t < NU:
                        u = t
                        lo = 512 if u < 4 else 0
                        act.wait_ge(max_ready, i * NU + u + 1)
                        act.activation(scr[:, u % 3, lo:768], scr[:, u % 3, lo:768], ACT.Exp,
                                       bias=rowstat[:, u % 3, 0:1], accum_out=rowstat[:, u % 3, 1:2]).then_inc(exp_done, 1)

            act.wait_ge(pool_steps, 1)
            with A.loop(0, NP, 3) as i:
                attention(i)
            def z_copy(idx, s, i=None):
                act.wait_ge(w_used, idx + 1)
                if not (isinstance(idx, int) and idx < 2):
                    act.wait_ge(conv_done, idx - 1)
                for g, (t0, n) in enumerate(SEGS):
                    at = t0 + (1 if g == 0 else 2)
                    ins = act.activation(zpad[:, s % 2, at:at + n], PS[:, 3 * (s % 2) + g, 0:n], ACT.Copy)
                    if g < 2:
                        A.step(ins)
                    else:
                        ins.then_inc(z_out, 1)

            act.wait_ge(zpad_zeroed, 1)
            for s in range(4):
                z_copy(s, s)
            with A.loop(1, 3, 8) as i:
                for s in range(4):
                    z_copy(i * 4 + s, s)
            act.wait_ge(w_used, 13)
            for g, (t0, n) in enumerate(SEGS):
                A.step(act.activation(xwa[0:64, t0:t0 + n], PS[0:64, g, 0:n], ACT.Tanh))
                ins = act.activation(xwa[64:128, t0:t0 + n], PS[64:128, g, 0:n], ACT.Copy)
                if g < 2:
                    A.step(ins)
                else:
                    ins.then_inc(z_out, 1)
            act.wait_ge(w_used, 14)
            for g, (t0, n) in enumerate(SEGS):
                ins = act.activation(sxg[:, t0:t0 + n], PS[:, 3 + g, 0:n], ACT.Sigmoid)
                if g < 2:
                    A.step(ins)
                else:
                    ins.then_inc(z_out, 1)
            for j in range(NP):
                act.wait_ge(kkraw_ready, j + 1)
                if j >= 2:
                    act.wait_ge(kksum_done, j - 1)
                act.activation(kksq[:, j % 2, :], kk[:, j, :], ACT.Square).then_inc(kksq_ready, 1)
            act.wait_ge(kksum_done, NP)
            act.activation(inv_tok.rearrange("p b h -> p (b h)"), PS[:, 0, 0:TB * 8], ACT.Sqrt).then_inc(norm_ready, 1)
            for g, (t0, n) in enumerate(SEGS):
                act.wait_ge(inv_back, g + 1)
                act.activation(norm8[0:8, t0:t0 + n], PS[0:8, 3 + g, 0:n], ACT.Copy).then_inc(inv_in, 1)
            for d in range(2):
                act.wait_ge(si_done, d + 1)
                act.activation(SI[:, d, :, :].rearrange("p j n -> p (j n)"), PS[:, 5 + d, :], ACT.Copy).then_inc(si_out, 1)

            def flat(v):
                return v.rearrange("p j n -> p (j n)")

            def act_values(n, e, at):
                if not (isinstance(n, int) and n == 0):
                    act.wait_ge(tr_done, n * 3)
                A.step(act.activation(BD_V[0:64, :, 0:64], vT[0:64, :, bass.ds(at, C)], ACT.Copy))
                act.activation(BD_V[64:128, :, 64:128], vT[64:128, :, bass.ds(at, C)], ACT.Copy).then_inc(vt_ready, 1)

            def act_sigmoid(n):
                act.wait_ge(sw_ready, n + 1)
                act.activation(SG[:, :, :, :].rearrange("p q j t -> p (q j t)"), SG[:, :, :, :].rearrange("p q j t -> p (q j t)"),
                               ACT.Sigmoid).then_inc(sig_done, 1)

            def act_decays(n):
                act.wait_ge(e_ready, n + 1)
                if not (isinstance(n, int) and n == 0):
                    act.wait_ge(front_done, n)
                A.step(act.activation(PX[:, 0:2, :, :].rearrange("p q j t -> p (q j t)"),
                                      E[:, :, :, :].rearrange("p q j t -> p (q j t)"), ACT.Exp, scale=-KAPPA))
                act.activation(flat(PX[:, 2, :, :]), flat(E[:, 1, :, :]), ACT.Exp, scale=KAPPA).then_inc(exps_done, 1)

            def act_half(n, d, seq, front):
                e = 1 - d
                if seq:
                    act_u(n - 1)
                for q, (dst, bank) in enumerate(((Bt, 7), (Kt, 0))):
                    act.wait_ge(tr_done, n * 3 + q + 1)
                    act.activation(flat(dst[:, d, :, :]), PS[:, bank, :], ACT.Copy).then_inc(tr_out, 1)
                act.wait_ge(tr_done, n * 3 + 3)
                act.activation(flat(Vt[:, d, :, :]), PS[:, 7, :], ACT.Copy).then_inc(tr_out, 1)
                act.wait_ge(tq_done, n * 10 + 1)
                act.activation(flat(Tm), PS[:, 2, :], ACT.Copy).then_inc(t_out, 1)
                for lv in range(5):
                    if lv < 4:
                        act.wait_ge(tq_done, n * 10 + 2 * lv + 2)
                        act.activation(flat(Tm), PS[:, 2, :], ACT.Copy).then_inc(t_out, 1)
                    else:
                        act_rh(n)
                    act.wait_ge(tq_done, n * 10 + min(2 * lv + 3, 10))
                    act.activation(flat(Q[:, d, :, :]), PS[:, 3, :], ACT.Copy).then_inc(q_out, 1)
                    if front is not None:
                        if lv == 0:
                            act_sigmoid(n + 1)
                        if lv == 2:
                            act_decays(n + 1)
                        if lv == 3:
                            act_values(n + 1, e, front)

            def act_rh(n):
                act.wait_ge(rh_done, n + 1)
                act.activation(flat(RH), PS[:, 4, :], ACT.Copy).then_inc(rh_out, 1)

            def act_u(n):
                act.wait_ge(u_done, n + 1)
                act.activation(flat(U), PS[:, 6, :], ACT.Copy).then_inc(u_out, 1)

            def act_keep_state(d):
                act.wait_ge(fin_done, d + 1)
                act.wait_ge(switched, d + 1)
                act.activation(flat(SI[:, d, :, :]), PS[:, 5, :], ACT.Copy).then_inc(fin_read, 1)

            def act_pair(i, ctx_f, seq=True, last=False):
                act_half(2 * i, 0, seq, chunk_at(1, i, ctx_f))
                act_half(2 * i + 1, 1, True, None if last else chunk_at(0, i + 1, ctx_f))

            act.wait_ge(scan_zeroed, SCAN_ZEROED)
            act_sigmoid(0)
            act_decays(0)
            act_values(0, 0, 0)
            act_pair(0, True, seq=False)
            with A.loop(1, NC_CTX, 4) as i:
                act_pair(i, True)
            act_keep_state(0)
            act_half(2 * NC_CTX, 0, True, chunk_at(1, NC_CTX, False))
            act_keep_state(1)
            act_half(2 * NC_CTX + 1, 1, True, chunk_at(0, NC_CTX + 1, False))
            with A.loop(NC_CTX + 1, NC - 1, 4) as i:
                act_pair(i, False)
            act_pair(NC - 1, False, last=True)
            act_u(NUNIT - 1)
            for j in range(NP):
                act.wait_ge(yc_ready, 3 * j + 3)
                act.activation(rT[:, j, :], ya[:, j, :], ACT.Square).then_inc(ysq_ready, 1)
            act.wait_ge(var_done, 1)
            act.activation(sd_tok.rearrange("p b h -> p (b h)"), PS[:, 6, 0:TB * 8], ACT.Sqrt, bias=eps_c[:, 1:2], scale=1.0 / HD) \
                .then_inc(norm_ready, 1)
            for g, (t0, n) in enumerate(SEGS):
                act.wait_ge(inv_back, 3 + g + 1)
                act.activation(norm8b[0:8, t0:t0 + n], PS[0:8, g, 0:n], ACT.Copy).then_inc(inv_in, 1)

            def first(n):
                return isinstance(n, int) and n == 0

            def mix_gates(n):
                for q in range(2):
                    act.wait_ge(w_used, n * 2 + (GATE_TILE + q + 1))
                    if not first(n):
                        act.wait_ge(mix_ready, n)
                    for g, (t0, m) in enumerate(SEGS):
                        ins = act.activation(gates[:, q, t0:t0 + m], PS[:, g, 0:m], ACT.Sigmoid)
                        if g < 2:
                            A.step(ins)
                        else:
                            ins.then_inc(gate_out, 1)

            mix_gates(0)
            with A.loop(1, KB, 4) as n:
                mix_gates(n)
            act.wait_ge(w_used, WO_TILE)
            for k in range(KB):
                act.wait_ge(mix_ready, k + 1)
                act.activation(mixH[:, k, :], mix[:, k, :], ACT.Copy).then_inc(mix_rounded, 1)
            for n in range(KB):
                act.wait_ge(xt_out, 3 * n + 3)
                if n >= 1:
                    act.wait_ge(x1sq_added, n)
                act.activation(x1sq, x1[:, n, :], ACT.Square).then_inc(x1sq_ready, 1)
            act.wait_ge(ms_done, 1)
            act.activation(tokstat[:, 0, :], PS[:, 6, 0:TB], ACT.Sqrt, bias=eps_c[:, 0:1], scale=1.0 / D).then_inc(ms_ready, 1)
            for g, (t0, m) in enumerate(SEGS):
                c = 0 if g == 0 else 1
                for k in range(KB):
                    act.wait_ge(h2_scaled, g * KB + k + 1)
                    act.activation(h2H[:, k, t0:t0 + m], h2_scaled_x[:, k, t0:t0 + m], ACT.Identity,
                                   bias=mod[:, 24 + k, c:c + 1]).then_inc(h2_rounded, 1)

            def ffn_values(i, odd, slot):
                f = i * 2 + odd
                _, used = up_at(i, odd)
                act.wait_ge(w_used, used + 1)
                if not first(i):
                    act.wait_ge(uconv_ready, f - 1)
                for g, (t0, m) in enumerate(SEGS):
                    at = t0 + (1 if g == 0 else 2)
                    ins = act.activation(upad[:, odd, at:at + m], PS[:, g, 0:m], ACT.Copy)
                    if g < 2:
                        A.step(ins)
                    else:
                        ins.then_inc(u_copied, 1)
                act.wait_ge(uconv_ready, f + 1)
                act.activation(uconv[odd][:, 0:T], uconv[odd][:, 0:T], ACT.Gelu_apprx_tanh).then_inc(gelu_ready, 1)
                act.wait_ge(fact_ready, f + 1)
                act.activation(factH[:, slot, :], fact[:, slot, :], ACT.Copy).then_inc(fact_rounded, 1)

            act.wait_ge(upad_zeroed, 1)
            ffn_values(0, 0, 1)
            ffn_values(0, 1, 0)
            with A.loop(0, (NG - 1) // 2, 8) as j:
                for i, even_slot in ((j * 2 + 1, 2), (j * 2 + 2, 1)):
                    ffn_values(i, 0, even_slot)
                    ffn_values(i, 1, 0)
            for b in range(TB):
                act.wait_ge(yt_done, b + 1)
                if b == 0:
                    act.wait_ge(down_out, NG * KB)
                else:
                    act.wait_ge(yss_ready, 2 * b)
                banks = PS[:, 2 * (b % 4):2 * (b % 4) + 2, :].rearrange("p a n -> p (a n)")
                act.activation(y_sq, banks, ACT.Square, accum_out=tstat[:, 0, b:b + 1]).then_inc(yss_ready, 1)
                act.wait_ge(yss_ready, 2 * b + 1)
                act.activation(tstat[:, 1, b:b + 1], tstat[:, 0, b:b + 1], ACT.Sqrt, bias=eps_c[:, 0:1], scale=1.0 / D) \
                    .then_inc(yss_ready, 1)

        @block.vector
        def _(dve):
            V = Steps(dve, dve_steps)
            stt, tt, ts = dve.scalar_tensor_tensor, dve.tensor_tensor, dve.tensor_scalar
            dve.memset(eps_c[:, 0:1], EPS).then_inc(zeroed, 1)
            V.step(dve.memset(eps_c[:, 1:2], GN_EPS))
            dve.wait_ge(act_steps, 1)
            tt(conds[:, :, :], conds[:, :, :], cond, ALU.mult).then_inc(cond_ready, 1)
            dve.wait_ge(sumsq_done, TB + 1)
            V.link(dve.reciprocal(tokstat[:, 1, :], tokstat[:, 1, :]))
            for b in range(TB):
                ts(diag[:, b, :], ident, tokstat[:, 1, b:b + 1], None, ALU.mult).then_inc(diag_ready, 1)

            def mod_blocks(a, b):
                tt(mod[:, a:b, :], PS[:, MODB, 2 * a:2 * b].rearrange("p (n c) -> p n c", c=2),
                   par("b_ada")[:, a:b].unsqueeze(2).to_broadcast([P, b - a, 2]), ALU.add).then_inc(mod_done, 1)

            def scale_with_gain(dst, blk, gain, ev):
                V.link(ts(dst[:, :, :], mod[:, blk:blk + KB, :], 1.0, None, ALU.add))
                tt(dst[:, :, :], dst[:, :, :], par(gain).unsqueeze(2).to_broadcast([P, KB, 2]), ALU.mult) \
                    .then_inc(ev, 1)

            dve.wait_ge(ada_used, ADA_FIRST)
            mod_blocks(0, ADA_FIRST)
            dve.wait_ge(mod_done, 1)
            scale_with_gain(gsc1, 8, "norm1", gsc_ready)
            dve.wait_ge(gsc_ready, 1)

            def rest_of_h(k):
                dve.wait_ge(h_rounded, k + 1)
                tt(hL[:, k, :], h_full[:, k, :], hH[:, k, :], ALU.subtract).then_inc(h_split, 1)

            for k in range(KB):
                for g in (0, 2):
                    t0, n = SEGS[g]
                    dve.wait_ge(h_done, 3 * k + g + 1)
                    c = 0 if g == 0 else 1
                    ts(h_full[:, k, t0:t0 + n], PS[:, 3 * (k % 2) + g, 0:n], gsc1[:, k, c:c + 1], mod[:, k, c:c + 1],
                       ALU.mult, ALU.add).then_inc(h_out_d, 1)
                if k >= 1:
                    rest_of_h(k - 1)
            rest_of_h(KB - 1)

            def attention(i):
                for g, (t0, n) in enumerate(SEGS):
                    dve.wait_ge(proj_done, i * PROJ + 1 + 4 + g)
                    dve.tensor_copy(kT[:, t0:t0 + n], PS[:, 3 + g, 0:n]).then_inc(proj_out_d, 1)
                for n, (bank, d0, nd) in enumerate([(6, 0, 8), (0, 8, 7)]):
                    dve.wait_ge(proj_done, i * PROJ + 1 + 7 + n)
                    part = bias[:, d0:d0 + nd, :]
                    V.link(tt(part, PS[:, bank, 0:nd * 64].rearrange("p (d c) -> p d c", c=64),
                              win_ok.unsqueeze(1).to_broadcast([P, nd, 64]), ALU.mult))
                    tt(part, part, win_neg.unsqueeze(1).to_broadcast([P, nd, 64]), ALU.add).then_inc(proj_out_d, 1)
                dve.wait_ge(proj_done, i * PROJ + 1 + 13)
                dve.wait_ge(newkv_out, i * 32 + 16)
                dve.tensor_copy(newk[:, :, :].rearrange("p b n -> p (b n)"), PS[:, 5, 0:256]).then_inc(proj_out_d, 1)
                dve.wait_ge(proj_out_d, i * PROJ_D + PROJ_D)
                for t in range(NU + 3):
                    if 1 <= t <= NU:
                        u = t - 1
                        dve.wait_ge(exp_done, i * NU + u + 1)
                        dve.reciprocal(rowstat[:, u % 3, 2:3], rowstat[:, u % 3, 1:2]).then_inc(recip_ready, 1)
                    if t < NU:
                        u, bank = t, 2 * (t % 2)
                        lo = 512 if u < 4 else 0
                        dve.wait_ge(ctx_out, i * NU + u + 1)
                        if u >= 4:
                            _, b0 = unit_window(u)
                            stt(scr[:, u % 3, 0:512], PS[:, bank, :], SCALE,
                                bias[:, b0 // 64:b0 // 64 + 8, :].rearrange("p d c -> p (d c)"), ALU.mult, ALU.add) \
                                .then_inc(win_out, 1)
                            dve.wait_ge(win_out, i * ROWS + u - 3)
                        if u >= 3:
                            dve.wait_ge(p_ready, i * NU + u - 2)
                        dve.tensor_reduce(rowstat[:, u % 3, 0:1], scr[:, u % 3, lo:768], AX.X, ALU.max, negate=True) \
                            .then_inc(max_ready, 1)
                    if 2 <= t < NU + 2:
                        u = t - 2
                        if u >= 4:
                            dve.wait_ge(pt_done, i * NU + u + 1)
                            dve.wait_ge(o_done, i * NU + u)
                            dve.tensor_copy(pT[u % 2][:, 4:6, :].rearrange("p b n -> p (b n)"), PS[:, 5, 0:256]).then_inc(pt_out_d, 1)
                    if t >= 3:
                        u = t - 3
                        dve.wait_ge(o_done, i * NU + u + 2)
                        for h in range(2):
                            dst = ybT[:, bass.ds(i, 1), u * 64:(u + 1) * 64].rearrange("p a t -> p (a t)")
                            dve.tensor_copy(dst[64 * h:64 * h + 64], PS[64 * h:64 * h + 64, 6, 64 * h:64 * h + 64]) \
                                .then_inc(o_out, 1)

            with V.loop(0, NP, 2) as i:
                attention(i)
            dve.wait_ge(ada_used, 48)
            mod_blocks(ADA_FIRST, 48)
            dve.wait_ge(mod_done, 2)
            scale_with_gain(gsc2, 32, "norm2", gsc_ready)
            dve.wait_ge(gsc_ready, 2)
            def conv_taps(name, idx, tap):
                at = PARAMS[name][0]
                return prm[:, bass.ds(idx * 3 + (at + tap), 1)]

            def conv(idx, s):
                dve.wait_ge(z_out, idx + 1)
                V.link(ts(convt, zpad[:, s % 2, 1:ZP - 1], conv_taps("conv_rkv", idx, 1), None, ALU.mult))
                V.link(stt(convt, zpad[:, s % 2, 0:ZP - 2], conv_taps("conv_rkv", idx, 0), convt, ALU.mult, ALU.add))
                dst = rkv[:, bass.ds(idx, 1), :].rearrange("p a t -> p (a t)")
                V.step(stt(dst[:, 0:CTX], zpad[:, s % 2, 2:CTX + 2], conv_taps("conv_rkv", idx, 2), convt[:, 0:CTX],
                           ALU.mult, ALU.add))
                stt(dst[:, CTX:T], zpad[:, s % 2, CTX + 3:ZP], conv_taps("conv_rkv", idx, 2), convt[:, CTX + 1:T + 1],
                    ALU.mult, ALU.add).then_inc(conv_done, 1)
                dve.wait_ge(conv_done, idx + 1)

            for s in range(4):
                conv(s, s)
            with V.loop(1, 3, 12) as i:
                for s in range(4):
                    conv(i * 4 + s, s)
            dve.wait_ge(w_used, RKV_TILES)
            dve.wait_ge(h_kept, 32)
            for j in range(NP):
                ts(kk[:, j, :], kTr[:, j, :], par("k_k", j), None, ALU.mult).then_inc(kkraw_ready, 1)
            dve.wait_ge(norm_ready, 1)
            V.link(ts(inv_tok, inv_tok, 1e-12, None, ALU.max))
            dve.reciprocal(inv_tok, inv_tok).then_inc(inv_ready, 1)
            dve.wait_ge(kkraw_ready, NP)
            for j in range(NP):
                for g, (t0, n) in enumerate(SEGS):
                    dve.wait_ge(kkinv_done, 3 * j + g + 1)
                    tt(kk[:, j, t0:t0 + n], kk[:, j, t0:t0 + n], PS[:, 3 * (j % 2) + g, 0:n], ALU.mult).then_inc(kk_ready, 1)
            dve.wait_ge(kk_ready, 3 * NP)
            for d in range(2):
                dve.memset(S[:, d, :, :], 0.0).then_inc(s_ready, 1)
            dve.wait_ge(scan_zeroed, SCAN_ZEROED)
            dve.wait_ge(codes_in, 16)

            def codes_bias(n, e):
                dve.wait_ge(code_done, n + 1)
                at = PARAMS["bias_wi"][0] + 8 * e
                tt(SG[:, :, :, :].rearrange("p q j t -> p (q j) t"), PS[:, 0, :].rearrange("p (q t) -> p q t", t=C),
                   prm[:, at:at + 8].unsqueeze(2).to_broadcast([P, 8, C]), ALU.add).then_inc(sw_ready, 1)

            def decay_sums(n, e, at):
                dve.wait_ge(sig_done, n + 1)
                sg, cs, e0, e1 = SG[:, 0, :, :], CS[:, :, :], E[:, 0, :, :], E[:, 1, :, :]
                out = e1 if e == 0 else cs
                V.link(dve.tensor_tensor_scan(out.rearrange("p j t -> p (j t)"), RESET, sg.rearrange("p j t -> p (j t)"),
                                              0.0, ALU.mult, ALU.add))
                if e == 0:
                    tt(e0, e1, sg, ALU.subtract).then_inc(e_ready, 1)
                else:
                    V.link(tt(e0, cs[:, :, C - 1:C].to_broadcast([P, NP, C]), cs, ALU.subtract))
                    tt(e1, e0, sg, ALU.add).then_inc(e_ready, 1)
                V.link(stt(TMP, SG[:, 1, :, :], -1.0, par("k_a").unsqueeze(2).to_broadcast([P, NP, C]), ALU.add, ALU.mult))
                V.link(stt(TMP, TMP, 1.0, kTr[:, :, bass.ds(at, C)], ALU.add, ALU.mult))

            def key_operands(n, e):
                dve.wait_ge(exps_done, n + 1)
                dve.wait_ge(bk_ready, n + 1)
                if not (isinstance(n, int) and n == 0):
                    dve.wait_ge(tr_done, n * 3)
                for h in range(2):
                    r, c = slice(64 * h, 64 * h + 64), slice(64 * h, 64 * h + 64)
                    V.step(tt(BD_B[r, :, c], BK[r, :, :], PX[r, 2, :, :], ALU.mult))
                    V.step(tt(BD_K[r, :, c], TMP[r, :, :], PX[r, 2, :, :], ALU.mult))

            def operands(n, e, at):
                for h in range(2):
                    r, c = slice(64 * h, 64 * h + 64), slice(64 * h, 64 * h + 64)
                    V.step(stt(AR[r, e, :, c], kk[r, :, bass.ds(at, C)], -1.0, PX[r, 0, :, :], ALU.mult, ALU.mult))
                V.step(tt(AR[:, e, :, P:192], rT[:, :, bass.ds(at, C)], PX[:, 1, :, :], ALU.mult))
                end = C - 1 if e == 0 else 0
                dve.tensor_copy(PEND[:, e, :].unsqueeze(2), PX[:, 1, :, end:end + 1]).then_inc(front_done, 1)
                V.settle()

            def dve_half(n, d, seq, front, y_at):
                e = 1 - d
                for q, dst in enumerate((GB, GK)):
                    for b in range(2):
                        dve.wait_ge(gram_done, n * 4 + 2 * q + b + 1)
                        tt(dst[:, d, 2 * b:2 * b + 2, :], PS[:, 1 + 2 * q + b, 0:384].rearrange("p (j t) -> p j t", t=192),
                           gram_mask[:, d, :].unsqueeze(1).to_broadcast([P, 2, 192]), ALU.mult).then_inc(gram_out, 1)
                    if q == 0:
                        dve.wait_ge(gram_out, n * 4 + 2)
                        V.link(tt(Q[:, d, :, :], GB[:, d, :, 0:P],
                                  level_mask[:, d, 0, :].unsqueeze(1).to_broadcast([P, NP, P]), ALU.mult))
                        tt(Q[:, d, :, :], Q[:, d, :, :], ident.unsqueeze(1).to_broadcast([P, NP, P]), ALU.add) \
                            .then_inc(q2_ready, 1)
                for lv in range(5):
                    dve.wait_ge(lz_done, n * 5 + lv + 1)
                    tt(Z, PS[:, 1, :].rearrange("p (j t) -> p j t", t=P), ident.unsqueeze(1).to_broadcast([P, NP, P]),
                       ALU.add).then_inc(lz_ready, 1)
                    if lv == 3 and seq:
                        dve_seq(n - 1, e, y_at)
                    if lv == 3 and front is not None:
                        key_operands(n + 1, e)
                    if lv == 0 and front is not None:
                        codes_bias(n + 1, e)
                    if lv == 1 and front is not None:
                        decay_sums(n + 1, e, front)
                if front is not None:
                    operands(n + 1, e, front)

            def dve_seq(n, d, at):
                dve.wait_ge(y_done, n + 1)
                yc = ya[:, :, bass.ds(at, C)]
                tt(yc, yc, PS[:, 5, 0:NP * C].rearrange("p (j t) -> p j t", t=C), ALU.add).then_inc(y_out, 1)
                dve.wait_ge(st_done, n + 1)
                s = S[:, d, :, :]
                V.link(tt(s, s, PS[:, 6, :].rearrange("p (j v) -> p j v", v=P), ALU.add))
                tt(s, s, PEND[:, d, :].unsqueeze(2).to_broadcast([P, NP, P]), ALU.mult).then_inc(s_ready, 1)
                dve.wait_ge(s_ready, n + 3)

            def switch_state(d):
                dve.wait_ge(fin_done, d + 1)
                dve.tensor_copy(S[:, d, :, :], SI[:, d, :, :]).then_inc(switched, 1)
                dve.wait_ge(switched, d + 1)

            def dve_pair(i, ctx_f, seq=True, last=False):
                dve_half(2 * i, 0, seq, chunk_at(1, i, ctx_f), chunk_at(1, i - 1, ctx_f))
                dve_half(2 * i + 1, 1, True, None if last else chunk_at(0, i + 1, ctx_f), chunk_at(0, i, ctx_f))

            dve.wait_ge(si_out, 2)
            codes_bias(0, 0)
            decay_sums(0, 0, 0)
            key_operands(0, 0)
            operands(0, 0, 0)
            dve_pair(0, True, seq=False)
            with V.loop(1, NC_CTX, OPS_PAIR) as i:
                dve_pair(i, True)
            switch_state(0)
            dve_half(2 * NC_CTX, 0, True, chunk_at(1, NC_CTX, False), chunk_at(1, NC_CTX - 1, True))
            switch_state(1)
            dve_half(2 * NC_CTX + 1, 1, True, chunk_at(0, NC_CTX + 1, False), chunk_at(0, NC_CTX, False))
            with V.loop(NC_CTX + 1, NC - 1, OPS_PAIR) as i:
                dve_pair(i, False)
            dve_pair(NC - 1, False, last=True)
            dve_seq(NUNIT - 1, 1, chunk_at(1, NC - 1, False))
            dve.wait_ge(y_out, NUNIT)
            for j in range(NP):
                stt(kTr[:, j, :], kTr[:, j, :], par("r_k", j), rT[:, j, :], ALU.mult, ALU.mult).then_inc(bonus_ready, 1)
                for g, (t0, n) in enumerate(SEGS):
                    dve.wait_ge(mean_done, 6 * j + g + 1)
                    stt(ya[:, j, t0:t0 + n], PS[:, g, 0:n], -1.0 / HD, ya[:, j, t0:t0 + n], ALU.mult, ALU.add) \
                        .then_inc(yc_ready, 1)
                for g, (t0, n) in enumerate(SEGS):
                    dve.wait_ge(mean_done, 6 * j + g + 4)
                    tt(vT[:, j, t0:t0 + n], PS[:, 3 + g, 0:n], vT[:, j, t0:t0 + n], ALU.mult).then_inc(bonus_out, 1)
            dve.wait_ge(norm_ready, 2)
            dve.reciprocal(sd_tok, sd_tok).then_inc(inv_ready, 1)
            dve.wait_ge(yc_ready, 3 * NP)
            dve.wait_ge(ysq_ready, NP)
            dve.wait_ge(bonus_out, 3 * NP)
            for j in range(NP):
                for g, (t0, n) in enumerate(SEGS):
                    dve.wait_ge(gn_done, 3 * j + g + 1)
                    stt(ya[:, j, t0:t0 + n], ya[:, j, t0:t0 + n], par("gn_w", j), PS[:, g, 0:n], ALU.mult, ALU.mult) \
                        .then_inc(gn_out, 1)
                dve.wait_ge(gn_out, 3 * j + 3)
                V.link(stt(ya[:, j, :], ya[:, j, :], par("gn_b", j), vT[:, j, :], ALU.add, ALU.add))
                for g, (t0, n) in enumerate(SEGS):
                    dve.wait_ge(gate_done, 3 * j + g + 1)
                    tt(ya[:, j, t0:t0 + n], ya[:, j, t0:t0 + n], PS[:, 3 + g, 0:n], ALU.mult).then_inc(ya_ready, 1)

            def mix_products(n):
                out = mix[:, bass.ds(n, 1), :].rearrange("p a t -> p (a t)")
                for q, dst in enumerate((out, gates[:, 1, :])):
                    dve.wait_ge(gate_out, n * 2 + q + 1)
                    dve.wait_ge(mix_mm, n * 2 + q + 1)
                    for g, (t0, m) in enumerate(SEGS):
                        ins = tt(dst[:, t0:t0 + m], gates[:, q, t0:t0 + m], PS[:, 3 + g, 0:m], ALU.mult)
                        if g < 2:
                            V.step(ins)
                        else:
                            ins.then_inc(mix_out, 1)
                dve.wait_ge(mix_out, n * 2 + 2)
                tt(out, out, gates[:, 1, :], ALU.add).then_inc(mix_ready, 1)
                dve.wait_ge(mix_ready, n + 1)

            dve.wait_ge(ya_ready, 3 * NP)
            mix_products(0)
            with V.loop(1, KB, 4) as n:
                mix_products(n)
            for k in range(KB):
                dve.wait_ge(mix_rounded, k + 1)
                tt(mixL[:, k, :], mix[:, k, :], mixH[:, k, :], ALU.subtract).then_inc(mix_split, 1)
            for n in range(KB):
                dve.wait_ge(w_used, WO_TILE + n + 1)
                for g, (t0, m) in enumerate(SEGS):
                    c = 0 if g == 0 else 1
                    ts(x1[:, n, t0:t0 + m], PS[:, 3 * (n % 2) + g, 0:m], mod[:, 16 + n, c:c + 1], None, ALU.mult) \
                        .then_inc(x1_out, 1)
                for g, (t0, m) in enumerate(SEGS):
                    dve.wait_ge(x1_out, 3 * n + g + 1)
                    dve.wait_ge(xt_done, 3 * n + g + 1)
                    tt(x1[:, n, t0:t0 + m], x1[:, n, t0:t0 + m], PS[:, 6 + (3 * n + g) % 2, 0:m], ALU.add).then_inc(xt_out, 1)
            dve.wait_ge(ms_ready, 1)
            V.link(dve.reciprocal(tokstat[:, 1, :], tokstat[:, 0, :]))
            for b in range(TB):
                ts(diag2[:, b, :], ident, tokstat[:, 1, b:b + 1], None, ALU.mult).then_inc(diag2_ready, 1)
            dve.wait_ge(xt_out, 3 * KB)
            parts = [(g, k) for g in range(3) for k in range(KB)]
            LAG = 2
            for at in range(len(parts) + LAG):
                if at < len(parts):
                    g, k = parts[at]
                    t0, m = SEGS[g]
                    c = 0 if g == 0 else 1
                    dve.wait_ge(rs_done, g + 1)
                    stt(h2_scaled_x[:, k, t0:t0 + m], x1[:, k, t0:t0 + m], gsc2[:, k, c:c + 1], PS[:, 3 + g, 0:m], ALU.mult, ALU.mult) \
                        .then_inc(h2_scaled, 1)
                if at >= LAG:
                    g, k = parts[at - LAG]
                    t0, m = SEGS[g]
                    c = 0 if g == 0 else 1
                    dve.wait_ge(h2_rounded, at - LAG + 1)
                    stt(h2L[:, k, t0:t0 + m], h2_scaled_x[:, k, t0:t0 + m], mod[:, 24 + k, c:c + 1],
                        h2H[:, k, t0:t0 + m], ALU.add, ALU.subtract).then_inc(h2_ready, 1)

            def ffn_values(i, odd, slot):
                f = i * 2 + odd
                _, used = up_at(i, odd)
                u = uconv[odd]
                dve.wait_ge(u_copied, f + 1)
                if not (isinstance(i, int) and i == 0):
                    dve.wait_ge(fact_ready, f - 1)
                V.link(ts(u, upad[:, odd, 1:ZP - 1], conv_taps("conv_ffn", f, 1), None, ALU.mult))
                V.link(stt(u, upad[:, odd, 0:ZP - 2], conv_taps("conv_ffn", f, 0), u, ALU.mult, ALU.add))
                V.link(stt(u[:, 0:CTX], upad[:, odd, 2:CTX + 2], conv_taps("conv_ffn", f, 2), u[:, 0:CTX],
                           ALU.mult, ALU.add))
                stt(u[:, CTX:T], upad[:, odd, CTX + 3:ZP], conv_taps("conv_ffn", f, 2), u[:, CTX + 1:T + 1],
                    ALU.mult, ALU.add).then_inc(uconv_ready, 1)
                dve.wait_ge(gelu_ready, f + 1)
                dve.wait_ge(w_used, used + 2)
                for g, (t0, m) in enumerate(SEGS):
                    ins = tt(fact[:, slot, t0:t0 + m], u[:, t0:t0 + m], PS[:, 3 + g, 0:m], ALU.mult)
                    if g < 2:
                        V.step(ins)
                    else:
                        ins.then_inc(fact_ready, 1)

            def ffn_adds(i):
                _, used = down_at(i)
                for n in range(KB):
                    dve.wait_ge(w_used, used + (n + 1))
                    if n == 0 and not (isinstance(i, int) and i == 1):
                        dve.wait_ge(down_out, (i - 1) * KB)
                    for g, (t0, m) in enumerate(SEGS):
                        c = 0 if g == 0 else 1
                        ins = stt(x1[:, n, t0:t0 + m], PS[:, 3 * (n % 2) + g, 0:m], mod[:, 40 + n, c:c + 1],
                                  x1[:, n, t0:t0 + m], ALU.mult, ALU.add)
                        if g < 2:
                            V.step(ins)
                        else:
                            ins.then_inc(down_out, 1)

            def ffn_turn(i, even_slot):
                ffn_values(i, 0, even_slot)
                ffn_adds(i)
                ffn_values(i, 1, 0)

            dve.wait_ge(upad_zeroed, 1)
            ffn_values(0, 0, 1)
            ffn_values(0, 1, 0)
            ffn_turn(1, 2)
            ffn_turn(2, 1)
            with V.loop(1, (NG - 1) // 2, 52) as j:
                ffn_turn(j * 2 + 1, 2)
                ffn_turn(j * 2 + 2, 1)
            ffn_adds(NG)
            dve.wait_ge(down_out, NG * KB)
            dve.wait_ge(gain_in, 16)
            for b in range(TB):
                dve.wait_ge(yss_ready, 2 * b + 2)
                V.link(dve.reciprocal(tstat[:, 1, b:b + 1], tstat[:, 1, b:b + 1]))
                if b >= 4:
                    dve.wait_ge(y_stored[b % 4], 16 * (b // 4))
                banks = PS[:, 2 * (b % 4):2 * (b % 4) + 2, :].rearrange("p a n -> p (a n)")
                stt(y_tok[:, b % 4, :], banks, tstat[:, 1, b:b + 1], gain_f, ALU.mult, ALU.mult).then_inc(y_ready, 1)

        @block.gpsimd
        def _(pool):
            G = Steps(pool, pool_steps)
            pool.wait_ge(h_done, 3 * KB)
            pool.wait_ge(consts_in, 32)
            G.link(pool.memset(qbd[:, :, :], 0.0))
            with G.loop(0, NP, 3) as i:
                for s in range(3):
                    pool.wait_ge(qkv_in[s], i * 16 + 16)
                    G.link(pool.tensor_tensor(qkv_hi[:, s, :, :], qkv_ring[:, s, :, :], ones_tile, ALU.mult))
                    pool.tensor_tensor(qkv_lo[:, s, :, :], qkv_ring[:, s, :, :], qkv_hi[:, s, :, :],
                                       ALU.subtract).then_inc(qkv_split, 1)
            def split_tile(s, loads, used, src=None):
                src = raw[s] if src is None else src
                pool.wait_ge(w_in[0 if src is raw[0] else 1], loads * 16)
                if used is not None:
                    pool.wait_ge(w_used, used)
                G.link(pool.tensor_tensor(hi[s], src, ones_tile, ALU.mult))
                pool.tensor_tensor(lo[s], src, hi[s], ALU.subtract).then_inc(w_split, 1)

            pool.wait_ge(ada_used, 48)
            for s in range(2):
                split_tile(s, 1, None)
            pool.wait_ge(yb_kept, 16)
            pool.memset(zpad[:, :, :], 0.0).then_inc(zpad_zeroed, 1)
            with G.loop(1, RKV_TILES // 2, 2) as i:
                for s in range(2):
                    split_tile(s, i + 1, i * 2 + (s - 1))
            pool.wait_ge(w_used, RKV_TILES)
            pool.wait_ge(h_kept, 32)
            pool.memset(SI[:, :, :, :], 0.0).then_inc(si_zeroed, 1)
            pool.memset(ya[:, :, :], 0.0).then_inc(scan_zeroed, 1)
            pool.wait_ge(kk_ready, 3 * NP)
            pool.memset(AR[:, :, :, :], 0.0).then_inc(scan_zeroed, 1)
            for bd in (BD_B, BD_K, BD_V):
                G.step(pool.memset(bd, 0.0))
            pool.wait_ge(sxg_kept, 16)
            pool.memset(RESET, 1.0).then_inc(scan_zeroed, 1)
            pool.wait_ge(scan_zeroed, 3)
            pool.memset(RESET.rearrange("p (j t) -> p j t", t=C)[:, :, 0:1], 0.0).then_inc(scan_zeroed, 1)
            G.settle()
            pool.memset(PEND[:, :, :], 0.0).then_inc(scan_zeroed, 1)

            def pool_keys(n, at):
                pool.wait_ge(sig_done, n + 1)
                if not (isinstance(n, int) and n == 0):
                    pool.wait_ge(front_done, n)
                pool.tensor_tensor(BK, kk[:, :, bass.ds(at, C)], SG[:, 1, :, :], ALU.mult).then_inc(bk_ready, 1)

            def pool_half(n, d, front):
                pool.wait_ge(gram_out, n * 4 + 2)
                for lv in range(5):
                    if not (isinstance(n, int) and n == 0):
                        pool.wait_ge(lz_done, n * 5 + (lv - 4))
                    pool.tensor_tensor(Lm[:, lv, :, :], GB[:, d, :, 0:P],
                                       level_mask[:, d, lv + 1, :].unsqueeze(1).to_broadcast([P, NP, P]), ALU.mult) \
                        .then_inc(lm_ready, 1)
                if front is not None:
                    pool_keys(n + 1, front)

            def pool_pair(i, ctx_f, last=False):
                pool_half(2 * i, 0, chunk_at(1, i, ctx_f))
                pool_half(2 * i + 1, 1, None if last else chunk_at(0, i + 1, ctx_f))

            pool_keys(0, 0)
            pool_pair(0, True)
            with pool.Fori(1, NC_CTX) as i:
                pool_pair(i, True)
            pool_pair(NC_CTX, False)
            with pool.Fori(NC_CTX + 1, NC - 1) as i:
                pool_pair(i, False)
            pool_pair(NC - 1, False, last=True)
            def split_gates(n):
                for q in range(2):
                    split_tile(q, n * 2 + (W4 + q + 1), n * 2 + (GATE_TILE + q - 1), src=raw[0])

            h_again_from = dram["h_kept"].rearrange("p (k t) -> p k t", t=T)
            pool.wait_ge(y_out, NUNIT)
            pool.wait_ge(rh_out, NUNIT)
            pool.wait_ge(s_ready, NUNIT + 2)
            pool.dma_start(hH, h_again_from[:, 0:KB]).then_inc(h_again, 16)
            pool.dma_start(hL4[:, 0:KB // 2], h_again_from[:, KB:KB + KB // 2]).then_inc(h_again, 16)
            pool.wait_ge(var_done, 1)
            pool.dma_start(hL4[:, KB // 2:KB], h_again_from[:, KB + KB // 2:2 * KB]).then_inc(h_again, 16)
            pool.wait_ge(fin_stored, 64)
            pool.wait_ge(gate_done, 3 * NP)
            split_gates(0)
            with G.loop(1, KB, 2) as n:
                split_gates(n)
            for n in range(2):
                split_tile(n, WO + 1, WO_TILE + n - 1)
            for n in range(KB):
                m = n + 2
                split_tile(m % 2, WO + m // 2 + 1, WO_TILE + m - 1)
                pool.wait_ge(x1sq_ready, n + 1)
                if n == 0:
                    pool.tensor_copy(x1sq_sum, x1sq).then_inc(x1sq_added, 1)
                else:
                    pool.wait_ge(x1sq_added, n)
                    pool.tensor_tensor(x1sq_sum, x1sq_sum, x1sq, ALU.add).then_inc(x1sq_added, 1)
            pool.wait_ge(ms_done, 1)
            pool.wait_ge(x1sq_added, KB)
            pool.memset(upad[:, :, :], 0.0).then_inc(upad_zeroed, 1)

            def split_up(i, odd):
                _, used = up_at(i, odd)
                turn = WF + 1 + odd if isinstance(i, int) and i == 0 else i * 3 + (WF + 2 * odd)
                if isinstance(i, int) and i == 0:
                    before = [used - 1, used]
                elif odd:
                    before = [used - KB // 2, used]
                else:
                    before = [used - 1, used]
                for s in range(2):
                    split_tile(s, turn, before[s])

            def split_down(i):
                _, used = down_at(i)
                turn = i * 3 + (WF if isinstance(i, int) and i == NG else WF + 1)
                for s in range(2):
                    split_tile(s, turn, used + (s - 1))

            def split_fact(f, slot):
                pool.wait_ge(fact_rounded, f + 1)
                pool.tensor_tensor(factL[:, slot, :], fact[:, slot, :], factH[:, slot, :], ALU.subtract) \
                    .then_inc(fact_split, 1)

            def ffn_turn(i, even_slot):
                split_up(i, 0)
                split_fact(i * 2 - 1, 0)
                split_down(i)
                split_fact(i * 2, even_slot)
                split_up(i, 1)

            split_up(0, 1)
            split_fact(0, 1)
            with G.loop(0, (NG - 1) // 2, 12) as j:
                ffn_turn(j * 2 + 1, 2)
                ffn_turn(j * 2 + 2, 1)
            split_fact(FB - 1, 0)
            split_down(NG)


def kernel(**inputs):
    import concourse.bacc as _bacc
    from concourse.bass_utils import run_bass_kernel_spmd as _run

    a = {k: np.asarray(v) for k, v in inputs.items()}
    one = {k: a[k][0] for k in ("w_ada", "b_ada", "w_in", "conv_rkv", "decay_w0", "decay_up", "iclr_a0", "iclr_up",
                                "gate_up", "k_k", "k_a", "r_k", "gn_w", "gn_b", "rel_bias", "w_out_a", "w_out_b",
                                "w_out", "w_ffn_up", "conv_ffn", "w_ffn_down", "norm1_g", "norm2_g")}

    def blocks(w):
        k, n = w.shape
        return w.reshape(k // P, P, n // P, P).transpose(2, 1, 0, 3).reshape(n // P, P, k)

    def per_feature(v, n):
        return v.reshape(-1, n, P).transpose(2, 1, 0).reshape(P, -1)

    params = np.empty((P, N_PARAMS), np.float32)

    def put(name, v):
        at, n = PARAMS[name]
        params[:, at:at + n] = v.reshape(P, n)

    put("cond", per_feature(np.stack([a["c_ctx"], a["c"][0]]), KB))
    put("b_ada", per_feature(one["b_ada"], 48))
    put("norm1", per_feature(one["norm1_g"], KB))
    put("norm2", per_feature(one["norm2_g"], KB))
    put("conv_rkv", per_feature(one["conv_rkv"], 12))
    put("conv_ffn", per_feature(one["conv_ffn"], FB))
    put("bias_wi", np.stack([one["decay_w0"], one["iclr_a0"]], 1).reshape(4, NP, P).transpose(2, 0, 1))
    for name in ("k_k", "k_a", "r_k", "gn_w", "gn_b"):
        put(name, per_feature(one[name].reshape(-1), NP))

    codes = np.zeros((P, 2, 2, NP * P), np.float32)
    codes[0:64, 0] = one["decay_up"].transpose(1, 0, 2)
    codes[64:128, 1] = one["iclr_up"].transpose(1, 0, 2)
    state = a["state_rwkv"][0, 0].reshape(2, NP, P, HD)

    def pairs(x):
        return x[0, 0].reshape(NP, 2, 2, P, HD).transpose(0, 2, 3, 1, 4).reshape(NP, 2, P, P)

    ins = {
        "consts": constants(),
        "params": params,
        "x": np.concatenate([a["x_prompt"][0], a["x_sample"][0]]).reshape(TB, P, D),
        "w_ada": blocks(one["w_ada"]),
        "w_in": blocks(one["w_in"]),
        "w_oa": blocks(one["w_out_a"]),
        "w_ob": blocks(one["w_out_b"]),
        "w_o": blocks(one["w_out"]),
        "w_up": blocks(one["w_ffn_up"]),
        "w_down": one["w_ffn_down"].reshape(FB // 2, 2, P, 2, 4, P).transpose(0, 3, 2, 4, 1, 5).reshape(FB, P, KB * P),
        "codes": codes.reshape(P, -1),
        "gate_up": one["gate_up"],
        "norm_f": a["norm_f_g"].reshape(1, D),
        "ck": pairs(a["cache_k"]),
        "cv": pairs(a["cache_v"]),
        "rel": np.pad(one["rel_bias"].reshape(-1), (GRID - WIN_C, 2 * GRID)),
        "state": state,
    }
    outs = {"y": (TB, P, D), "new_k": (NP, 2, P, P), "new_v": (NP, 2, P, P), "new_state": (2, NP, P, HD)}
    nc = _bacc.Bacc("TRN2", target_bir_lowering=False, num_devices=1)
    arrays, dram = {}, {}
    for name, v in ins.items():
        arrays[f"in_{name}"] = np.ascontiguousarray(v)
        dram[name] = nc.dram_tensor(f"in_{name}", v.shape, mybir.dt.from_np(v.dtype), kind="ExternalInput").ap()
    for name, shape in outs.items():
        dram[name] = nc.dram_tensor(f"out_{name}", shape, F32, kind="ExternalOutput").ap()
    dram["start"] = nc.dram_tensor("start", (1, 64), F32).ap()
    dram["h_kept"] = nc.dram_tensor("h_kept", (P, 2 * KB * T), F32).ap()
    dram["sxg_kept"] = nc.dram_tensor("sxg_kept", (P, T), F32).ap()
    dram["yb_kept"] = nc.dram_tensor("yb_kept", (P, NP * T), F32).ap()
    build(nc, dram)
    r = _run(nc, [arrays], core_ids=[0]).results[0]
    y = r["out_y"].reshape(1, T, D)

    def unpair(x):
        return x.reshape(NP, 2, P, 2, HD).transpose(0, 3, 1, 2, 4).reshape(1, 1, 2 * NP, CTX, HD)

    return (y[:, :CTX], y[:, CTX:], unpair(r["out_new_k"]), unpair(r["out_new_v"]),
            r["out_new_state"].reshape(1, 1, 2, 2 * NP, HD, HD))
```
